# Optimizing a Trainium2 kernel written in Bass

```python
import math
import jax
import jax.numpy as jnp
from jax import lax
import numpy as np

D_MODEL = 1024
BATCH = 1
SEQ = 1024
DEPTH = 1
DEC_BATCH = 8
DEC_SEQ = 1
PAST_LEN = 4096
PAGE_SIZE = 128

D_MIX = D_MODEL
NSA_WIDTH = D_MIX // 2
SSM_WIDTH = D_MIX - NSA_WIDTH
HEAD_DIM = 64
N_HEADS = NSA_WIDTH // HEAD_DIM
N_KV = 2
GQA = N_HEADS // N_KV
KV_WIDTH = N_KV * HEAD_DIM
N_BRANCH = 3
CMP_BLOCK = 32
SEL_BLOCK = 64
CMP_PER_SEL = SEL_BLOCK // CMP_BLOCK
N_SEL = 16
WINDOW = 512
WIN_QBLOCK = 128
SEL_QCHUNK = 32
SSM_GROUP = 16
N_SSM_GROUPS = SSM_WIDTH // SSM_GROUP
SSM_STATE = 64
N_BUCKETS = 32
MAX_DISTANCE = 128
N_MEM = 256
MEM_HEADS = 4
MEM_HEAD_DIM = 128
MEM_WIDTH = MEM_HEADS * MEM_HEAD_DIM
D_FF = -(-(8 * D_MODEL) // (3 * 256)) * 256
EPS = 1e-6
NEG = -1e30
TINY = 1e-30
FORCE = 1e4
SCALE = HEAD_DIM ** -0.5
MEM_SCALE = MEM_HEAD_DIM ** -0.5

OFF_KVC = NSA_WIDTH
OFF_KVS = OFF_KVC + 2 * KV_WIDTH
OFF_KVW = OFF_KVS + 2 * KV_WIDTH
OFF_GATE = OFF_KVW + 2 * KV_WIDTH
OFF_U = OFF_GATE + N_HEADS * N_BRANCH
IN_COLS = OFF_U + SSM_WIDTH

kernel_name = 'hymba_nsa_s5_memxattn_decode_step'

def rmsnorm(x, g):
    xf = x.astype(jnp.float32)
    y = xf * lax.rsqrt(jnp.mean(xf * xf, axis=-1, keepdims=True) + EPS)
    return (y * g.astype(jnp.float32)).astype(x.dtype)

def masked_softmax(s, mask, axis=-1):
    s = jnp.where(mask, s.astype(jnp.float32), NEG)
    m = jnp.max(s, axis=axis, keepdims=True)
    e = jnp.where(mask, jnp.exp(s - m), 0.0)
    return e / jnp.maximum(jnp.sum(e, axis=axis, keepdims=True), TINY)

def t5_bucket(dist):
    n = jnp.maximum(dist, 0)
    exact = N_BUCKETS // 2
    nf = jnp.maximum(n, exact).astype(jnp.float32)
    big = exact + (jnp.log(nf / exact) / math.log(MAX_DISTANCE / exact) * (N_BUCKETS - exact)).astype(jnp.int32)
    return jnp.where(n < exact, n, jnp.minimum(big, N_BUCKETS - 1))

def project(h, w_in):
    z = h @ w_in
    B, S, _ = z.shape
    q = z[..., :NSA_WIDTH].reshape(B, S, N_KV, GQA, HEAD_DIM)
    kv_c = z[..., OFF_KVC:OFF_KVS].reshape(B, S, 2, N_KV, HEAD_DIM)
    kv_s = z[..., OFF_KVS:OFF_KVW].reshape(B, S, 2, N_KV, HEAD_DIM)
    kv_w = z[..., OFF_KVW:OFF_GATE].reshape(B, S, 2, N_KV, HEAD_DIM)
    gates = jax.nn.sigmoid(z[..., OFF_GATE:OFF_U].astype(jnp.float32)).reshape(B, S, N_KV, GQA, N_BRANCH).astype(z.dtype)
    u = z[..., OFF_U:IN_COLS]
    return q, kv_c, kv_s, kv_w, gates, u

def compress_blocks(rows, cmp_pos, cmp_proj):
    B, N = rows.shape[:2]
    blk = rows.reshape(B, N // CMP_BLOCK, CMP_BLOCK, 2, N_KV, HEAD_DIM)
    summ = jnp.einsum('bnlcgd,cld->bncgd', blk, cmp_pos)
    return jnp.einsum('bncgd,cde->bncge', summ, cmp_proj)

def cmp_attention(q, blocks, qpos, table):
    S = q.shape[1]
    NC = blocks.shape[1]
    end = jnp.arange(NC, dtype=jnp.int32) * CMP_BLOCK + (CMP_BLOCK - 1)
    dist = qpos[:, None] - end[None, :]
    bias = table[t5_bucket(dist)].reshape(S, NC, N_KV, GQA).transpose(0, 2, 3, 1)
    s = jnp.einsum('bsgrd,bcgd->bsgrc', q, blocks[:, :, 0]).astype(jnp.float32) * SCALE + bias.astype(jnp.float32)
    p = masked_softmax(s, (dist >= 0)[:, None, None, :], -1)
    o = jnp.einsum('bsgrc,bcgd->bsgrd', p.astype(q.dtype), blocks[:, :, 1])
    return o, p

def select_blocks(p, qpos):
    B, S, G, R, NC = p.shape
    nbs = NC // CMP_PER_SEL
    ps = p.sum(3).reshape(B, S, G, nbs, CMP_PER_SEL).sum(-1)
    j = jnp.arange(nbs, dtype=jnp.int32)
    cur = (qpos // SEL_BLOCK)[:, None]
    forced = ((j == 0) | (j == cur) | (j == cur - 1))[None, :, None, :]
    visible = (j <= cur)[None, :, None, :]
    score = jnp.where(visible, jnp.where(forced, ps + FORCE, ps), -jnp.inf)
    _, idx = lax.top_k(score, min(N_SEL, nbs))
    valid = idx <= cur[None, :, :, None]
    return idx.astype(jnp.int32), valid

def sel_attention(q, kv, idx, valid, qpos, table):
    tok = idx[..., None] * SEL_BLOCK + jnp.arange(SEL_BLOCK, dtype=jnp.int32)
    dist = qpos[None, :, None, None, None] - tok
    mask = valid[..., None] & (dist >= 0)
    gi = jnp.arange(N_KV)[None, None, :, None, None]
    bias = table.reshape(N_BUCKETS, N_KV, GQA)[t5_bucket(dist), gi]
    s = jnp.einsum('bsgrd,bsgkld->bsgrkl', q, kv[..., 0, :]).astype(jnp.float32) * SCALE + jnp.moveaxis(bias, -1, 3).astype(jnp.float32)
    p = masked_softmax(s, mask[:, :, :, None], axis=(-2, -1))
    return jnp.einsum('bsgrkl,bsgkld->bsgrd', p.astype(q.dtype), kv[..., 1, :])

def window_prompt(q, kvw, table):
    B, T = q.shape[:2]
    nq = T // WIN_QBLOCK
    span = WINDOW + WIN_QBLOCK
    kvp = jnp.pad(kvw, ((0, 0), (WINDOW, 0), (0, 0), (0, 0), (0, 0)))
    rows = jnp.arange(nq)[:, None] * WIN_QBLOCK + jnp.arange(span)[None, :]
    kb = kvp[:, rows]
    qb = q.reshape(B, nq, WIN_QBLOCK, N_KV, GQA, HEAD_DIM)
    dist = jnp.arange(WIN_QBLOCK)[:, None] + WINDOW - jnp.arange(span)[None, :]
    mask = ((dist >= 0) & (dist < WINDOW))[None] & (rows >= WINDOW)[:, None, :]
    bias = table[t5_bucket(dist)].reshape(WIN_QBLOCK, span, N_KV, GQA).transpose(2, 3, 0, 1)
    s = jnp.einsum('bnqgrd,bnkgd->bngrqk', qb, kb[:, :, :, 0]).astype(jnp.float32) * SCALE + bias.astype(jnp.float32)
    p = masked_softmax(s, mask[None, :, None, None], -1)
    o = jnp.einsum('bngrqk,bnkgd->bnqgrd', p.astype(q.dtype), kb[:, :, :, 1])
    return o.reshape(q.shape)

def window_sample(q, buf, kvw, past_len, table):
    S = q.shape[1]
    wb = buf.shape[1]
    keys = jnp.concatenate([buf.astype(kvw.dtype), kvw], axis=1)
    qpos = past_len + jnp.arange(S, dtype=jnp.int32)
    kpos = past_len - wb + jnp.arange(wb + S, dtype=jnp.int32)
    dist = qpos[:, None] - kpos[None, :]
    mask = (dist >= 0) & (dist < WINDOW)
    bias = table[t5_bucket(dist)].reshape(S, wb + S, N_KV, GQA).transpose(2, 3, 0, 1)
    s = jnp.einsum('bsgrd,bkgd->bgrsk', q, keys[:, :, 0]).astype(jnp.float32) * SCALE + bias.astype(jnp.float32)
    p = masked_softmax(s, mask, -1)
    o = jnp.einsum('bgrsk,bkgd->bsgrd', p.astype(q.dtype), keys[:, :, 1])
    return o, keys[:, S:]

def combine_branches(gates, o_c, o_s, o_w):
    o = gates[..., 0:1] * o_c + gates[..., 1:2] * o_s + gates[..., 2:3] * o_w
    return o.reshape(o.shape[0], o.shape[1], NSA_WIDTH)

def nsa_prompt(q, kvc, kvs, kvw, gates, cmp_pos, cmp_proj, table):
    B, T = q.shape[:2]
    qpos = jnp.arange(T, dtype=jnp.int32)
    padw = ((0, 0), (0, (-T) % SEL_BLOCK), (0, 0), (0, 0), (0, 0))
    blocks = compress_blocks(jnp.pad(kvc, padw), cmp_pos, cmp_proj)
    o_c, p = cmp_attention(q, blocks, qpos, table)
    idx, valid = select_blocks(p, qpos)
    kvb = jnp.pad(kvs, padw).reshape(B, -1, SEL_BLOCK, 2, N_KV, HEAD_DIM).transpose(0, 4, 1, 2, 3, 5)
    bi = jnp.arange(B)[:, None, None, None]
    gi = jnp.arange(N_KV)[None, None, :, None]
    n_chunk = T // SEL_QCHUNK

    def to_chunks(a):
        return jnp.moveaxis(a.reshape(B, n_chunk, SEL_QCHUNK, *a.shape[2:]), 1, 0)

    def one_chunk(args):
        qc, ic, vc, pc = args
        kv = kvb[bi, gi, ic]
        return sel_attention(qc, kv, ic, vc, pc, table)

    o_s = lax.map(one_chunk, (to_chunks(q), to_chunks(idx), to_chunks(valid), qpos.reshape(n_chunk, SEL_QCHUNK)))
    o_s = jnp.moveaxis(o_s, 0, 1).reshape(q.shape)
    o_w = window_prompt(q, kvw, table)
    return combine_branches(gates, o_c, o_s, o_w)

def nsa_sample(q, kvc, kvs, kvw, gates, pool_c, pool_s, buf_w, page_table, layer, cmp_pos, cmp_proj, table):
    DB, S = q.shape[:2]
    n_pages = page_table.shape[1]
    past_len = n_pages * PAGE_SIZE
    qpos = past_len + jnp.arange(S, dtype=jnp.int32)
    padw = ((0, 0), (0, (-S) % SEL_BLOCK), (0, 0), (0, 0), (0, 0))
    past_c = pool_c[layer, page_table].reshape(DB, past_len, 2, N_KV, HEAD_DIM)
    blocks = jnp.concatenate([compress_blocks(past_c, cmp_pos, cmp_proj),
                              compress_blocks(jnp.pad(kvc, padw), cmp_pos, cmp_proj)], axis=1)
    o_c, p = cmp_attention(q, blocks, qpos, table)
    idx, valid = select_blocks(p, qpos)
    nb_past = past_len // SEL_BLOCK
    bpp = PAGE_SIZE // SEL_BLOCK
    bi = jnp.arange(DB)[:, None, None, None]
    gi = jnp.arange(N_KV)[None, None, :, None]
    jp = jnp.minimum(idx, nb_past - 1)
    phys = page_table[bi, jp // bpp]
    pool_r = pool_s.reshape(pool_s.shape[0], pool_s.shape[1], bpp, SEL_BLOCK, 2, N_KV, HEAD_DIM)
    kv_past = pool_r[layer, phys, jp % bpp, :, :, gi, :]
    new_r = jnp.pad(kvs, padw).reshape(DB, -1, SEL_BLOCK, 2, N_KV, HEAD_DIM).transpose(0, 4, 1, 2, 3, 5)
    jn = jnp.clip(idx - nb_past, 0, new_r.shape[2] - 1)
    kv_new = new_r[bi, gi, jn]
    kv = jnp.where((idx < nb_past)[..., None, None, None], kv_past.astype(kv_new.dtype), kv_new)
    o_s = sel_attention(q, kv, idx, valid, qpos, table)
    o_w, new_buf = window_sample(q, buf_w, kvw, past_len, table)
    return combine_branches(gates, o_c, o_s, o_w), new_buf

def _ssm_combine(e1, e2):
    ar1, ai1, br1, bi1 = e1
    ar2, ai2, br2, bi2 = e2
    return (ar2 * ar1 - ai2 * ai1, ar2 * ai1 + ai2 * ar1,
            ar2 * br1 - ai2 * bi1 + br2, ar2 * bi1 + ai2 * br1 + bi2)

def ssm_apply(u, h0, ssm_p):
    a_re, a_im, b_re, b_im, c_re, c_im, d, log_dt, glu_w, glu_b = ssm_p
    f32 = jnp.float32
    a_re = a_re.astype(f32)
    a_im = a_im.astype(f32)
    dt = jnp.exp(log_dt.astype(f32))[:, None]
    mag = jnp.exp(a_re * dt)
    ab_re = mag * jnp.cos(a_im * dt)
    ab_im = mag * jnp.sin(a_im * dt)
    den = a_re * a_re + a_im * a_im
    co_re = ((ab_re - 1.0) * a_re + ab_im * a_im) / den
    co_im = (ab_im * a_re - (ab_re - 1.0) * a_im) / den
    b_re = b_re.astype(f32)
    b_im = b_im.astype(f32)
    bb_re = co_re[..., None] * b_re - co_im[..., None] * b_im
    bb_im = co_re[..., None] * b_im + co_im[..., None] * b_re
    B, S, _ = u.shape
    uf = u.astype(f32)
    ug = uf.reshape(B, S, N_SSM_GROUPS, SSM_GROUP)
    bu_re = jnp.einsum('bsgi,gpi->bsgp', ug, bb_re)
    bu_im = jnp.einsum('bsgi,gpi->bsgp', ug, bb_im)
    shape_a = (1, S, N_SSM_GROUPS, SSM_STATE)
    elems = (jnp.broadcast_to(ab_re, shape_a), jnp.broadcast_to(ab_im, shape_a), bu_re, bu_im)
    pa_re, pa_im, h_re, h_im = lax.associative_scan(_ssm_combine, elems, axis=1)
    if h0 is not None:
        h0_re = h0[0].astype(f32)[:, None]
        h0_im = h0[1].astype(f32)[:, None]
        h_re, h_im = (h_re + pa_re * h0_re - pa_im * h0_im,
                      h_im + pa_re * h0_im + pa_im * h0_re)
    y = (jnp.einsum('gip,bsgp->bsgi', c_re.astype(f32), h_re)
         - jnp.einsum('gip,bsgp->bsgi', c_im.astype(f32), h_im))
    y = y.reshape(B, S, SSM_WIDTH) + d.astype(f32) * uf
    g = jax.nn.gelu(y)
    out = g * jax.nn.sigmoid(g @ glu_w.astype(f32) + glu_b.astype(f32))
    return out.astype(u.dtype), h_re[:, -1], h_im[:, -1]

def merge_groups(o_nsa, o_ssm, grp_g, w_out):
    m = jnp.concatenate([rmsnorm(o_nsa, grp_g[:NSA_WIDTH]), rmsnorm(o_ssm, grp_g[NSA_WIDTH:])], axis=-1)
    return m @ w_out

def memory_kv(mem, g, w_kv):
    B, M, _ = mem.shape
    return (rmsnorm(mem, g) @ w_kv).reshape(B, M, 2, MEM_HEADS, MEM_HEAD_DIM)

def cross_attn(h, mkv, w_q, w_o):
    B, S, _ = h.shape
    q = (h @ w_q).reshape(B, S, MEM_HEADS, MEM_HEAD_DIM)
    s = jnp.einsum('bshd,bmhd->bhsm', q, mkv[:, :, 0].astype(q.dtype)).astype(jnp.float32) * MEM_SCALE
    p = jax.nn.softmax(s, axis=-1).astype(q.dtype)
    o = jnp.einsum('bhsm,bmhd->bshd', p, mkv[:, :, 1].astype(q.dtype)).reshape(B, S, MEM_WIDTH)
    return o @ w_o

def swiglu(h, w_i, w_o):
    z = h @ w_i
    return (jax.nn.silu(z[..., :D_FF]) * z[..., D_FF:]) @ w_o

def cross_and_ffn(x, mkv, ng, w_q, w_o, ffn_wi, ffn_wo):
    x = x + rmsnorm(cross_attn(rmsnorm(x, ng[2]), mkv, w_q, w_o), ng[3])
    return x + rmsnorm(swiglu(rmsnorm(x, ng[4]), ffn_wi, ffn_wo), ng[5])

def setup_inputs(seed: int = 0) -> dict:
    key = jax.random.key(seed)
    ks = iter(jax.random.split(key, 40))
    f32 = jnp.float32

    def nrm(shape, scale=1.0):
        return jax.random.normal(next(ks), shape, f32) * scale

    n_pages = PAST_LEN // PAGE_SIZE
    n_used = DEC_BATCH * n_pages
    n_phys = n_used + n_used // 4
    win_rows = min(WINDOW, PAST_LEN)
    n_idx = jnp.arange(SSM_STATE, dtype=f32)
    gshape = (DEPTH, N_SSM_GROUPS, SSM_STATE)
    return {
        'x_prompt': nrm((BATCH, SEQ, D_MODEL)),
        'x_sample': nrm((DEC_BATCH, DEC_SEQ, D_MODEL)),
        'cache_kv_cmp': nrm((DEPTH, n_phys, PAGE_SIZE, 2, N_KV, HEAD_DIM)),
        'cache_kv_sel': nrm((DEPTH, n_phys, PAGE_SIZE, 2, N_KV, HEAD_DIM)),
        'cache_kv_win': nrm((DEPTH, DEC_BATCH, win_rows, 2, N_KV, HEAD_DIM)),
        'state_ssm_re': nrm((DEPTH, DEC_BATCH, N_SSM_GROUPS, SSM_STATE), 0.3),
        'state_ssm_im': nrm((DEPTH, DEC_BATCH, N_SSM_GROUPS, SSM_STATE), 0.3),
        'cache_mem_kv': nrm((DEPTH, DEC_BATCH, N_MEM, 2, MEM_HEADS, MEM_HEAD_DIM)),
        'page_table': jax.random.permutation(next(ks), n_phys)[:n_used].reshape(DEC_BATCH, n_pages).astype(jnp.int32),
        'mem_prompt': nrm((BATCH, N_MEM, D_MODEL)),
        'w_in': nrm((DEPTH, D_MODEL, IN_COLS), D_MODEL ** -0.5),
        'w_out': nrm((DEPTH, D_MIX, D_MODEL), D_MIX ** -0.5),
        'norm_g': 1.0 + nrm((DEPTH, 6, D_MODEL), 0.02),
        'grp_norm_g': 1.0 + nrm((DEPTH, D_MIX), 0.02),
        'cmp_pos': (1.0 + nrm((DEPTH, 2, CMP_BLOCK, HEAD_DIM), 0.1)) * CMP_BLOCK ** -0.5,
        'cmp_proj': nrm((DEPTH, 2, HEAD_DIM, HEAD_DIM), HEAD_DIM ** -0.5),
        'rel_bias': nrm((N_BUCKETS, N_HEADS), 0.5),
        'ssm_a_re': -0.5 + nrm(gshape, 0.01),
        'ssm_a_im': jnp.broadcast_to(jnp.pi * n_idx, gshape) + nrm(gshape, 0.01),
        'ssm_b_re': nrm((DEPTH, N_SSM_GROUPS, SSM_STATE, SSM_GROUP), (2 * SSM_GROUP) ** -0.5),
        'ssm_b_im': nrm((DEPTH, N_SSM_GROUPS, SSM_STATE, SSM_GROUP), (2 * SSM_GROUP) ** -0.5),
        'ssm_c_re': nrm((DEPTH, N_SSM_GROUPS, SSM_GROUP, SSM_STATE), (2 * SSM_STATE) ** -0.5),
        'ssm_c_im': nrm((DEPTH, N_SSM_GROUPS, SSM_GROUP, SSM_STATE), (2 * SSM_STATE) ** -0.5),
        'ssm_d': nrm((DEPTH, SSM_WIDTH)),
        'ssm_log_dt': jax.random.uniform(next(ks), (DEPTH, N_SSM_GROUPS), f32, math.log(0.001), math.log(0.1)),
        'glu_w': nrm((DEPTH, SSM_WIDTH, SSM_WIDTH), SSM_WIDTH ** -0.5),
        'glu_b': nrm((DEPTH, SSM_WIDTH), 0.02),
        'mem_norm_g': 1.0 + nrm((DEPTH, D_MODEL), 0.02),
        'xq': nrm((DEPTH, D_MODEL, MEM_WIDTH), D_MODEL ** -0.5),
        'xkv': nrm((DEPTH, D_MODEL, 2 * MEM_WIDTH), D_MODEL ** -0.5),
        'xo': nrm((DEPTH, MEM_WIDTH, D_MODEL), MEM_WIDTH ** -0.5),
        'ffn_wi': nrm((DEPTH, D_MODEL, 2 * D_FF), D_MODEL ** -0.5),
        'ffn_wo': nrm((DEPTH, D_FF, D_MODEL), D_FF ** -0.5),
    }

def reference(x_prompt, x_sample, cache_kv_cmp, cache_kv_sel, cache_kv_win, state_ssm_re, state_ssm_im,
              cache_mem_kv, page_table, mem_prompt, w_in, w_out, norm_g, grp_norm_g, cmp_pos, cmp_proj,
              rel_bias, ssm_a_re, ssm_a_im, ssm_b_re, ssm_b_im, ssm_c_re, ssm_c_im, ssm_d, ssm_log_dt,
              glu_w, glu_b, mem_norm_g, xq, xkv, xo, ffn_wi, ffn_wo):
    xp = x_prompt
    xs = x_sample
    l_pc, l_ps, l_pw, l_pre, l_pim, l_pm = [], [], [], [], [], []
    l_sc, l_ss, l_sw, l_sre, l_sim = [], [], [], [], []
    for l in range(DEPTH):
        ssm_p = (ssm_a_re[l], ssm_a_im[l], ssm_b_re[l], ssm_b_im[l], ssm_c_re[l], ssm_c_im[l],
                 ssm_d[l], ssm_log_dt[l], glu_w[l], glu_b[l])
        h = rmsnorm(xp, norm_g[l, 0])
        q, kvc, kvs, kvw, gates, u = project(h, w_in[l])
        o_nsa = nsa_prompt(q, kvc, kvs, kvw, gates, cmp_pos[l], cmp_proj[l], rel_bias)
        o_ssm, h_re, h_im = ssm_apply(u, None, ssm_p)
        xp = xp + rmsnorm(merge_groups(o_nsa, o_ssm, grp_norm_g[l], w_out[l]), norm_g[l, 1])
        mkv = memory_kv(mem_prompt, mem_norm_g[l], xkv[l])
        xp = cross_and_ffn(xp, mkv, norm_g[l], xq[l], xo[l], ffn_wi[l], ffn_wo[l])
        T = kvw.shape[1]
        l_pc.append(kvc)
        l_ps.append(kvs)
        l_pw.append(kvw[:, T - min(WINDOW, T):])
        l_pre.append(h_re)
        l_pim.append(h_im)
        l_pm.append(mkv)
        h = rmsnorm(xs, norm_g[l, 0])
        q, kvc, kvs, kvw, gates, u = project(h, w_in[l])
        o_nsa, new_buf = nsa_sample(q, kvc, kvs, kvw, gates, cache_kv_cmp, cache_kv_sel, cache_kv_win[l],
                                    page_table, l, cmp_pos[l], cmp_proj[l], rel_bias)
        o_ssm, h_re, h_im = ssm_apply(u, (state_ssm_re[l], state_ssm_im[l]), ssm_p)
        xs = xs + rmsnorm(merge_groups(o_nsa, o_ssm, grp_norm_g[l], w_out[l]), norm_g[l, 1])
        xs = cross_and_ffn(xs, cache_mem_kv[l], norm_g[l], xq[l], xo[l], ffn_wi[l], ffn_wo[l])
        l_sc.append(kvc)
        l_ss.append(kvs)
        l_sw.append(new_buf)
        l_sre.append(h_re)
        l_sim.append(h_im)
    p_kv_cmp = jnp.stack(l_pc, axis=0)
    p_kv_sel = jnp.stack(l_ps, axis=0)
    p_kv_win = jnp.stack(l_pw, axis=0)
    p_ssm_re = jnp.stack(l_pre, axis=0)
    p_ssm_im = jnp.stack(l_pim, axis=0)
    p_mem_kv = jnp.stack(l_pm, axis=0)
    s_kv_cmp = jnp.stack(l_sc, axis=0)
    s_kv_sel = jnp.stack(l_ss, axis=0)
    s_kv_win = jnp.stack(l_sw, axis=0)
    s_ssm_re = jnp.stack(l_sre, axis=0)
    s_ssm_im = jnp.stack(l_sim, axis=0)
    return (xp, xs, p_kv_cmp, p_kv_sel, p_kv_win, p_ssm_re, p_ssm_im, p_mem_kv,
            s_kv_cmp, s_kv_sel, s_kv_win, s_ssm_re, s_ssm_im)


_drawn_inputs = setup_inputs


def setup_inputs(seed=0):
    import zlib

    import numpy as np

    out = dict(_drawn_inputs(seed))
    spreads = {}
    factors = {'grp_norm_g': 3.573, 'ssm_a_re': 3.981, 'glu_b': 8.0, 'mem_norm_g': 3.131}
    for name, (base, spread) in spreads.items():
        noise = np.random.default_rng([zlib.crc32(name.encode()), seed]).standard_normal(out[name].shape)
        drawn = base * np.exp(spread * noise) if base else spread * noise
        out[name] = jnp.asarray(drawn.astype(out[name].dtype))
    for name, factor in factors.items():
        out[name] = (out[name] * factor).astype(out[name].dtype)
    return out
```

```python
from contextlib import ExitStack
from math import log, pi

import numpy as np

import concourse.bass as bass
from concourse import mybir

F32 = mybir.dt.float32
I32 = mybir.dt.int32
U32 = mybir.dt.uint32
ALU = mybir.AluOpType
ACT = mybir.ActivationFunctionType
X = mybir.AxisListType.X

P = 128
D = 1024
KD = D // P
T = 1024
NT = T // P
DB = 8
TC = T + DB
CH = TC // 3
HD = 64
NH = 8
NKV = 2
GQ = NH // NKV
KVC = 3 * 2 * NKV * HD
NG = 3 * NH
OFF_U = NH * HD + KVC + NG
CB = 32
WIN = 512
PAST = 4096
PAGE = 128
NPAGE = PAST // PAGE
NCB = PAST // CB
NSB = PAST // 64
PICK = 13
SLOTS = PICK + 2
PARAM_DMAS = 9
ROWS = 8
LINES = 64 // ROWS
SL = SLOTS * LINES
SK = SL + 1
GAT0 = [11, 11, 10]
NPAIR = 16
L4 = 4
NC = T // L4
NF = 22
DFF = NF * P
XH = 4
NM = 256
EPS = 1e-6
TINY = 1e-30
SC = HD ** -0.5
NEG = -1e30 / SC
FLOOR = -1e20 / SC
XSC = P ** -0.5
VL = T + P - 1


def bucket_ranges():
    n = np.arange(T)
    big = 16 + (np.log(np.maximum(n, 16).astype(np.float32) / 16) / log(8) * 16).astype(np.int32)
    b = np.where(n < 16, n, np.minimum(big, 31))
    return [(int(v), int(np.argmax(b == v)), int(T - 1 - np.argmax(b[::-1] == v))) for v in np.unique(b)]


def token_tile(i):
    return (i * P, P) if i < NT else (T, DB)


def attention_units():
    out = []
    for i in range(NT):
        for h in range(NH):
            out.append((i, h, 0, 0, 4 * (i + 1)))
            out.append((i, h, 1, 0, P * (i + 1)))
            k0 = max(0, i - 4) * P
            out.append((i, h, 2, k0, P * (i + 1) - k0))
    return out


def residual_plan(n):
    order = []
    for i in range(NT + 2):
        if i <= NT:
            order.append((f"b{n}", i))
        if i >= 1:
            order.append((f"f{n}", i - 1))
    return order


def psum_plan():
    order = ["par"] + [("n1", i) for i in range(NT + 1)]
    for i in range(NT + 1):
        order += [("kv", i)] + ([("kT", i - 1)] if i else [])
    order += ["cproj"]
    order += [("in", m, c) for m in range(8) for c in range(2)]
    order += ["C", "h0", ("SA", 0)]
    for j in range(NPAIR):
        order += ([("SA", j + 1)] if j + 1 < NPAIR else []) + [("SB", j)]
    for b in range(DB):
        order += [("sT", b), ("sP", b)]
    order += ["sc", "sps", "scT", "sov", "ix1", "ix2"]
    order += [("V", j) for j in range(NPAIR)]
    order += ["ys", "st"] + [("sst", q) for q in range(4)]
    order += [("bt", h) for h in range(NH)]
    n = len(attention_units())
    for a in range(n + 2):
        if a < n:
            order.append(("SC", a))
        if 1 <= a <= n:
            order.append(("TR", a - 1))
        if a >= 2:
            order.append(("PV", a - 2))
    order += [("wT", b) for b in range(DB)] + ["wS", "wP", "wO"]
    order += [("gT", b, g) for b in range(DB) for g in range(NKV)] + ["gS", "gP", "gO"]
    order += ["oT0", "oT1"]
    order += [("glu", m, c) for m in range(4) for c in range(2)]
    order += [("ss", c) for c in range(2)]
    order += [("n0", i) for i in range(NT + 1)]
    order += [("wo", m, c) for m in range(8) for c in range(2)]
    order += residual_plan(1)
    order += [("mn", i) for i in range(2)] + [("mk", c) for c in range(8)] + ["mT"]
    order += [("xq", m, c) for m in range(4) for c in range(2)]
    order += [("xT", b) for b in range(DB)] + ["xS", "xP", "xO"]
    for i in range(NT + 1):
        if i < NT:
            order += [("XS", i)]
        if i >= 1:
            order += [("XT", i - 1), ("XO", i - 1)]
    order += [("xo", m, c) for m in range(8) for c in range(2)]
    order += residual_plan(2)
    order += [("wi", m, c) for m in range(2 * NF) for c in range(2)]
    order += [("wf", m, c) for m in range(8) for c in range(2)]
    order += [("b3", i) for i in range(NT + 1)]
    return {k: n for n, k in enumerate(order)}


def hymba_step(nc, x_prompt, x_sample, cache_kv_cmp, cache_kv_sel, cache_kv_win, state_ssm_re, state_ssm_im,
               cache_mem_kv, page_table, mem_prompt, w_in, w_out, norm_g, grp_norm_g, cmp_pos, cmp_proj,
               rel_bias, ssm_a_re, ssm_a_im, ssm_b_re, ssm_b_im, ssm_c_re, ssm_c_im, ssm_d, ssm_log_dt,
               glu_w, glu_b, mem_norm_g, xq, xkv, xo, ffn_wi, ffn_wo,
               y_prompt, y_sample, p_kv_cmp, p_kv_sel, p_kv_win, p_ssm_re, p_ssm_im, p_mem_kv,
               s_kv_cmp, s_kv_sel, s_kv_win, s_ssm_re, s_ssm_im):
    U = psum_plan()
    AT = attention_units()
    ctx = ExitStack()
    with ctx:
        def sb(name, shape, dt=F32):
            return ctx.enter_context(nc.sbuf_tensor(name, shape, dt))

        def sem(name):
            return ctx.enter_context(nc.semaphore(name))

        ident = sb("ident", [P, P])
        flip = sb("flip", [P, P])
        ones = sb("ones", [P, P])
        same = sb("same", [64, 64])
        spread = sb("spread", [SLOTS, SL])
        block_of = sb("block_of", [P, 4])
        dt2 = sb("dt2", [NPAIR, 2])
        cols = sb("cols", [P, 120])
        d_rows = sb("d_rows", [P, NPAIR])
        gates = sb("gates", [P, NT + 1, NG])
        tab = sb("tab", [NH, 32])
        eps_c = sb("eps_c", [P, 1])
        st = sb("st", [P, 64])
        kcT = sb("kcT", [P, NKV, 32])
        vc = sb("vc", [32, NKV * HD])
        csum = sb("csum", [P, 2, 32])
        pblk = sb("pblk", [P, 2, P])
        osT = sb("osT", [P, 3, 64])
        V64 = sb("V64", [64, WIN + 1])
        yS = sb("yS", [P, 4, DB])
        uS = sb("uS", [P, 4, DB])
        apow = sb("apow", [P, 6, 2, NPAIR])
        line = sb("line", [SL, 64], U32)
        pline = sb("pline", [P, 4, DB], U32)
        ptc = sb("ptc", [P, DB], I32)
        tiny = sb("tiny", [P, 16], I32)
        tinyf = sb("tinyf", [P, 16])
        jota_i = sb("jota_i", [64, 64], I32)
        jota = sb("jota", [64, 64])
        ptrow = sb("ptrow", [64, NPAGE], I32)
        co = sb("co", [P, 2, NPAIR])

        A = sb("A", [P, 49504])

        def at(first, *shape):
            n = int(np.prod(shape))
            v = A[:, first:first + n]
            if len(shape) == 2:
                v = v.rearrange("p (a b) -> p a b", b=shape[1])
            elif len(shape) == 3:
                v = v.rearrange("p (a b c) -> p a b c", b=shape[1], c=shape[2])
            elif len(shape) == 4:
                v = v.rearrange("p (a b c d) -> p a b c d", b=shape[1], c=shape[2], d=shape[3])
            return v

        qT = at(0, 4, TC)
        vkeep = at(4128, NT, 2 * P)
        kTd = at(6176, 2, NKV, T)
        U2 = at(10272, NPAIR, NC)
        summ = at(14368, DB, 2 * P)
        kcTs = at(16416, DB, P)
        vcs = at(17440, DB, P)
        hT = at(18464, KD, TC)
        wkv = at(26720, KD, KVC + NG)
        gring = at(26720, 3, ROWS * 256)
        NS = 4
        wring = at(33056, NS, KD, P)
        xin = at(37152, 2, D)
        junk = at(39200, D)
        uTm = at(40224, 2, TC)
        kvst = at(42288, 2, KVC + NG)
        posP = at(43872, 256)
        cprod = at(44128, 2, 256)
        prow = at(44896, P)
        drow = at(45024, P)
        dtrow = at(49376, P)
        kvS = at(45152, KVC)
        H = at(18464, NC + 1, 2, NPAIR)
        CP = at(37152, 2, NPAIR, 5, 32)
        Tm = [at(42272, P), at(43296, P)]
        Wm = [at(42400, 2, P), at(43424, 2, P)]
        sTm = Wm
        posB = at(43872, ROWS, P)
        WT = at(44896, 2, NPAIR, P)
        bb = at(18464, 2, NPAIR, 16)
        braw = at(18464 + 512, 2, NPAIR, 16)
        cc = at(18464 + 1024, 2, NPAIR, 16)
        q = at(18464 + 1536, 4, NPAIR, 16)
        craw = at(18464 + 2560, 8, HD)
        h0row = at(18464 + 3072, 2, 2048)
        V8 = at(46000, VL)
        prm = at(47200, 16, NPAIR)
        st_rows = at(44352, P)
        sst_rows = at(40224, 4 * D)
        r1 = at(44896, 16, 2, NPAIR)
        r2 = at(44896 + 512, 16, 2, NPAIR)
        apw = at(44896 + 1024, 15, 2, NPAIR)
        us3 = at(42656, NPAIR, DB)
        h0T = at(42784, 2, NPAIR, DB)
        hs = at(49024, 2, NPAIR, DB)
        yF = at(44896, 4, TC)
        SQ = at(37152, 4, TC)
        RS = at(41280, TC)
        oF = at(26720, 4, TC)
        scr = at(17952, 512)
        junk2 = at(14368, D)
        BT = at(18464, NH, T)
        far = at(37152, NH, P)
        Pm = at(38176, 2, T)
        PT = at(40224, 2, T)
        hank = at(38176, 2, T)
        oN = at(10272, NT, NH * HD)
        nbuf = at(18464, DB, 4, 256)
        kTw = at(37152, DB, 512)
        Pw = at(41248, 512)
        PTw = at(41760, 4, 64)
        Pc = at(14368, P)
        PcT = at(14496, 64)
        score = at(14560, 64)
        score2 = at(14624, 64)
        top = at(14688, 16)
        topi = at(14704, 16).bitcast(U32)
        pick = at(14720, 16)
        phys = at(14736, 16)
        is62 = at(14752, 16)
        p15 = at(14768, 64)
        cbias = at(14832, P)
        jphys = at(15024, 64)
        onehot = at(15152, SLOTS, 64)
        sbias = at(15152, ROWS, SK)
        sdiff = at(16128, PICK, LINES)
        kTs = at(37152, DB, ROWS, SK)
        Vs = at(18464, 2 * DB, ROWS, HD)
        Ps = at(10272 + 4096, ROWS, SK)
        PTs = at(10272 + 4096 + 1024, ROWS, 64)
        qz = sb("qz", [P, DB, 64])
        oS = at(16416, 3, NH * HD)
        mT = hT
        x1 = at(0, NT + 1, D)
        yT = at(37152, KD, TC)
        q2T = at(26720, XH, TC)
        mkv = at(30848, 2, D)
        mkT = at(46432, XH, NM)
        grow = at(45408, D)
        tb = at(47456, 2, D)
        Px = at(10272, 2, XH * NM)
        PTx = at(12320, 2, XH * NM)
        kst = at(14368, 2, 2, 512)
        qxz = at(16416, XH, DB, 32)
        mrow = at(10272, 2, D)
        memT = at(12320, KD, NM)
        Vm = at(18464, DB, 2, 512)
        kTm = at(37152, DB, XH, NM)
        Pxs = at(17440, NM)
        PTxs = at(17440 + 256, 2, 32)
        sT = at(17440 + 320, 1)

        def g_tile(k):
            if k < 8:
                return at(9216 + k * TC, TC)
            if k < 14:
                return at(26720 + (k - 8) * TC, TC)
            return at(37152 + (k - 14) * TC, TC)

        PS = ctx.enter_context(nc.psum_tensor("PS", [P, 8, 512], F32))

        def slot(key):
            s = U[key] % 4
            return PS[:, 2 * s:2 * s + 2, :].rearrange("p a b -> p (a b)")

        def chunked(key):
            s = U[key] % 4
            return PS[:, 2 * s:2 * s + 2, 0:CH]

        bias_dram = nc.dram_tensor("bias_by_distance", [NH, VL], F32, kind="Internal").ap()
        win_row = nc.dram_tensor("new_window_row", [DB, 256], F32, kind="Internal").ap()
        sel_row = nc.dram_tensor("new_selected_row", [DB, 256], F32, kind="Internal").ap()

        filled = sem("filled")
        emptied = [sem(f"emptied{s}") for s in range(4)]
        w_loaded = [sem(f"w_loaded{s}") for s in range(NS)]
        w_spent = sem("w_spent")
        consts = sem("consts")
        params = sem("params")
        x_in = [sem(f"x_in{s}") for s in range(2)]
        wkv_in = sem("wkv_in")
        pos_in = sem("pos_in")
        pblk_zero = sem("pblk_zero")
        tab_in = sem("tab_in")
        s5_arg = sem("s5_arg")
        s5_fun = sem("s5_fun")
        win_stored = sem("win_stored")
        states_staged = sem("states_staged")
        res_stat2 = sem("res_stat2")
        mem_stat = sem("mem_stat")
        on_stat = sem("on_stat")
        pw_stat = sem("pw_stat")
        px_stat = sem("px_stat")
        oF_ready = sem("oF_ready")
        mkv_out = sem("mkv_out")
        qxz_zero = sem("qxz_zero")
        lanes = sem("lanes")
        b_in = sem("b_in")
        c_in = sem("c_in")
        xn_ready = sem("xn_ready")
        rt_ready = sem("rt_ready")
        kv_stored = [sem(f"kv_stored{s}") for s in range(2)]
        kv_ready = sem("kv_ready")
        prod_ready = sem("prod_ready")
        rows_saved = sem("rows_saved")
        gat = [sem(f"gat{s}") for s in range(3)]
        gat_used = sem("gat_used")
        posB_in = sem("posB_in")
        posB_used = sem("posB_used")
        summ_ready = sem("summ_ready")
        pline_ready = sem("pline_ready")
        pt_in = sem("pt_in")
        s5_built = sem("s5_built")
        s5_states = sem("s5_states")
        hs_ready = sem("hs_ready")
        u_moved = sem("u_moved")
        uT_ready = sem("uT_ready")
        qz_ready = sem("qz_ready")
        pc_ready = sem("pc_ready")
        phys_ready = sem("phys_ready")
        line_ready = sem("line_ready")
        v8_ready = sem("v8_ready")
        v8_out = sem("v8_out")
        V64_in = sem("V64_in")
        hank_in = [sem(f"hank_in{s}") for s in range(2)]
        far_ready = sem("far_ready")
        bt_ready = sem("bt_ready")
        raw_ready = sem("raw_ready")
        exp_ready = sem("exp_ready")
        branch_done = sem("branch_done")
        nbuf_in = sem("nbuf_in")
        nrow_in = sem("nrow_in")
        vs_ready = sem("vs_ready")
        pw_raw = sem("pw_raw")
        pw_exp = sem("pw_exp")
        pw_ready = sem("pw_ready")
        oS_ready = sem("oS_ready")
        y_ready = sem("y_ready")
        gelu_ready = sem("gelu_ready")
        sq_ready = sem("sq_ready")
        ssr_ready = sem("ssr_ready")
        m_ready = sem("m_ready")
        on_ready = sem("on_ready")
        x1_in = sem("x1_in")
        grow_in = sem("grow_in")
        tb_free = sem("tb_free")
        res_stat = sem("res_stat")
        res_sum = sem("res_sum")
        res_norm = sem("res_norm")
        mem_in = sem("mem_in")
        mem_norm = sem("mem_norm")
        vm_in = sem("vm_in")
        kst_in = [sem(f"kst_in{s}") for s in range(2)]
        qxz_ready = sem("qxz_ready")
        px_raw = sem("px_raw")
        px_exp = sem("px_exp")
        px_ready = sem("px_ready")
        silu_ready = sem("silu_ready")
        g_ready = sem("g_ready")
        states_out = sem("states_out")
        out_ready = sem("out_ready")
        stored = sem("stored")
        dve_own = sem("dve_own")
        act_own = sem("act_own")
        pool_own = sem("pool_own")

        def full(eng, key):
            eng.wait_ge(filled, U[key] + 1)

        def read_out(eng, key):
            eng.wait_ge(emptied[U[key] % 4], U[key] // 4 + 1)

        def free(ins, key):
            ins.then_inc(emptied[U[key] % 4], 1)

        class Own:

            def __init__(self, eng, s):
                self.eng, self.sem, self.n = eng, s, 0

            def step(self, ins):
                ins.then_inc(self.sem, 1)
                self.n += 1

            def settle(self):
                self.eng.wait_ge(self.sem, self.n)

            def then(self, ins):
                self.step(ins)
                self.settle()

        stream = []
        wi_, wo_ = w_in[0], w_out[0]
        for m in range(8):
            c0 = m * P if m < 4 else OFF_U + (m - 4) * P
            stream.append((wi_[:, c0:c0 + P], KD, ("in", m, 1)))
        for m in range(4):
            stream.append((glu_w[0][:, m * P:(m + 1) * P], 4, ("glu", m, 1)))
        for m in range(8):
            stream.append((wo_[:, m * P:(m + 1) * P], KD, ("wo", m, 1)))
        for m in range(8):
            stream.append((xkv[0][:, m * P:(m + 1) * P], KD, ("mk", m)))
        for m in range(4):
            stream.append((xq[0][:, m * P:(m + 1) * P], KD, ("xq", m, 1)))
        for m in range(8):
            stream.append((xo[0][:, m * P:(m + 1) * P], 4, ("xo", m, 1)))
        for m in range(2 * NF):
            c0 = (m // 2) * P + (m % 2) * DFF
            stream.append((ffn_wi[0][:, c0:c0 + P], KD, ("wi", m, 1)))
        WFK = [8, 8, 6]
        for m in range(8):
            r = 0
            for n, kt in enumerate(WFK):
                stream.append((ffn_wo[0][r * P:(r + kt) * P, m * P:(m + 1) * P], kt,
                               ("wf", m, 1) if n == 2 else None))
                r += kt

        block = ctx.enter_context(nc.Block())

        @block.sync
        def _(sp):
            for i in range(NT + 1):
                c0, n = token_tile(i)
                if i >= 2:
                    full(sp, ("n1", i - 2))
                src = x_prompt[0, c0:c0 + n, :] if i < NT else x_sample[:, 0, :]
                sp.dma_start(xin[0:n, i % 2, :], src).then_inc(x_in[i % 2], 16)
                if i == 1:
                    sp.dma_start(wkv, wi_[:, NH * HD:OFF_U].rearrange("(k p) n -> p k n", p=P)).then_inc(wkv_in, 16)
            spent = 0
            for it, (src, kt, _) in enumerate(stream):
                if it >= NS:
                    if stream[it - NS][2] is None:
                        spent += 1
                        sp.wait_ge(w_spent, spent)
                    else:
                        full(sp, stream[it - NS][2])
                sp.dma_start(wring[:, it % NS, 0:kt, :],
                             src.rearrange("(k p) n -> p k n", p=P)).then_inc(w_loaded[it % NS], 16)

        @block.tensor
        def _(pe):
            item = [0]

            def open_(key):
                if U[key] >= 4:
                    pe.wait_ge(emptied[U[key] % 4], U[key] // 4)
                return slot(key)

            def mm(out, lhsT, rhs, start=True, stop=True):
                return nc.tensor.matmul(out, lhsT=lhsT, rhs=rhs, start=start, stop=stop, skip_group_check=True)

            def tr(out, in_):
                b, n = in_.base_partition(), in_.shape[0]
                return nc.tensor.transpose(out, in_, ident[b:b + n, b:b + n])

            def next_weights():
                it = item[0]
                item[0] += 1
                pe.wait_ge(w_loaded[it % NS], 16 * (it // NS + 1))
                return wring[:, it % NS]

            def dense(stage, tiles, kts, rhs, before=None):
                for m in range(tiles):
                    if before:
                        before(m)
                    a, b = (stage, m, 0), (stage, m, 1)
                    open_(a)
                    open_(b)
                    outs = [chunked(a)[:, 0], chunked(a)[:, 1], chunked(b)[:, 0]]
                    k, last = 0, sum(kts) - 1
                    for n, kt in enumerate(kts):
                        w = next_weights()
                        for kk in range(kt):
                            r = rhs(k)
                            for c in range(3):
                                ins = mm(outs[c], w[:, kk], r[:, c * CH:(c + 1) * CH], k == 0, k == last)
                                if k == last and c >= 1:
                                    ins.then_inc(filled, 1)
                            k += 1
                        if n < len(kts) - 1:
                            ins.then_inc(w_spent, 1)

            pe.wait_ge(consts, 5)
            pe.wait_ge(params, 16 * PARAM_DMAS)
            s = open_("par")
            tr(s[:, 0:104], prow[0:104])
            tr(s[:, 104:120], dtrow[0:NPAIR])
            tr(s[:, 128:128 + NPAIR], drow[0:NPAIR]).then_inc(filled, 1)

            for i in range(NT + 1):
                n = token_tile(i)[1]
                pe.wait_ge(xn_ready, i + 1)
                s = open_(("n1", i))
                for k in range(KD):
                    ins = tr(s[:, k * P:k * P + n], xin[0:n, i % 2, k * P:(k + 1) * P])
                ins.then_inc(filled, 1)

            def kv_transposes(i):
                pe.wait_ge(prod_ready, i + 1)
                s = open_(("kT", i))
                for br in range(2):
                    tr(s[:, br * P:(br + 1) * P], kvst[:, i % 2, 256 * (br + 1):256 * (br + 1) + P])
                for c in range(2):
                    ins = mm(s[:, 256 + 4 * c:260 + 4 * c], cprod[:, i % 2, c * P:(c + 1) * P], block_of[:, :])
                ins.then_inc(filled, 1)

            pe.wait_ge(wkv_in, 16)
            for i in range(NT + 1):
                c0, n = token_tile(i)
                read_out(pe, ("n1", i))
                s = open_(("kv", i))
                for k in range(KD):
                    mm(s[0:n, 0:512], hT[:, k, c0:c0 + n], wkv[:, k, 0:512], k == 0, k == KD - 1)
                    ins = mm(s[0:n, 512:KVC + NG], hT[:, k, c0:c0 + n], wkv[:, k, 512:KVC + NG], k == 0, k == KD - 1)
                ins.then_inc(filled, 1)
                if i:
                    kv_transposes(i - 1)
            read_out(pe, ("kT", NT - 1))
            s = open_("cproj")
            mm(s[:, 0:32], pblk[:, 0], csum[:, 0])
            mm(s[0:32, 32:32 + P], csum[:, 1], pblk[:, 1]).then_inc(filled, 1)

            dense("in", 8, [KD], lambda k: hT[:, k])

            pe.wait_ge(c_in, 64)
            s = open_("C")
            for n in range(8):
                ins = tr(s[0:HD, n * P:(n + 1) * P], craw[:, n])
            ins.then_inc(filled, 1)
            s = open_("h0")
            for part in range(2):
                for j in range(NPAIR):
                    c = (part * NPAIR + j) * DB
                    ins = tr(s[:, c:c + DB], h0row[0:DB, part, j * P:(j + 1) * P])
            ins.then_inc(filled, 1)

            def s5_matrices(j):
                s = open_(("SA", j))
                for part in range(2):
                    tr(s[:, part * P:(part + 1) * P], WT[:, part, j])
                for l in range(L4):
                    for part in range(2):
                        ins = mm(s[32 * l:32 * l + 32, 512 + 32 * l:640], WT[:, part, j, 96:P],
                                 CP[:, part, j, 0:L4 - l].rearrange("p k c -> p (k c)"), part == 0, part == 1)
                ins.then_inc(filled, 1)

            pe.wait_ge(s5_built, 1)
            pe.wait_ge(u_moved, 1)
            s5_matrices(0)
            for j in range(NPAIR):
                if j + 1 < NPAIR:
                    s5_matrices(j + 1)
                read_out(pe, ("SA", j))
                s = open_(("SB", j))
                for part in range(2):
                    mm(s[:, part * NC:(part + 1) * NC], Wm[j % 2][:, part], U2[:, j])
                for part in range(2):
                    mm(s[:, 512 + part * DB:512 + (part + 1) * DB], Wm[j % 2][96:P, part], us3[96:P, j])
                mm(s[:, 528:528 + NC], Tm[j % 2], U2[:, j]).then_inc(filled, 1)

            for b in range(DB):
                pe.wait_ge(summ_ready, b + 1)
                s = open_(("sT", b))
                for c in range(2):
                    ins = tr(s[:, c * P:(c + 1) * P], summ[:, b, c * P:(c + 1) * P])
                ins.then_inc(filled, 1)
                read_out(pe, ("sT", b))
                s = open_(("sP", b))
                mm(s[:, 0:P], pblk[:, 0], sTm[b % 2][:, 0])
                mm(s[:, P:2 * P], sTm[b % 2][:, 1], pblk[:, 1]).then_inc(filled, 1)
            read_out(pe, ("sP", DB - 1))
            read_out(pe, ("sP", DB - 2))
            pe.wait_ge(qz_ready, 1)
            s = open_("sc")
            for b in range(DB):
                ins = mm(s[0:64, 0:P], qz[:, b], kcTs[:, b], b == 0, b == DB - 1)
            ins.then_inc(filled, 1)
            pe.wait_ge(pc_ready, 1)
            s = open_("sps")
            mm(s[0:64, 0:P], same[:, :], Pc[0:64]).then_inc(filled, 1)
            s = open_("scT")
            tr(s[:, 0:64], Pc[0:64]).then_inc(filled, 1)
            read_out(pe, "scT")
            s = open_("sov")
            for b in range(DB):
                ins = mm(s[:, b * 8:b * 8 + 8], vcs[:, b], PcT[:, b * 8:b * 8 + 8])
            ins.then_inc(filled, 1)
            pe.wait_ge(phys_ready, 1)
            s = open_("ix1")
            tr(s[0:SLOTS, 0:64], phys[0:64, 0:SLOTS]).then_inc(filled, 1)
            read_out(pe, "ix1")
            s = open_("ix2")
            mm(s[0:SL, 0:64], spread[:, :], p15[0:SLOTS]).then_inc(filled, 1)

            pe.wait_ge(s5_states, 1)
            for j in range(NPAIR):
                s = open_(("V", j))
                for part in range(2):
                    ins = mm(s[:, 0:NC], CP[:, part, j, 1:5].rearrange("p k c -> p (k c)"), H[:, 0:NC, part, j],
                             part == 0, part == 1)
                ins.then_inc(filled, 1)
            pe.wait_ge(hs_ready, 1)
            s = open_("ys")
            for j in range(NPAIR):
                q, m = j % 4, j // 4
                for part in range(2):
                    ins = mm(s[32 * q:32 * q + 32, m * DB:(m + 1) * DB], CP[:, part, j, 0], hs[:, part, j],
                             part == 0, part == 1)
            ins.then_inc(filled, 1)
            s = open_("st")
            tr(s[0:32, 0:P], H[:, NC].rearrange("p a j -> p (a j)")).then_inc(filled, 1)
            for q in range(4):
                s = open_(("sst", q))
                for n in range(8):
                    r = q * 8 + n
                    ins = tr(s[0:DB, n * P:(n + 1) * P], hs[:, r // NPAIR, r % NPAIR])
                ins.then_inc(filled, 1)

            for h in range(NH):
                pe.wait_ge(hank_in[h % 2], 16 * (h // 2 + 1))
                s = open_(("bt", h))
                for c in range(2):
                    ins = mm(s[:, c * 512:(c + 1) * 512], flip[:, :], hank[:, h % 2, c * 512:(c + 1) * 512])
                ins.then_inc(filled, 1)

            n_at = len(AT)

            def keys_of(a):
                i, h, br, k0, nk = AT[a]
                lo, g = 64 * (h % 2), h // GQ
                return kcT[lo:lo + 64, g, 0:nk] if br == 0 else kTd[lo:lo + 64, br - 1, g, k0:k0 + nk]

            for a in range(n_at + 2):
                if a < n_at:
                    i, h, br, k0, nk = AT[a]
                    lo = 64 * (h % 2)
                    s = open_(("SC", a))
                    ks = keys_of(a)
                    for c in range(0, nk, 512):
                        w = min(512, nk - c)
                        ins = mm(s[:, c:c + w], qT[lo:lo + 64, h // 2, i * P:(i + 1) * P], ks[:, c:c + w])
                    ins.then_inc(filled, 1)
                if 1 <= a <= n_at:
                    nk = AT[a - 1][4]
                    pe.wait_ge(exp_ready, a)
                    s = open_(("TR", a - 1))
                    for c in range(0, nk, P):
                        w = min(P, nk - c)
                        ins = tr(s[0:w, c:c + P], Pm[:, (a - 1) % 2, c:c + w])
                    ins.then_inc(filled, 1)
                if a >= 2:
                    i, h, br, k0, nk = AT[a - 2]
                    g = h // GQ
                    read_out(pe, ("TR", a - 2))
                    s = open_(("PV", a - 2))
                    tiles = max(1, nk // P)
                    for n in range(tiles):
                        if br == 0:
                            v, rows = vc[0:nk, g * HD:(g + 1) * HD], nk
                        else:
                            c = (br - 1) * P + g * HD
                            v, rows = vkeep[:, k0 // P + n, c:c + HD], P
                        ins = mm(s[:, 0:HD], PT[0:rows, (a - 2) % 2, n * P:(n + 1) * P], v, n == 0, n == tiles - 1)
                    ins.then_inc(filled, 1)

            pe.wait_ge(nbuf_in, 16 * 3 * DB)
            for b in range(DB):
                s = open_(("wT", b))
                for j in range(4):
                    ins = tr(s[:, j * P:(j + 1) * P], nbuf[:, b, j, 0:P])
                ins.then_inc(filled, 1)
            for b in range(DB - 4, DB):
                read_out(pe, ("wT", b))
            s = open_("wS")
            for b in range(DB):
                ins = mm(s[0:64, 0:512], qz[:, b], kTw[:, b], b == 0, b == DB - 1)
            ins.then_inc(filled, 1)
            pe.wait_ge(pw_ready, 1)
            s = open_("wP")
            for j in range(4):
                ins = tr(s[:, j * 64:(j + 1) * 64], Pw[0:64, j * P:(j + 1) * P])
            ins.then_inc(filled, 1)
            read_out(pe, "wP")
            s = open_("wO")
            for b in range(DB):
                for j in range(4):
                    ins = mm(s[:, b * 8:b * 8 + 8], nbuf[:, b, j, P:2 * P], PTw[:, j, b * 8:b * 8 + 8], j == 0, j == 3)
            ins.then_inc(filled, 1)

            for n in range(2 * DB):
                b, g = n // 2, n % 2
                pe.wait_ge(gat[n % 3], 16 * GAT0[n % 3] + 16 * 2 * (n // 3 + 1))
                s = open_(("gT", b, g))
                for r in range(ROWS):
                    c = r * SK if r < 4 else 512 + (r - 4) * SK
                    ins = tr(s[0:HD, c:c + SK], gring[0:SK, n % 3, r * 256 + g * HD:r * 256 + (g + 1) * HD])
                ins.then_inc(filled, 1)
            for n in range(2 * DB - 4, 2 * DB):
                read_out(pe, ("gT", n // 2, n % 2))
            s = open_("gS")
            for b in range(DB):
                for half in range(2):
                    ins = mm(s[0:64, half * 512:half * 512 + 4 * SK], qz[:, b],
                             kTs[:, b, 4 * half:4 * half + 4].rearrange("p r c -> p (r c)"), b == 0, b == DB - 1)
            ins.then_inc(filled, 1)
            pe.wait_ge(pw_ready, 2)
            s = open_("gP")
            for r in range(ROWS):
                ins = tr(s[0:SK, r * 64:(r + 1) * 64], Ps[0:64, r])
            ins.then_inc(filled, 1)
            read_out(pe, "gP")
            pe.wait_ge(vs_ready, 2 * DB)
            s = open_("gO")
            for n in range(2 * DB):
                b, g = n // 2, n % 2
                c = b * 8 + 4 * g
                for r in range(ROWS):
                    ins = mm(s[64 * g:64 * g + 64, c:c + 4], Vs[0:SK, n, r], PTs[0:SK, r, c:c + 4],
                             r == 0, r == ROWS - 1)
            ins.then_inc(filled, 1)
            read_out(pe, "sov")
            read_out(pe, "wO")
            read_out(pe, "gO")
            for key, brs in (("oT0", (0, 1)), ("oT1", (2,))):
                s = open_(key)
                for br in brs:
                    for h in range(NH):
                        g = h // GQ
                        c = g * 512 + (br % 2) * 256 + (h % GQ) * HD
                        ins = tr(s[0:DB, c:c + HD],
                                 osT[64 * g:64 * g + 64, br].rearrange("p (b h) -> p h b", h=NH)[:, h])
                ins.then_inc(filled, 1)

            pe.wait_ge(gelu_ready, 1)
            dense("glu", 4, [4], lambda k: yF[:, k])
            pe.wait_ge(sq_ready, 1)
            for c in range(2):
                s = open_(("ss", c))
                for n in range(2 - c):
                    for k in range(4):
                        c0 = (2 * c + n) * CH
                        ins = mm(chunked(("ss", c))[:, n], ones[:, :], SQ[:, k, c0:c0 + CH], k == 0, k == 3)
                ins.then_inc(filled, 1)
            for i in range(NT + 1):
                n = token_tile(i)[1]
                pe.wait_ge(on_ready, i + 1)
                s = open_(("n0", i))
                for k in range(4):
                    src = oN[:, i, k * P:(k + 1) * P] if i < NT else oS[0:DB, 0, k * P:(k + 1) * P]
                    ins = tr(s[:, k * P:k * P + n], src)
                ins.then_inc(filled, 1)
            pe.wait_ge(m_ready, 2)
            dense("wo", 8, [KD], lambda k: mT[:, k])

            def residual(n):
                last = {1: "wo", 2: "xo", 3: "wf"}[n]
                for m in (6, 7):
                    for c in range(2):
                        read_out(pe, (last, m, c))
                for i in range(NT + 2):
                    if i <= NT:
                        c0, r = token_tile(i)
                        s = open_((f"b{n}", i))
                        for k in range(KD):
                            ins = tr(s[0:r, k * P:(k + 1) * P], (hT if n == 3 else yT)[:, k, c0:c0 + r])
                        ins.then_inc(filled, 1)
                    if i >= 1 and n < 3:
                        c0, r = token_tile(i - 1)
                        pe.wait_ge(res_norm, (n - 1) * (NT + 1) + i)
                        s = open_((f"f{n}", i - 1))
                        for k in range(KD):
                            ins = tr(s[:, k * P:k * P + r], tb[0:r, (i - 1) % 2, k * P:(k + 1) * P])
                        ins.then_inc(filled, 1)

            residual(1)

            for i in range(2):
                pe.wait_ge(mem_norm, i + 1)
                s = open_(("mn", i))
                for k in range(KD):
                    ins = tr(s[:, k * P:(k + 1) * P], mrow[:, i, k * P:(k + 1) * P])
                ins.then_inc(filled, 1)
            read_out(pe, ("mn", 0))
            read_out(pe, ("mn", 1))
            for c in range(8):
                w = next_weights()
                s = open_(("mk", c))
                for i in range(2):
                    for k in range(KD):
                        ins = mm(s[:, i * P:(i + 1) * P], memT[:, k, i * P:(i + 1) * P], w[:, k], k == 0, k == KD - 1)
                ins.then_inc(filled, 1)
            for c in range(4):
                read_out(pe, ("mk", c))
            s = open_("mT")
            for h in range(XH):
                for i in range(2):
                    ins = tr(s[:, (2 * h + i) * P:(2 * h + i + 1) * P], mkv[:, i, h * P:(h + 1) * P])
            ins.then_inc(filled, 1)
            for i in range(NT - 3, NT + 1):
                read_out(pe, ("f1", i))
            dense("xq", 4, [KD], lambda k: hT[:, k])

            for b in range(DB):
                pe.wait_ge(kst_in[b % 2], 16 * (b // 2 + 1))
                s = open_(("xT", b))
                for h in range(XH):
                    for i in range(2):
                        ins = tr(s[:, (2 * h + i) * P:(2 * h + i + 1) * P], kst[:, b % 2, i, h * P:(h + 1) * P])
                ins.then_inc(filled, 1)
            for b in range(DB - 4, DB):
                read_out(pe, ("xT", b))
            pe.wait_ge(qxz_ready, 1)
            s = open_("xS")
            for b in range(DB):
                for h in range(XH):
                    ins = mm(s[0:32, 0:NM], qxz[:, h, b], kTm[:, b, h], b + h == 0, b + h == DB + XH - 2)
            ins.then_inc(filled, 1)
            pe.wait_ge(px_ready, 1)
            s = open_("xP")
            for i in range(2):
                ins = tr(s[:, i * 32:(i + 1) * 32], Pxs[0:32, i * P:(i + 1) * P])
            ins.then_inc(filled, 1)
            read_out(pe, "xP")
            pe.wait_ge(vm_in, 16 * DB)
            s = open_("xO")
            for b in range(DB):
                for h in range(XH):
                    for i in range(2):
                        ins = mm(s[:, h * DB + b:h * DB + b + 1], Vm[:, b, i, h * P:(h + 1) * P],
                                 PTxs[:, i, b * XH + h:b * XH + h + 1], i == 0, i == 1)
            ins.then_inc(filled, 1)

            read_out(pe, "mT")
            for i in range(NT + 1):
                if i < NT:
                    s = open_(("XS", i))
                    for h in range(XH):
                        ins = mm(s[:, h * NM:(h + 1) * NM], q2T[:, h, i * P:(i + 1) * P], mkT[:, h])
                    ins.then_inc(filled, 1)
                if i >= 1:
                    pe.wait_ge(px_ready, i + 1)
                    s = open_(("XT", i - 1))
                    for c in range(8):
                        ins = tr(s[:, c * P:(c + 1) * P], Px[:, (i - 1) % 2, c * P:(c + 1) * P])
                    ins.then_inc(filled, 1)
                    read_out(pe, ("XT", i - 1))
                    s = open_(("XO", i - 1))
                    for h in range(XH):
                        for c in range(2):
                            ins = mm(s[:, h * P:(h + 1) * P], mkv[:, c, 512 + h * P:512 + (h + 1) * P],
                                     PTx[:, (i - 1) % 2, (2 * h + c) * P:(2 * h + c + 1) * P], c == 0, c == 1)
                    ins.then_inc(filled, 1)
            read_out(pe, "xO")
            for i in range(NT - 2, NT):
                read_out(pe, ("XO", i))
            dense("xo", 8, [4], lambda k: q2T[:, k])
            residual(2)

            for i in range(NT - 3, NT + 1):
                read_out(pe, ("f2", i))
            dense("wi", 2 * NF, [KD], lambda k: hT[:, k])
            pe.wait_ge(g_ready, NF)
            dense("wf", 8, WFK, g_tile)
            residual(3)

        @block.gpsimd
        def _(pool):
            own = Own(pool, pool_own)
            g = nc.gpsimd

            own.step(g.memset(ident[:, :], 0.0))
            own.step(g.memset(flip[:, :], 0.0))
            own.step(g.memset(same[:, :], 1.0))
            own.step(g.memset(block_of[:, :], 1.0))
            own.step(g.memset(spread[:, :], 0.0))
            own.step(g.memset(qz[:, :, :], 0.0))
            g.memset(pblk[:, :, :], 0.0).then_inc(pblk_zero, 1)
            own.settle()
            g.affine_select(out=ident[:, :], in_=ident[:, :], compare_op=ALU.not_equal, fill=1.0, base=0,
                            pattern=[[-1, P]], channel_multiplier=1).then_inc(consts, 1)
            own.step(g.memset(ones[:, :], 1.0))
            g.affine_select(out=flip[:, :], in_=flip[:, :], compare_op=ALU.not_equal, fill=1.0, base=1 - P,
                            pattern=[[1, P]], channel_multiplier=1).then_inc(consts, 1)
            own.step(g.affine_select(out=same[:, :], in_=same[:, :], compare_op=ALU.is_ge, fill=0.0, base=0,
                                     pattern=[[-4, 16], [0, 4]], channel_multiplier=1))
            own.step(g.affine_select(out=block_of[:, :], in_=block_of[:, :], compare_op=ALU.is_ge, fill=0.0, base=0,
                                     pattern=[[-CB, 4]], channel_multiplier=1))
            own.step(g.iota(tiny[:, 0:1], pattern=[[0, 1]], base=0, channel_multiplier=1))
            own.step(g.iota(jota_i[:, :], pattern=[[1, 64]], base=0, channel_multiplier=0))
            own.settle()
            own.step(g.affine_select(out=same[:, :], in_=same[:, :], compare_op=ALU.is_ge, fill=0.0, base=3,
                                     pattern=[[4, 16], [0, 4]], channel_multiplier=-1))
            own.step(g.affine_select(out=spread[:, :], in_=spread[:, :], compare_op=ALU.not_equal, fill=1.0, base=0,
                                     pattern=[[-1, SLOTS], [0, LINES]], channel_multiplier=1))
            g.affine_select(out=block_of[:, :], in_=block_of[:, :], compare_op=ALU.is_ge, fill=0.0, base=CB - 1,
                            pattern=[[CB, 4]], channel_multiplier=-1).then_inc(consts, 1)
            own.settle()
            g.memset(eps_c[:, :], EPS).then_inc(consts, 1)

            pool.wait_ge(params, 16 * PARAM_DMAS)
            g.tensor_copy(dtrow[0:NPAIR].rearrange("j (a p) -> j a p", a=2),
                          dt2[:, :].unsqueeze(2).to_broadcast([NPAIR, 2, 64])).then_inc(consts, 1)

            pool.wait_ge(tab_in, 16)
            own.then(g.tensor_scalar(tab[:, :], tab[:, :], 1.0 / SC, None, ALU.mult))
            for bucket, d0, d1 in bucket_ranges():
                own.step(g.tensor_copy(V8[0:NH, T - 1 - d1:T - d0],
                                       tab[:, bucket:bucket + 1].to_broadcast([NH, d1 - d0 + 1])))
            own.step(g.memset(V8[0:NH, T:VL], NEG))
            own.settle()
            pool.dma_start(bias_dram, V8[0:NH]).then_inc(v8_out, 16)
            pool.wait_ge(v8_out, 16)
            pool.dma_start(V64[:, :], bass.AP(bias_dram.tensor, T - 1 - WIN, [[0, DB], [VL, NH], [1, WIN + 1]]))\
                .then_inc(V64_in, 16)

            for i in range(NT + 1):
                pool.wait_ge(kv_ready, i + 1)
                if i < NT:
                    rows = slice(i * P, (i + 1) * P)
                    k = kvst[:, i % 2]
                    done = kv_stored[i % 2]
                    pool.dma_start(p_kv_cmp[0, 0, rows].rearrange("s c g d -> s (c g d)"), k[:, 0:256]).then_inc(done, 16)
                    pool.dma_start(p_kv_sel[0, 0, rows].rearrange("s c g d -> s (c g d)"), k[:, 256:512]).then_inc(done, 16)
                    if i >= NT - WIN // P:
                        w = slice(i * P - (T - WIN), (i + 1) * P - (T - WIN))
                        pool.dma_start(p_kv_win[0, 0, w].rearrange("s c g d -> s (c g d)"), k[:, 512:768]).then_inc(done, 16)
                else:
                    pool.dma_start(s_kv_cmp[0, :, 0].rearrange("b c g d -> b (c g d)"), kvS[0:DB, 0:256]).then_inc(rows_saved, 16)
                    pool.dma_start(s_kv_sel[0, :, 0].rearrange("b c g d -> b (c g d)"), kvS[0:DB, 256:512]).then_inc(rows_saved, 16)
                    pool.dma_start(sel_row, kvS[0:DB, 256:512]).then_inc(rows_saved, 16)
                    pool.dma_start(win_row, kvS[0:DB, 512:768]).then_inc(rows_saved, 16)

            pool.wait_ge(pline_ready, 1)
            full(pool, "cproj")
            pool_c = cache_kv_cmp[0].rearrange("n (a r) c g d -> (n a) (r c g d)", r=ROWS)
            for n in range(4 * DB):
                k, b = n // DB, n % DB
                if n >= 3:
                    pool.wait_ge(gat_used, n - 2)
                if b == 0:
                    if k:
                        pool.wait_ge(gat_used, n)
                    for c in range(2):
                        pool.dma_start(posB[:, :, c * HD:(c + 1) * HD],
                                       bass.AP(cmp_pos.tensor, (c * CB + k * ROWS) * HD,
                                               [[0, P], [HD, ROWS], [1, HD]])).then_inc(posB_in, 16)
                pool.indirect_dma_start(out=gring[:, n % 3], out_offset=None, in_=pool_c,
                                        in_offset=bass.IndirectOffsetOnAxis(ap=pline[:, k, b:b + 1], axis=0))\
                    .then_inc(gat[n % 3], 16)

            pool.wait_ge(gat_used, 4 * DB)
            full(pool, "ys")
            for h in range(NH):
                if h >= 2:
                    full(pool, ("bt", h - 2))
                pool.dma_start(hank[:, h % 2], bass.AP(bias_dram.tensor, h * VL, [[1, P], [1, T]]))\
                    .then_inc(hank_in[h % 2], 16)
            pool.wait_ge(states_staged, 1)
            pool.dma_start(p_ssm_re[0, 0].rearrange("(j a) p -> j (a p)", a=2), st_rows[0:NPAIR]).then_inc(states_out, 16)
            pool.dma_start(p_ssm_im[0, 0].rearrange("(j a) p -> j (a p)", a=2), st_rows[NPAIR:2 * NPAIR]).then_inc(states_out, 16)
            pool.wait_ge(states_staged, 2)
            pool.dma_start(s_ssm_re[0].rearrange("b g p -> b (g p)"), sst_rows[0:DB, 0:2048]).then_inc(states_out, 16)
            pool.dma_start(s_ssm_im[0].rearrange("b g p -> b (g p)"), sst_rows[0:DB, 2048:4096]).then_inc(states_out, 16)
            read_out(pool, ("bt", NH - 1))
            for h in range(NH):
                g.affine_select(out=far[:, h], in_=BT[:, h, T - P - WIN:T - WIN], compare_op=ALU.is_gt, fill=NEG,
                                base=0, pattern=[[1, P]], channel_multiplier=-1).then_inc(far_ready, 1)

            pool_s = cache_kv_sel[0].rearrange("n (a r) c g d -> (n a) (r c g d)", r=ROWS)

            def gather(n):
                b, gg = n // 2, n % 2
                col = b * 8 + 4 * gg
                pool.indirect_dma_start(out=gring[0:SL, n % 3], out_offset=None, in_=pool_s,
                                        in_offset=bass.IndirectOffsetOnAxis(ap=line[:, col:col + 1], axis=0))\
                    .then_inc(gat[n % 3], 16)
                pool.dma_start(gring[SL:SK, n % 3, 0:256], sel_row[b:b + 1]).then_inc(gat[n % 3], 16)

            pool.wait_ge(line_ready, 1)
            for n in range(3):
                gather(n)

            last = len(AT) - 1
            for a in range(last - 3, last + 1):
                read_out(pool, ("SC", a))
            pool.wait_ge(rows_saved, 64)
            for b in range(DB):
                pool.dma_start(nbuf[0:P - 1, b].rearrange("p r c -> p (r c)"),
                               bass.AP(cache_kv_win.tensor, (b * WIN + 1) * 256, [[1024, P - 1], [1, 1024]])).then_inc(nbuf_in, 16)
                pool.dma_start(nbuf[P - 1:P, b, 0:3].rearrange("p r c -> p (r c)"),
                               bass.AP(cache_kv_win.tensor, (b * WIN + WIN - 3) * 256, [[768, 1], [1, 768]])).then_inc(nbuf_in, 16)
                pool.dma_start(nbuf[P - 1:P, b, 3], win_row[b:b + 1]).then_inc(nbuf_in, 16)
            pool.wait_ge(nbuf_in, 16 * 3 * DB)
            for b in range(DB):
                pool.dma_start(s_kv_win[0, b].rearrange("(p r) c g d -> p (r c g d)", r=4),
                               nbuf[:, b].rearrange("p r c -> p (r c)")).then_inc(win_stored, 16)
            for n in range(3, 2 * DB):
                full(pool, ("gT", (n - 3) // 2, (n - 3) % 2))
                pool.wait_ge(vs_ready, n - 2)
                gather(n)

            full(pool, ("f1", NT))
            g.memset(qxz, 0.0).then_inc(qxz_zero, 1)
            for b in range(DB):
                if b >= 2:
                    full(pool, ("xT", b - 2))
                if b == 0:
                    full(pool, ("mn", 1))
                kv = cache_mem_kv[0, b].rearrange("(i p) c h d -> p i c (h d)", p=P)
                pool.dma_start(kst[:, b % 2], kv[:, :, 0]).then_inc(kst_in[b % 2], 16)
            full(pool, ("xq", XH - 1, 1))
            for b in range(DB):
                kv = cache_mem_kv[0, b].rearrange("(i p) c h d -> p i c (h d)", p=P)
                pool.dma_start(Vm[:, b], kv[:, :, 1]).then_inc(vm_in, 16)
            for c in range(4, 8):
                read_out(pool, ("mk", c))
            pool.dma_start(p_mem_kv[0, 0].rearrange("(i p) c h d -> p i (c h d)", p=P), mkv).then_inc(mkv_out, 16)

            for i in range(NT + 1):
                n = token_tile(i)[1]
                pool.wait_ge(out_ready, i + 1)
                dst = y_prompt[0, i * P:(i + 1) * P] if i < NT else y_sample[:, 0]
                pool.dma_start(dst, x1[0:n, i]).then_inc(stored, 16)
            pool.wait_ge(stored, 16 * (NT + 1))
            pool.wait_ge(mkv_out, 16)
            pool.wait_ge(win_stored, 16 * DB)
            pool.wait_ge(states_out, 64)
            pool.wait_ge(rows_saved, 64)
            pool.wait_ge(kv_stored[0], 16 * (2 * 4 + 2))
            pool.wait_ge(kv_stored[1], 16 * (2 * 4 + 2))

        @block.scalar
        def _(act):
            own = Own(act, act_own)
            a_ = nc.scalar

            def f(out, in_, func=ACT.Copy, **kw):
                return a_.activation(out, in_, func, **kw)

            ng = norm_g[0].rearrange("n (k p) -> (n k) p", p=P)
            act.dma_start(prow[0:48], ng).then_inc(params, 16)
            act.dma_start(prow[48:56], grp_norm_g[0].rearrange("(k p) -> k p", p=P)).then_inc(params, 16)
            act.dma_start(prow[56:64], mem_norm_g[0].rearrange("(k p) -> k p", p=P)).then_inc(params, 16)
            act.dma_start(prow[64:68], glu_b[0].rearrange("(k p) -> k p", p=P)).then_inc(params, 16)
            act.dma_start(prow[68:72], ssm_d[0].rearrange("(k p) -> k p", p=P)).then_inc(params, 16)
            act.dma_start(prow[72:88], ssm_a_re[0].rearrange("(j a) p -> j (a p)", a=2)).then_inc(params, 16)
            act.dma_start(prow[88:104], ssm_a_im[0].rearrange("(j a) p -> j (a p)", a=2)).then_inc(params, 16)
            act.dma_start(dt2[:, :], ssm_log_dt[0].rearrange("(j a) -> j a", a=2)).then_inc(params, 16)
            act.dma_start(drow[0:NPAIR].rearrange("j (l c) -> j l c", l=L4),
                          bass.AP(ssm_d.tensor, 0, [[32, NPAIR], [0, L4], [1, 32]])).then_inc(params, 16)
            with nc.allow_non_contiguous_dma(reason="a table of 32 by 8, transposed"):
                act.dma_start(tab[:, :], rel_bias.rearrange("b h -> h b")).then_inc(tab_in, 16)
            for n in range(4):
                for c in range(2):
                    act.dma_start(posP[32 * n:32 * n + 32, c * P:(c + 1) * P].rearrange("l (g d) -> l g d", g=2),
                                  bass.AP(cmp_pos.tensor, c * CB * HD, [[HD, CB], [0, NKV], [1, HD]])).then_inc(pos_in, 16)
            act.wait_ge(pblk_zero, 1)
            for c in range(2):
                for h in range(2):
                    act.dma_start(pblk[64 * h:64 * h + 64, c, 64 * h:64 * h + 64], cmp_proj[0, c]).then_inc(pos_in, 16)
            with nc.allow_non_contiguous_dma(reason="page numbers, one for each compressed block"):
                for b in range(DB):
                    act.dma_start(ptc[:, b:b + 1], bass.AP(page_table.tensor, b * NPAGE, [[1, NPAGE], [0, 4], [1, 1]])).then_inc(pt_in, 16)
            act.dma_start(ptrow[:, :], bass.AP(page_table.tensor, 0, [[NPAGE, DB], [0, NH], [1, NPAGE]])).then_inc(pt_in, 16)

            act.wait_ge(s5_arg, 1)
            f(prm[:, 0], cols[:, 104:120], ACT.Exp).then_inc(s5_fun, 1)
            act.wait_ge(s5_arg, 2)
            f(prm[:, 2], prm[:, 1], ACT.Exp).then_inc(s5_fun, 1)
            own.step(f(prm[:, 5], prm[:, 4], ACT.Sin))
            f(prm[:, 7], prm[:, 6], ACT.Sin).then_inc(s5_fun, 1)

            act.wait_ge(consts, 4)
            for i in range(NT + 1):
                n = token_tile(i)[1]
                act.wait_ge(x_in[i % 2], 16 * (i // 2 + 1))
                own.then(f(junk[0:n], xin[0:n, i % 2], ACT.Square, accum_out=st[0:n, i:i + 1]))
                f(st[0:n, 16 + i:17 + i], st[0:n, i:i + 1], ACT.Sqrt, scale=1.0 / D, bias=eps_c[0:n]).then_inc(rt_ready, 1)

            for i in range(NT + 1):
                n = token_tile(i)[1]
                full(act, ("kv", i))
                if i < NT:
                    if i >= 2:
                        u = i // 2
                        act.wait_ge(kv_stored[i % 2], 16 * (2 * u + max(0, u - 2)))
                        act.wait_ge(prod_ready, i - 1)
                        full(act, ("kT", i - 2))
                    dst = kvst[:, i % 2, 0:KVC]
                else:
                    dst = kvS[0:DB]
                f(dst, slot(("kv", i))[0:n, 0:KVC]).then_inc(kv_ready, 1)
                free(f(gates[0:n, i], slot(("kv", i))[0:n, KVC:KVC + NG], ACT.Sigmoid), ("kv", i))
                if i >= 1:
                    kt = i - 1
                    key = ("kT", kt)
                    full(act, key)
                    s = slot(key)[:, 0:256].rearrange("p (a t) -> p a t", a=2)
                    for half in range(2):
                        for g in range(NKV):
                            own.step(f(kTd[64 * half:64 * half + 64, :, g, kt * P:(kt + 1) * P], s[64 * g:64 * g + 64]))
                    free(f(csum[:, :, 4 * kt:4 * kt + 4], slot(key)[:, 256:264].rearrange("p (a t) -> p a t", a=2)), key)
            full(act, "cproj")
            for half in range(2):
                for g in range(NKV):
                    own.step(f(kcT[64 * half:64 * half + 64, g], slot("cproj")[64 * g:64 * g + 64, 0:32]))
            free(f(vc[:, :], slot("cproj")[0:32, 32:32 + P]), "cproj")

            def dense_out(stage, m, dst):
                for c in range(2):
                    key = (stage, m, c)
                    full(act, key)
                    if c == 0:
                        ins = f(dst[:, 0:2 * CH].rearrange("p (a n) -> p a n", a=2), chunked(key))
                    else:
                        ins = f(dst[:, 2 * CH:TC], chunked(key)[:, 0])
                    free(ins, key)

            for m in range(8):
                if m >= 6:
                    act.wait_ge(uT_ready, m - 5)
                dense_out("in", m, qT[:, m] if m < 4 else uTm[:, m % 2])

            with nc.allow_non_contiguous_dma(reason="rows of 16 numbers"):
                for part, src in enumerate((ssm_b_re, ssm_b_im)):
                    act.dma_start(braw[:, part], src[0].rearrange("(j a) p i -> (a p) j i", a=2)).then_inc(b_in, 16)
            for part, src in enumerate((ssm_c_re, ssm_c_im)):
                act.dma_start(craw[:, 4 * part:4 * part + 4],
                              src[0].rearrange("(q g) i p -> (g i) q p", g=8)).then_inc(c_in, 16)
            for part, src in enumerate((state_ssm_re, state_ssm_im)):
                act.dma_start(h0row[0:DB, part], src[0].rearrange("b g p -> b (g p)")).then_inc(c_in, 16)
            full(act, "C")
            for half in range(2):
                for part in range(2):
                    s = slot("C")[0:HD, part * 512:part * 512 + 512]\
                        .rearrange("p (q g i) -> p q g i", g=2, i=16)[:, :, half]
                    ins = f(cc[64 * half:64 * half + 64, part], s)
                    free(ins, "C") if half and part else own.step(ins)
            full(act, "h0")
            free(f(h0T.rearrange("p a j b -> p (a j b)"), slot("h0")[:, 0:2 * NPAIR * DB]), "h0")

            def s5_out(j):
                key = ("SA", j)
                full(act, key)
                if j >= 2:
                    full(act, ("SB", j - 2))
                s = slot(key)
                own.step(f(Wm[j % 2].rearrange("p a c -> p (a c)"), s[:, 0:256]))
                for l in range(L4):
                    ins = f(Tm[j % 2][32 * l:32 * l + 32, 32 * l:P], s[32 * l:32 * l + 32, 512 + 32 * l:640])
                    free(ins, key) if l == L4 - 1 else own.step(ins)

            for j in range(NPAIR):
                s5_out(j)

            for b in range(DB):
                full(act, ("sT", b))
                if b >= 2:
                    full(act, ("sP", b - 2))
                free(f(sTm[b % 2].rearrange("p a c -> p (a c)"), slot(("sT", b))[:, 0:256]), ("sT", b))
                full(act, ("sP", b))
                own.step(f(kcTs[:, b], slot(("sP", b))[:, 0:P]))
                free(f(vcs[:, b], slot(("sP", b))[:, P:2 * P]), ("sP", b))

            def softmax_rows(n, src_ready, stat, x, s, scale=SC):
                act.wait_ge(src_ready, n)
                f(x, x, ACT.Exp, bias=st[0:s, 33:34], scale=scale, accum_out=st[0:s, 34:35]).then_inc(stat, 1)

            softmax_rows(1, pw_raw, pw_exp, Pc[0:64], 64)
            full(act, "scT")
            free(f(PcT, slot("scT")[:, 0:64]), "scT")
            full(act, "sov")
            free(f(osT[:, 0], slot("sov")[:, 0:64]), "sov")
            full(act, "ix1")
            free(f(p15[0:SLOTS], slot("ix1")[0:SLOTS, 0:64]), "ix1")

            full(act, "st")
            own.step(f(st_rows[0:32], slot("st")[0:32, 0:P]))
            free(f(tinyf[0:32, 8:9], slot("st")[0:32, 0:1]), "st")
            act.wait_ge(own.sem, own.n)
            act.sem_inc(states_staged, 1)
            for q_ in range(4):
                key = ("sst", q_)
                full(act, key)
                free(f(sst_rows[0:DB, q_ * D:(q_ + 1) * D], slot(key)[0:DB]), key)
            for q_ in range(4):
                read_out(act, ("sst", q_))
            act.sem_inc(states_staged, 1)

            for h in range(NH):
                full(act, ("bt", h))
                free(f(BT[:, h], slot(("bt", h))), ("bt", h))

            act.wait_ge(states_out, 64)
            n_at = len(AT)
            for a in range(n_at + 1):
                if a < n_at:
                    nk, r = AT[a][4], a % 8
                    act.wait_ge(raw_ready, a + 1)
                    f(Pm[:, a % 2, 0:nk], Pm[:, a % 2, 0:nk], ACT.Exp, bias=st[:, 8 + r:9 + r], scale=SC,
                      accum_out=st[:, 16 + r:17 + r]).then_inc(exp_ready, 1)
                if a >= 1:
                    key, nk = ("TR", a - 1), AT[a - 1][4]
                    full(act, key)
                    if a >= 3:
                        full(act, ("PV", a - 3))
                    rows, w = (nk, P) if nk < P else (P, nk)
                    free(f(PT[0:rows, (a - 1) % 2, 0:w], slot(key)[0:rows, 0:w]), key)

            for b in range(DB):
                full(act, ("wT", b))
                free(f(kTw[:, b], slot(("wT", b))[:, 0:512]), ("wT", b))
            softmax_rows(2, pw_raw, pw_exp, Pw[0:64], 64)
            full(act, "wP")
            free(f(PTw.rearrange("p a c -> p (a c)"), slot("wP")[:, 0:256]), "wP")
            full(act, "wO")
            free(f(osT[:, 2], slot("wO")[:, 0:64]), "wO")
            for n in range(2 * DB):
                b, g = n // 2, n % 2
                key = ("gT", b, g)
                full(act, key)
                s = slot(key)[0:HD].rearrange("p (a x) -> p a x", a=2)[:, :, 0:4 * SK]
                free(f(kTs[64 * g:64 * g + 64, b].rearrange("p (a r) c -> p a (r c)", a=2), s), key)
            softmax_rows(3, pw_raw, pw_exp, Ps[0:64].rearrange("p a c -> p (a c)"), 64)
            full(act, "gP")
            free(f(PTs[0:SK].rearrange("p a c -> p (a c)"), slot("gP")[0:SK, 0:512]), "gP")
            full(act, "gO")
            free(f(osT[:, 1], slot("gO")[:, 0:64]), "gO")

            act.wait_ge(y_ready, 1)
            f(yF, yF, ACT.Gelu_apprx_tanh).then_inc(gelu_ready, 1)
            for m in range(4):
                for c in range(2):
                    key = ("glu", m, c)
                    full(act, key)
                    if c == 0:
                        ins = f(oF[:, m, 0:2 * CH].rearrange("p (a n) -> p a n", a=2), chunked(key), ACT.Sigmoid,
                                bias=cols[:, 64 + m:65 + m])
                    else:
                        ins = f(oF[:, m, 2 * CH:TC], chunked(key)[:, 0], ACT.Sigmoid, bias=cols[:, 64 + m:65 + m])
                    free(ins, key)
            act.wait_ge(oF_ready, 1)
            f(SQ, oF, ACT.Square).then_inc(sq_ready, 1)
            for c in range(2):
                key = ("ss", c)
                full(act, key)
                if c == 0:
                    ins = f(RS[:, 0:2 * CH].rearrange("p (a n) -> p a n", a=2), chunked(key), ACT.Sqrt,
                            scale=1.0 / 512, bias=eps_c[:, :])
                else:
                    ins = f(RS[:, 2 * CH:TC], chunked(key)[:, 0], ACT.Sqrt, scale=1.0 / 512, bias=eps_c[:, :])
                free(ins, key)
            act.wait_ge(oS_ready, 1)
            for i in range(NT + 1):
                n = token_tile(i)[1]
                src = oN[:, i] if i < NT else oS[0:DB, 0]
                own.then(f(scr[0:n], src, ACT.Square, accum_out=st[0:n, i:i + 1]))
                f(st[0:n, 16 + i:17 + i], st[0:n, i:i + 1], ACT.Sqrt, scale=1.0 / 512, bias=eps_c[0:n]).then_inc(on_stat, 1)

            for i in range(NT + 1):
                c0, n = token_tile(i)
                src = x_prompt[0, c0:c0 + n] if i < NT else x_sample[:, 0]
                act.dma_start(x1[0:n, i], src).then_inc(x1_in, 16)

            def residual(n):
                stage = {1: "wo", 2: "xo", 3: "wf"}[n]
                for m in range(8):
                    if m == 0 and n == 1:
                        act.wait_ge(m_ready, 2)
                    dense_out(stage, m, (hT if n == 3 else yT)[:, m])
                if n == 1:
                    act.wait_ge(m_ready, 2)
                if n > 1:
                    act.wait_ge(res_sum, (n - 1) * (NT + 1))
                act.dma_start(grow, bass.AP(norm_g.tensor, (2 * n - 1) * D, [[0, P], [1, D]])).then_inc(grow_in, 16)
                base = (n - 1) * (NT + 1)

                def first(i):
                    r = token_tile(i)[1]
                    full(act, (f"b{n}", i))
                    if n < 3 and i >= 2:
                        full(act, (f"f{n}", i - 2))
                    if n == 3 and i >= 2:
                        act.wait_ge(out_ready, i - 1)
                    own.then(f(tb[0:r, i % 2], slot((f"b{n}", i))[0:r], ACT.Square, accum_out=st[0:r, i:i + 1]))
                    f(st[0:r, 16 + i:17 + i], st[0:r, i:i + 1], ACT.Sqrt, scale=1.0 / D, bias=eps_c[0:r]).then_inc(res_stat, 1)

                first(0)
                for i in range(NT + 1):
                    if i < NT:
                        first(i + 1)
                    if n < 3:
                        r = token_tile(i)[1]
                        act.wait_ge(res_sum, base + i + 1)
                        own.then(f(tb[0:r, i % 2], x1[0:r, i], ACT.Square, accum_out=st[0:r, 32 + i:33 + i]))
                        f(st[0:r, 48 + i:49 + i], st[0:r, 32 + i:33 + i], ACT.Sqrt, scale=1.0 / D,
                          bias=eps_c[0:r]).then_inc(res_stat2, 1)

            residual(1)

            act.dma_start(mrow, mem_prompt[0].rearrange("(i p) d -> p i d", p=P)).then_inc(mem_in, 16)
            act.wait_ge(mem_in, 16)
            for i in range(2):
                own.then(f(junk2, mrow[:, i], ACT.Square, accum_out=st[:, i:i + 1]))
                f(st[:, 16 + i:17 + i], st[:, i:i + 1], ACT.Sqrt, scale=1.0 / D, bias=eps_c[:, :]).then_inc(mem_stat, 1)
            for c in range(8):
                full(act, ("mk", c))
                free(f(mkv[:, :, c * P:(c + 1) * P], slot(("mk", c))[:, 0:256].rearrange("p (i n) -> p i n", i=2)), ("mk", c))
            full(act, "mT")
            free(f(mkT.rearrange("p h n -> p (h n)"), slot("mT")), "mT")
            for m in range(4):
                dense_out("xq", m, q2T[:, m])
            for b in range(DB):
                full(act, ("xT", b))
                free(f(kTm[:, b].rearrange("p h n -> p (h n)"), slot(("xT", b))), ("xT", b))
            act.wait_ge(px_raw, 1)
            free(f(Pxs[0:32], slot("xS")[0:32, 0:NM], ACT.Exp, bias=st[0:32, 33:34], scale=XSC,
                   accum_out=st[0:32, 34:35]), "xS")
            full(act, "xP")
            free(f(PTxs.rearrange("p a c -> p (a c)"), slot("xP")[:, 0:64]), "xP")
            for i in range(NT + 1):
                if i < NT:
                    act.wait_ge(px_raw, i + 2)
                    if i >= 2:
                        full(act, ("XT", i - 2))
                    b0 = 8 * (i % 2)
                    for h in range(XH):
                        ins = f(Px[:, i % 2, h * NM:(h + 1) * NM], slot(("XS", i))[:, h * NM:(h + 1) * NM], ACT.Exp,
                                bias=st[:, b0 + h:b0 + h + 1], scale=XSC, accum_out=st[:, 16 + b0 + h:17 + b0 + h])
                        free(ins, ("XS", i)) if h == XH - 1 else own.step(ins)
                if i >= 1:
                    full(act, ("XT", i - 1))
                    if i >= 3:
                        full(act, ("XO", i - 3))
                    free(f(PTx[:, (i - 1) % 2], slot(("XT", i - 1))), ("XT", i - 1))
            residual(2)

            act.wait_ge(mkv_out, 16)
            for m in range(2 * NF):
                if m % 2 == 0:
                    k = m // 2
                    for c in range(2):
                        key = ("wi", m, c)
                        full(act, key)
                        if c == 0:
                            ins = f(g_tile(k)[:, 0:2 * CH].rearrange("p (a n) -> p a n", a=2), chunked(key), ACT.Silu)
                        else:
                            ins = f(g_tile(k)[:, 2 * CH:TC], chunked(key)[:, 0], ACT.Silu)
                        free(ins, key)
            residual(3)

        @block.vector
        def _(dve):
            own = Own(dve, dve_own)
            v = nc.vector

            def tt(out, a, b, op=ALU.mult):
                return v.tensor_tensor(out, a, b, op)

            def cmul(out_re, out_im, a, b, t, neg_im=False):
                own.step(tt(t[0], a[0], b[0]))
                own.step(tt(t[1], a[1], b[1]))
                own.step(tt(t[2], a[0], b[1]))
                own.step(tt(t[3], a[1], b[0]))
                own.settle()
                for o in out_re:
                    own.step(tt(o[0], o[1](t[0]), o[1](t[1]), ALU.subtract))
                for o in out_im:
                    if neg_im:
                        own.step(v.scalar_tensor_tensor(o[0], o[1](t[2]), -1.0, o[1](t[3]), ALU.mult, ALU.subtract))
                    else:
                        own.step(tt(o[0], o[1](t[2]), o[1](t[3]), ALU.add))
                own.settle()

            def whole(o):
                return [(o, lambda x: x)]

            def bcast(col, shape, axis=-1):
                return col.unsqueeze(axis).to_broadcast(shape)

            full(dve, "par")
            own.step(v.tensor_copy(cols[:, :], slot("par")[:, 0:120]))
            free(v.tensor_copy(d_rows[:, :], slot("par")[:, 128:128 + NPAIR]), "par")
            read_out(dve, "par")
            v.tensor_copy(jota[:, :], jota_i[:, :]).then_inc(s5_arg, 1)
            dve.wait_ge(s5_fun, 1)
            a_re, a_im, dt = cols[:, 72:88], cols[:, 88:104], prm[:, 0]
            own.step(tt(prm[:, 1], a_re, dt))
            own.then(tt(prm[:, 8], a_im, dt))
            TWO_PI = [6.28125, 0.0019350051879882812, 3.0199159819567e-07]
            for shift, dst in ((0.0, 4), (0.25, 6)):
                own.then(v.tensor_scalar(prm[:, 9], prm[:, 8], 1.0 / (2 * pi), shift, ALU.mult, ALU.add))
                own.then(v.tensor_scalar(prm[:, 9], prm[:, 9], 12582912.0, None, ALU.add))
                own.then(v.tensor_scalar(prm[:, 9], prm[:, 9], -12582912.0, None, ALU.add))
                own.then(v.scalar_tensor_tensor(prm[:, dst], prm[:, 9], -TWO_PI[0], prm[:, 8], ALU.mult, ALU.add))
                own.then(v.scalar_tensor_tensor(prm[:, dst], prm[:, 9], -TWO_PI[1], prm[:, dst], ALU.mult, ALU.add))
                own.then(v.scalar_tensor_tensor(prm[:, dst], prm[:, 9], -TWO_PI[2], prm[:, dst], ALU.mult, ALU.add))
                if shift:
                    own.then(v.tensor_scalar(prm[:, dst], prm[:, dst], pi / 2, None, ALU.add))
                own.then(v.tensor_scalar(prm[:, dst], prm[:, dst], 3.1415925, -3.1415925, ALU.min, ALU.max))
            dve.sem_inc(s5_arg, 1)
            dve.wait_ge(s5_fun, 3)
            ab = apow[:, 1]
            own.step(tt(ab[:, 0], prm[:, 2], prm[:, 7]))
            own.step(tt(ab[:, 1], prm[:, 2], prm[:, 5]))
            own.step(v.memset(apow[:, 0, 0], 1.0))
            own.step(v.memset(apow[:, 0, 1], 0.0))
            own.step(tt(prm[:, 9], a_re, a_re))
            own.step(tt(prm[:, 10], a_im, a_im))
            own.settle()
            own.step(tt(prm[:, 9], prm[:, 9], prm[:, 10], ALU.add))
            own.step(v.tensor_scalar(prm[:, 11], ab[:, 0], -1.0, None, ALU.add))
            own.settle()
            own.step(v.reciprocal(prm[:, 9], prm[:, 9]))
            own.step(tt(prm[:, 12], prm[:, 11], a_re))
            own.step(tt(prm[:, 13], ab[:, 1], a_im))
            own.step(tt(prm[:, 14], ab[:, 1], a_re))
            own.step(tt(prm[:, 15], prm[:, 11], a_im))
            own.settle()
            own.step(tt(prm[:, 12], prm[:, 12], prm[:, 13], ALU.add))
            own.step(tt(prm[:, 14], prm[:, 14], prm[:, 15], ALU.subtract))
            own.settle()
            own.step(tt(co[:, 0], prm[:, 12], prm[:, 9]))
            own.step(tt(co[:, 1], prm[:, 14], prm[:, 9]))
            own.settle()
            sm = [prm[:, 12 + n] for n in range(4)]
            for k in range(2, 5):
                cmul(whole(apow[:, k, 0]), whole(apow[:, k, 1]), (apow[:, k - 1, 0], apow[:, k - 1, 1]),
                     (ab[:, 0], ab[:, 1]), sm)

            dve.wait_ge(pt_in, 16 * (DB + 1))
            own.step(v.tensor_copy(tinyf[:, 0:1], tiny[:, 0:1]))
            own.step(v.tensor_single_scalar(tiny[:, 1:2], tiny[:, 0:1], 3, ALU.bitwise_and))
            own.step(v.tensor_single_scalar(tiny[:, 2:3], tiny[:, 0:1], 7, ALU.bitwise_and))
            own.settle()
            own.step(v.tensor_copy(tinyf[:, 1:2], tiny[:, 1:2]))
            own.step(v.tensor_copy(tinyf[:, 2:3], tiny[:, 2:3]))
            own.settle()
            own.step(v.tensor_scalar(tinyf[:, 3:4], tinyf[:, 1:2], 4.0, None, ALU.mult))
            own.settle()
            for k in range(4):
                own.step(v.tensor_scalar(tinyf[:, 4 + k:5 + k], tinyf[:, 3:4], float(k), None, ALU.add))
            own.settle()
            for k in range(4):
                ins = v.tensor_scalar(pline[:, k], ptc[:, :], 16.0, tinyf[:, 4 + k:5 + k], ALU.mult, ALU.add)
                own.step(ins) if k < 3 else ins.then_inc(pline_ready, 1)

            for i in range(NT + 1):
                n = token_tile(i)[1]
                c0 = token_tile(i)[0]
                dve.wait_ge(rt_ready, i + 1)
                own.then(v.reciprocal(st[0:n, 32 + i:33 + i], st[0:n, 16 + i:17 + i]))
                v.tensor_scalar(xin[0:n, i % 2], xin[0:n, i % 2], st[0:n, 32 + i:33 + i], None, ALU.mult).then_inc(xn_ready, 1)
                full(dve, ("n1", i))
                s = slot(("n1", i)).rearrange("p (k t) -> p k t", k=KD)[:, :, 0:n]
                free(tt(hT[:, :, c0:c0 + n], s, bcast(cols[:, 0:8], [P, KD, n])), ("n1", i))

            dve.wait_ge(pos_in, 16 * 12)
            for i in range(NT):
                dve.wait_ge(kv_ready, i + 1)
                own.step(v.tensor_copy(vkeep[:, i].rearrange("p (a c) -> p a c", a=2),
                                       kvst[:, i % 2, 256:768].rearrange("p (a b c) -> p a b c", a=2, b=2)[:, :, 1]))
                if i >= 2:
                    full(dve, ("kT", i - 2))
                tt(cprod[:, i % 2], kvst[:, i % 2, 0:256], posP).then_inc(prod_ready, 1)

            dve.wait_ge(kv_stored[0], 16 * (2 * 4 + 2))
            dve.wait_ge(kv_stored[1], 16 * (2 * 4 + 2))
            for m in range(4):
                for c in range(2):
                    read_out(dve, ("in", 4 + m, c))
                for q_ in range(4):
                    src = uTm[32 * q_:32 * q_ + 32, m % 2]
                    for l in range(L4):
                        own.step(v.tensor_copy(U2[32 * l:32 * l + 32, 4 * m + q_], src[:, l:T:L4]))
                    own.step(v.tensor_copy(us3[96:P, 4 * m + q_], src[:, T:TC]))
                own.settle()
                v.tensor_copy(uS[:, m], uTm[:, m % 2, T:TC]).then_inc(uT_ready, 1)
            for h in range(NH):
                g = h // GQ
                lo = 64 * (h % 2)
                ins = v.tensor_copy(qz[64 * g:64 * g + 64].rearrange("p b c -> p (b c)")[:, h::72],
                                    qT[lo:lo + 64, h // 2, T:TC])
                own.step(ins) if h < NH - 1 else ins.then_inc(qz_ready, 1)
            dve.wait_ge(uT_ready, 4)
            dve.sem_inc(u_moved, 1)

            dve.wait_ge(b_in, 32)
            dve.wait_ge(rows_saved, 64)
            own.step(v.memset(WT, 0.0))
            own.step(v.memset(CP, 0.0))
            own.step(v.memset(Tm[0], 0.0))
            own.step(v.memset(Tm[1], 0.0))
            sh = [P, NPAIR, 16]
            qq = [q[:, n] for n in range(4)]
            cmul(whole(bb[:, 0]), whole(bb[:, 1]), (bcast(co[:, 0], sh), bcast(co[:, 1], sh)),
                 (braw[:, 0], braw[:, 1]), qq)

            def halves(dst):
                return [(dst(g)[64 * g:64 * g + 64], lambda x, g=g: x[64 * g:64 * g + 64]) for g in range(2)]

            for l in range(L4):
                pw = apow[:, L4 - 1 - l]
                cmul(halves(lambda g: WT[:, 0, :, 32 * l + 16 * g:32 * l + 16 * g + 16]),
                     halves(lambda g: WT[:, 1, :, 32 * l + 16 * g:32 * l + 16 * g + 16]),
                     (bcast(pw[:, 0], sh), bcast(pw[:, 1], sh)), (bb[:, 0], bb[:, 1]), qq)
            read_out(dve, "C")
            for k in range(5):
                pw = apow[:, k]
                cmul(halves(lambda g: CP[:, 0, :, k, 16 * g:16 * g + 16]),
                     halves(lambda g: CP[:, 1, :, k, 16 * g:16 * g + 16]),
                     (bcast(pw[:, 0], sh), bcast(pw[:, 1], sh)), (cc[:, 0], cc[:, 1]), qq, neg_im=True)
            read_out(dve, "h0")
            dve.sem_inc(s5_built, 1)
            own.then(v.memset(H[:, 0], 0.0))

            for j in range(NPAIR):
                key = ("SB", j)
                full(dve, key)
                s = slot(key)
                own.step(v.tensor_copy(H[:, 1:NC + 1, :, j].rearrange("p c a -> p a c"),
                                       s[:, 0:512].rearrange("p (a c) -> p a c", a=2)))
                own.step(v.tensor_copy(hs[:, :, j], s[:, 512:528].rearrange("p (a b) -> p a b", a=2)))
                free(v.scalar_tensor_tensor(U2[:, j], U2[:, j], d_rows[:, j:j + 1], s[:, 528:528 + NC],
                                            ALU.mult, ALU.add), key)
            read_out(dve, ("SB", NPAIR - 1))
            own.settle()

            sm2 = [r1[:, n, 0] for n in range(4)]
            apw_ = lambda n: (apw[:, n, 0], apw[:, n, 1])
            own.step(v.tensor_copy(apw[:, 0], apow[:, 4]))
            own.settle()
            for n in range(1, 15):
                cmul(whole(apw[:, n, 0]), whole(apw[:, n, 1]), apw_(n - 1), (apow[:, 4, 0], apow[:, 4, 1]), sm2)
            cmul(whole(apow[:, 5, 0]), whole(apow[:, 5, 1]), apw_(14), (apow[:, 4, 0], apow[:, 4, 1]), sm2)
            Hm = H[:, 1:NC + 1].rearrange("p (m n) a j -> p m n a j", n=16)

            def advance(dst, src, power, m):
                shape = [P, m, NPAIR]
                pr = power[0].unsqueeze(1).to_broadcast(shape)
                pi_ = power[1].unsqueeze(1).to_broadcast(shape)
                own.step(tt(r1[:, 0:m, 0], src[:, :, 0], pr))
                own.step(tt(r1[:, 0:m, 1], src[:, :, 1], pr))
                own.step(tt(r2[:, 0:m, 0], src[:, :, 1], pi_))
                own.step(tt(r2[:, 0:m, 1], src[:, :, 0], pi_))
                own.settle()
                own.step(tt(dst, dst, r1[:, 0:m], ALU.add))
                own.settle()
                own.step(tt(dst[:, :, 0], dst[:, :, 0], r2[:, 0:m, 0], ALU.subtract))
                own.step(tt(dst[:, :, 1], dst[:, :, 1], r2[:, 0:m, 1], ALU.add))
                own.settle()

            for n in range(1, 16):
                advance(Hm[:, :, n], Hm[:, :, n - 1], (apow[:, 4, 0], apow[:, 4, 1]), 16)
            for m in range(1, 16):
                advance(Hm[:, m:m + 1, 15], Hm[:, m - 1:m, 15], (apow[:, 5, 0], apow[:, 5, 1]), 1)
            for n in range(15):
                advance(Hm[:, 1:16, n], Hm[:, 0:15, 15], apw_(n), 15)
            sb4 = [P, NPAIR, DB]
            t = [r1[:, 4 * n:4 * n + 4].rearrange("p m a j -> p (m a j)").rearrange("p (j b) -> p j b", b=DB)
                 for n in range(4)]
            abr, abi = bcast(ab[:, 0], sb4), bcast(ab[:, 1], sb4)
            own.step(tt(t[0], h0T[:, 0], abr))
            own.step(tt(t[1], h0T[:, 1], abi))
            own.step(tt(t[2], h0T[:, 1], abr))
            own.step(tt(t[3], h0T[:, 0], abi))
            own.settle()
            own.step(tt(t[0], t[0], t[1], ALU.subtract))
            own.step(tt(t[2], t[2], t[3], ALU.add))
            own.settle()
            own.step(tt(hs[:, 0], hs[:, 0], t[0], ALU.add))
            own.step(tt(hs[:, 1], hs[:, 1], t[2], ALU.add))
            own.settle()
            dve.sem_inc(s5_states, 1)
            dve.sem_inc(hs_ready, 1)

            for n in range(4 * DB):
                k, b = n // DB, n % DB
                r = gring[:, n % 3].rearrange("p (r c g d) -> p (r c) g d", r=ROWS, c=2, g=2)
                dve.wait_ge(gat[n % 3], 16 * (n // 3 + 1))
                if b == 0:
                    dve.wait_ge(posB_in, 32 * (k + 1))
                own.then(tt(r, r, posB.rearrange("p r (c d) -> p (r c) d", c=2).unsqueeze(2)
                            .to_broadcast([P, 2 * ROWS, NKV, HD])))
                flat = gring[:, n % 3]
                for half in (1024, 512):
                    own.then(tt(flat[:, 0:half], flat[:, 0:half], flat[:, half:2 * half], ALU.add))
                if k == 0:
                    tt(summ[:, b], flat[:, 0:256], flat[:, 256:512], ALU.add).then_inc(gat_used, 1)
                else:
                    own.step(tt(summ[:, b], summ[:, b], flat[:, 0:256], ALU.add))
                    own.settle()
                    tt(summ[:, b], summ[:, b], flat[:, 256:512], ALU.add).then_inc(gat_used, 1)
                if k == 0:
                    dve.wait_ge(gat_used, n + 1)
                if k == 3:
                    dve.wait_ge(gat_used, n + 1)
                    dve.sem_inc(summ_ready, 1)

            full(dve, "sc")
            dve.wait_ge(V64_in, 16)
            own.step(v.tensor_copy(cbias[0:64, 0:112], V64[:, 0:1].to_broadcast([64, 112])))
            own.step(v.tensor_copy(cbias[0:64, 112:P], V64[:, 31::CB][:, 0:16]))
            own.settle()

            def softmax_in(out, x, bias, release=None):
                ins = v.tensor_tensor_reduce(out=out, in0=x, in1=bias, scale=1.0, scalar=FLOOR, op0=ALU.add,
                                             op1=ALU.max, accum_out=st[0:64, 32:33])
                if release:
                    free(ins, release)
                    read_out(dve, release)
                v.tensor_scalar(st[0:64, 33:34], st[0:64, 32:33], -SC, None, ALU.mult).then_inc(pw_raw, 1)

            def softmax_out(n, x):
                dve.wait_ge(pw_exp, n)
                own.then(v.tensor_scalar(st[0:64, 35:36], st[0:64, 34:35], TINY, None, ALU.max))
                own.then(v.reciprocal(st[0:64, 36:37], st[0:64, 35:36]))
                return v.tensor_scalar(x, x, st[0:64, 36:37], None, ALU.mult)

            softmax_in(Pc[0:64], slot("sc")[0:64, 0:P], cbias[0:64], "sc")
            softmax_out(1, Pc[0:64]).then_inc(pc_ready, 1)
            full(dve, "sps")
            free(v.tensor_reduce(score[0:64], slot("sps")[0:64, 0:P].rearrange("p (j a) -> p j a", a=2), X, ALU.add), "sps")
            read_out(dve, "sps")
            own.step(v.memset(score[0:64, 0:1], -1.0))
            own.then(v.memset(score[0:64, NSB - 1:NSB], -1.0))
            own.then(v.max(top[0:64, 0:8], score[0:64]))
            own.step(v.max_index(topi[0:64, 0:8], top[0:64, 0:8], score[0:64]))
            own.step(v.match_replace(out=score2[0:64], in_to_replace=top[0:64, 0:8], in_values=score[0:64], imm_value=-1.0))
            own.settle()
            own.then(v.max(top[0:64, 8:16], score2[0:64]))
            own.then(v.max_index(topi[0:64, 8:16], top[0:64, 8:16], score2[0:64]))
            own.then(v.tensor_copy(pick[0:64], topi[0:64]))
            own.step(v.memset(pick[0:64, PICK:PICK + 1], 0.0))
            own.step(v.memset(pick[0:64, PICK + 1:PICK + 2], float(NSB - 1)))
            own.step(v.tensor_scalar(jphys[0:64].rearrange("p (j a) -> p j a", a=2)[:, :, 0], ptrow[:, :], 2.0, None, ALU.mult))
            own.step(v.tensor_scalar(jphys[0:64].rearrange("p (j a) -> p j a", a=2)[:, :, 1], ptrow[:, :], 2.0, 1.0, ALU.mult, ALU.add))
            own.settle()
            s3 = [64, SLOTS, 64]
            own.step(tt(onehot[0:64], bcast(pick[0:64, 0:SLOTS], s3), jota[:, :].unsqueeze(1).to_broadcast(s3), ALU.is_equal))
            own.step(v.tensor_scalar(is62[0:64, 0:PICK], pick[0:64, 0:PICK], float(NSB - 2), None, ALU.is_equal))
            own.settle()
            own.then(tt(onehot[0:64], onehot[0:64], jphys[0:64].unsqueeze(1).to_broadcast(s3)))
            v.tensor_reduce(phys[0:64, 0:SLOTS], onehot[0:64], X, ALU.add).then_inc(phys_ready, 1)
            full(dve, "ix2")
            free(v.tensor_scalar(line[:, :], slot("ix2")[0:SL, 0:64], 8.0, tinyf[0:SL, 2:3], ALU.mult, ALU.add), "ix2")
            read_out(dve, "ix2")
            dve.sem_inc(line_ready, 1)

            for j in range(NPAIR):
                key = ("V", j)
                full(dve, key)
                q_, m = j % 4, j // 4
                for l in range(L4):
                    ins = tt(yF[32 * q_:32 * q_ + 32, m, l:T:L4], slot(key)[32 * l:32 * l + 32, 0:NC],
                             U2[32 * l:32 * l + 32, j], ALU.add)
                    free(ins, key) if l == L4 - 1 else own.step(ins)
            full(dve, "ys")
            for m in range(4):
                ins = v.scalar_tensor_tensor(yF[:, m, T:TC], uS[:, m], cols[:, 68 + m:69 + m],
                                             slot("ys")[:, m * DB:(m + 1) * DB], ALU.mult, ALU.add)
                free(ins, "ys") if m == 3 else own.step(ins)
            read_out(dve, "ys")
            dve.sem_inc(y_ready, 1)

            far_bias = V64[:, 0:1]
            own.step(v.tensor_copy(sbias[0:64], far_bias.to_broadcast([64, ROWS * SK]).rearrange("p (r c) -> p r c", r=ROWS)))
            own.settle()
            last_block = V64[:, WIN - 64:WIN].rearrange("p (c r) -> p r c", r=ROWS)
            prev_block = V64[:, WIN - 128:WIN - 64]
            own.step(v.tensor_copy(sbias[0:64, :, (SLOTS - 1) * LINES:SL], last_block))
            own.step(v.tensor_scalar(score[0:64], prev_block, far_bias, None, ALU.subtract))
            own.step(v.tensor_copy(sbias[0:64, 0, SL:SK], V64[:, WIN:WIN + 1]))
            own.step(v.memset(sbias[0:64, 1:ROWS, SL:SK], NEG))
            own.settle()
            s4 = [64, PICK, LINES]
            for r in range(ROWS):
                diff = score[0:64].rearrange("p (c r) -> p r c", r=ROWS)[:, r].unsqueeze(1).to_broadcast(s4)
                own.then(tt(sdiff[0:64], bcast(is62[0:64, 0:PICK], s4), diff))
                own.then(tt(sbias[0:64, r, 0:PICK * LINES].rearrange("p (s c) -> p s c", c=LINES),
                            sbias[0:64, r, 0:PICK * LINES].rearrange("p (s c) -> p s c", c=LINES), sdiff[0:64], ALU.add))

            dve.wait_ge(far_ready, NH)
            n_at = len(AT)
            for a in range(n_at + 2):
                if a < n_at:
                    i, h, br, k0, nk = AT[a]
                    r = a % 8
                    key = ("SC", a)
                    s = slot(key)
                    full(dve, key)
                    if a >= 2:
                        full(dve, ("TR", a - 2))
                    x0 = T - P - i * P
                    mx = st[:, r:r + 1]
                    start, done = FLOOR, 0
                    if br == 0:
                        bias = BT[:, h, x0 + CB - 1::CB][:, 0:nk]
                    else:
                        bias = BT[:, h, x0 + k0:x0 + k0 + nk]
                        if br == 2 and i >= 4:
                            own.then(v.tensor_tensor_reduce(out=Pm[:, a % 2, 0:P], in0=s[:, 0:P], in1=far[:, h],
                                                            scale=1.0, scalar=FLOOR, op0=ALU.add, op1=ALU.max,
                                                            accum_out=mx))
                            start, done, bias = mx, P, bias[:, P:]
                    free(v.tensor_tensor_reduce(out=Pm[:, a % 2, done:nk], in0=s[:, done:nk], in1=bias, scale=1.0,
                                                scalar=start, op0=ALU.add, op1=ALU.max,
                                                accum_out=mx if not done else st[:, 40 + r:41 + r]), key)
                    read_out(dve, key)
                    v.tensor_scalar(st[:, 8 + r:9 + r], mx if not done else st[:, 40 + r:41 + r], -SC, None,
                                    ALU.mult).then_inc(raw_ready, 1)
                if a >= 2:
                    i, h, br, k0, nk = AT[a - 2]
                    key = ("PV", a - 2)
                    r = (a - 2) % 8
                    own.then(v.tensor_scalar(st[:, 24 + r:25 + r], st[:, 16 + r:17 + r], TINY, None, ALU.max))
                    own.then(v.reciprocal(st[:, 48 + r:49 + r], st[:, 24 + r:25 + r]))
                    own.then(tt(st[:, 56 + r:57 + r], st[:, 48 + r:49 + r], gates[:, i, 3 * h + br:3 * h + br + 1]))
                    full(dve, key)
                    o = oN[:, i, h * HD:(h + 1) * HD]
                    p_ = slot(key)[:, 0:HD]
                    w = st[:, 56 + r:57 + r]
                    if br == 0:
                        free(v.tensor_scalar(o, p_, w, None, ALU.mult), key)
                    else:
                        free(v.scalar_tensor_tensor(o, p_, w, o, ALU.mult, ALU.add), key)
                    read_out(dve, key)

            full(dve, "wS")
            softmax_in(Pw[0:64].rearrange("p (j c) -> p j c", j=4), slot("wS")[0:64, 0:512].rearrange("p (j c) -> p j c", j=4),
                       V64[:, 1:WIN + 1].rearrange("p (c j) -> p j c", j=4), "wS")
            softmax_out(2, Pw[0:64]).then_inc(pw_ready, 1)
            full(dve, "wO")
            dve.wait_ge(win_stored, 16 * DB)
            for n in range(2 * DB):
                g = n % 2
                dve.wait_ge(gat[n % 3], 16 * GAT0[n % 3] + 32 * (n // 3 + 1))
                v.tensor_copy(Vs[0:SK, n], gring[0:SK, n % 3].rearrange("p (r c) -> p r c", r=ROWS)
                              [:, :, P + g * HD:P + (g + 1) * HD]).then_inc(vs_ready, 1)
            full(dve, "gS")
            two = lambda x: x.rearrange("p (a c) -> p a c", a=2)
            flatS = Ps[0:64].rearrange("p a c -> p (a c)")
            softmax_in(two(flatS), two(slot("gS")[0:64])[:, :, 0:4 * SK],
                       two(sbias[0:64].rearrange("p a c -> p (a c)")), "gS")
            softmax_out(3, flatS).then_inc(pw_ready, 1)
            gt = gates[0:DB, NT].rearrange("b (h r) -> b h r", r=3)
            for br in range(3):
                key = "oT0" if br < 2 else "oT1"
                full(dve, key)
                ins = tt(oS[0:DB, br].rearrange("b (g h d) -> b g h d", g=NKV, h=GQ),
                         slot(key)[0:DB].rearrange("b (g r h d) -> b g r h d", g=NKV, r=2, h=GQ)[:, :, br % 2],
                         bcast(gt[:, :, br].rearrange("b (g h) -> b g h", g=NKV), [DB, NKV, GQ, HD]))
                own.step(ins) if br == 0 else free(ins, key)
            own.settle()
            read_out(dve, "oT0")
            read_out(dve, "oT1")
            own.then(tt(oS[0:DB, 0], oS[0:DB, 0], oS[0:DB, 1], ALU.add))
            tt(oS[0:DB, 0], oS[0:DB, 0], oS[0:DB, 2], ALU.add).then_inc(oS_ready, 1)

            for m in range(4):
                for c in range(2):
                    read_out(dve, ("glu", m, c))
            own.then(tt(oF, oF, yF))
            dve.sem_inc(oF_ready, 1)
            read_out(dve, ("ss", 0))
            read_out(dve, ("ss", 1))
            own.then(v.reciprocal(RS, RS))
            for k in range(4):
                ins = v.scalar_tensor_tensor(mT[:, 4 + k], oF[:, k], cols[:, 52 + k:53 + k], RS, ALU.mult, ALU.mult)
                own.step(ins)
            own.settle()
            dve.sem_inc(m_ready, 1)
            for i in range(NT + 1):
                c0, n = token_tile(i)
                src = oN[:, i] if i < NT else oS[0:DB, 0]
                dve.wait_ge(on_stat, i + 1)
                own.then(v.reciprocal(st[0:n, 32 + i:33 + i], st[0:n, 16 + i:17 + i]))
                v.tensor_scalar(src, src, st[0:n, 32 + i:33 + i], None, ALU.mult).then_inc(on_ready, 1)
                key = ("n0", i)
                full(dve, key)
                free(tt(mT[:, 0:4, c0:c0 + n], slot(key)[:, 0:512].rearrange("p (k t) -> p k t", k=4)[:, :, 0:n],
                        bcast(cols[:, 48:52], [P, 4, n])), key)
            for i in range(NT + 1):
                read_out(dve, ("n0", i))
            dve.sem_inc(m_ready, 1)

            def residual(n):
                base = (n - 1) * (NT + 1)
                dve.wait_ge(grow_in, 16 * n)
                if n == 1:
                    dve.wait_ge(x1_in, 16 * (NT + 1))

                def add(i):
                    r = token_tile(i)[1]
                    key = (f"b{n}", i)
                    dve.wait_ge(res_stat, base + i + 1)
                    own.then(v.reciprocal(st[0:r, 9 + i % 2:10 + i % 2], st[0:r, 16 + i:17 + i]))
                    free(v.scalar_tensor_tensor(tb[0:r, i % 2], slot(key)[0:r], st[0:r, 9 + i % 2:10 + i % 2], grow[0:r],
                                                ALU.mult, ALU.mult), key)
                    read_out(dve, key)
                    tt(x1[0:r, i], x1[0:r, i], tb[0:r, i % 2], ALU.add).then_inc(res_sum if n < 3 else out_ready, 1)

                def scale(i):
                    r = token_tile(i)[1]
                    dve.wait_ge(res_stat2, base + i + 1)
                    own.then(v.reciprocal(st[0:r, 11 + i % 2:12 + i % 2], st[0:r, 48 + i:49 + i]))
                    v.tensor_scalar(tb[0:r, i % 2], x1[0:r, i], st[0:r, 11 + i % 2:12 + i % 2], None, ALU.mult)\
                        .then_inc(res_norm, 1)

                def forward(i):
                    c0, r = token_tile(i)
                    key = (f"f{n}", i)
                    full(dve, key)
                    free(tt(hT[:, :, c0:c0 + r], slot(key).rearrange("p (k t) -> p k t", k=KD)[:, :, 0:r],
                            bcast(cols[:, 16 * n:16 * n + 8], [P, KD, r])), key)

                add(0)
                for i in range(NT + 1):
                    if i < NT:
                        add(i + 1)
                    if n < 3:
                        scale(i)
                        forward(i)

            residual(1)

            for i in range(2):
                dve.wait_ge(mem_stat, i + 1)
                own.then(v.reciprocal(st[:, 32 + i:33 + i], st[:, 16 + i:17 + i]))
                v.tensor_scalar(mrow[:, i], mrow[:, i], st[:, 32 + i:33 + i], None, ALU.mult).then_inc(mem_norm, 1)
            for i in range(2):
                full(dve, ("mn", i))
                free(tt(memT[:, :, i * P:(i + 1) * P], slot(("mn", i)).rearrange("p (k t) -> p k t", k=KD),
                        bcast(cols[:, 56:64], [P, KD, P])), ("mn", i))
            for m in range(4):
                for c in range(2):
                    read_out(dve, ("xq", m, c))
            dve.wait_ge(qxz_zero, 1)
            for h in range(XH):
                own.step(v.tensor_copy(qxz[:, h].rearrange("p b c -> p (b c)")[:, h::36], q2T[:, h, T:TC]))
            own.settle()
            dve.sem_inc(qxz_ready, 1)
            full(dve, "xS")
            own.then(v.tensor_reduce(st[0:32, 32:33], slot("xS")[0:32, 0:NM], X, ALU.max))
            v.tensor_scalar(st[0:32, 33:34], st[0:32, 32:33], -XSC, None, ALU.mult).then_inc(px_raw, 1)
            read_out(dve, "xS")
            own.then(v.reciprocal(st[0:32, 36:37], st[0:32, 34:35]))
            v.tensor_scalar(Pxs[0:32], Pxs[0:32], st[0:32, 36:37], None, ALU.mult).then_inc(px_ready, 1)
            full(dve, "xO")
            free(v.tensor_copy(q2T[:, :, T:TC], slot("xO")[:, 0:32].rearrange("p (h b) -> p h b", h=XH)), "xO")
            for i in range(NT + 1):
                if i < NT:
                    key = ("XS", i)
                    full(dve, key)
                    b0 = 8 * (i % 2)
                    own.then(v.tensor_reduce(st[:, 32 + b0:36 + b0], slot(key).rearrange("p (h n) -> p h n", h=XH), X, ALU.max))
                    v.tensor_scalar(st[:, b0:b0 + 4], st[:, 32 + b0:36 + b0], -XSC, None, ALU.mult).then_inc(px_raw, 1)
                    read_out(dve, key)
                    own.then(v.reciprocal(st[:, 48 + b0:52 + b0], st[:, 16 + b0:20 + b0]))
                    px = Px[:, i % 2].rearrange("p (h n) -> p h n", h=XH)
                    tt(px, px, bcast(st[:, 48 + b0:52 + b0], [P, XH, NM])).then_inc(px_ready, 1)
                if i >= 1:
                    key = ("XO", i - 1)
                    full(dve, key)
                    free(v.tensor_copy(q2T[:, :, (i - 1) * P:i * P], slot(key)[:, 0:512].rearrange("p (h n) -> p h n", h=XH)), key)
            residual(2)

            for k in range(NF):
                for c in range(2):
                    read_out(dve, ("wi", 2 * k, c))
                    key = ("wi", 2 * k + 1, c)
                    full(dve, key)
                    if c == 0:
                        w = g_tile(k)[:, 0:2 * CH].rearrange("p (a n) -> p a n", a=2)
                        s = chunked(key)
                    else:
                        w, s = g_tile(k)[:, 2 * CH:TC], chunked(key)[:, 0]
                    free(tt(w, w, s), key)
            for c in range(2):
                read_out(dve, ("wi", 2 * NF - 1, c))
                read_out(dve, ("wi", 2 * NF - 3, c))
            dve.sem_inc(g_ready, NF)
            residual(3)


_INPUTS = ["x_prompt", "x_sample", "cache_kv_cmp", "cache_kv_sel", "cache_kv_win", "state_ssm_re", "state_ssm_im",
           "cache_mem_kv", "page_table", "mem_prompt", "w_in", "w_out", "norm_g", "grp_norm_g", "cmp_pos", "cmp_proj",
           "rel_bias", "ssm_a_re", "ssm_a_im", "ssm_b_re", "ssm_b_im", "ssm_c_re", "ssm_c_im", "ssm_d", "ssm_log_dt",
           "glu_w", "glu_b", "mem_norm_g", "xq", "xkv", "xo", "ffn_wi", "ffn_wo"]
_OUTPUTS = [(1, T, D), (DB, 1, D), (1, 1, T, 2, NKV, HD), (1, 1, T, 2, NKV, HD), (1, 1, WIN, 2, NKV, HD),
            (1, 1, 32, 64), (1, 1, 32, 64), (1, 1, NM, 2, XH, P), (1, DB, 1, 2, NKV, HD), (1, DB, 1, 2, NKV, HD),
            (1, DB, WIN, 2, NKV, HD), (1, DB, 32, 64), (1, DB, 32, 64)]


def kernel(**inputs):
    import concourse.bacc as bacc
    from concourse.bass_utils import run_bass_kernel_spmd

    nc = bacc.Bacc("TRN2", target_bir_lowering=False, num_devices=1)
    arrays, args = {}, []
    for name in _INPUTS:
        a = np.ascontiguousarray(inputs[name])
        arrays[f"in_{name}"] = a
        args.append(nc.dram_tensor(f"in_{name}", a.shape, mybir.dt.from_np(a.dtype), kind="ExternalInput").ap())
    for i, shape in enumerate(_OUTPUTS):
        args.append(nc.dram_tensor(f"out_{i}", shape, F32, kind="ExternalOutput").ap())
    hymba_step(nc, *args)
    r = run_bass_kernel_spmd(nc, [arrays], core_ids=[0])
    return tuple(r.results[0][f"out_{i}"] for i in range(len(_OUTPUTS)))
```

```python
from contextlib import ExitStack
from math import log, pi

import numpy as np

import concourse.bass as bass
from concourse import mybir

F32 = mybir.dt.float32
F32R = mybir.dt.float32r
I32 = mybir.dt.int32
U32 = mybir.dt.uint32
ALU = mybir.AluOpType
ACT = mybir.ActivationFunctionType
X = mybir.AxisListType.X

P = 128
D = 1024
KD = D // P
T = 1024
NT = T // P
DB = 8
TC = T + DB
CH = TC // 3
HD = 64
NH = 8
NKV = 2
GQ = NH // NKV
KVC = 3 * 2 * NKV * HD
NG = 3 * NH
OFF_U = NH * HD + KVC + NG
CB = 32
WIN = 512
PAST = 4096
PAGE = 128
NPAGE = PAST // PAGE
NCB = PAST // CB
NSB = PAST // 64
PICK = 13
SLOTS = PICK + 2
PARAM_DMAS = 9
ROWS = 8
LINES = 64 // ROWS
SL = SLOTS * LINES
SK = SL + 1
GAT0 = [11, 11, 10]
NPAIR = 16
L4 = 4
NC = T // L4
NF = 22
DFF = NF * P
FG = 3
NGRP = -(-NF // FG)
FFN_ITEMS = 2 * NF + 4 * NGRP
XH = 4
NM = 256
EPS = 1e-6
TINY = 1e-30
SC = HD ** -0.5
NEG = -1e30 / SC
FLOOR = -1e20 / SC
XSC = P ** -0.5
QS = 4
AHEAD = 2
NPM = AHEAD + 1
VL = T + P - 1


def bucket_ranges():
    n = np.arange(T)
    big = 16 + (np.log(np.maximum(n, 16).astype(np.float32) / 16) / log(8) * 16).astype(np.int32)
    b = np.where(n < 16, n, np.minimum(big, 31))
    return [(int(v), int(np.argmax(b == v)), int(T - 1 - np.argmax(b[::-1] == v))) for v in np.unique(b)]


def token_tile(i):
    return (i * P, P) if i < NT else (T, DB)


def attention_units():
    out = []
    for i in range(NT):
        for h in range(NH):
            out.append((i, h, 0, 0, 4 * (i + 1)))
            out.append((i, h, 1, 0, P * (i + 1)))
            k0 = max(0, i - 4) * P
            out.append((i, h, 2, k0, P * (i + 1) - k0))
    return out


BETWEEN = {4 * 4 * DB + 2 + 4 * b: [("sT", b), ("sP", b)] for b in range(DB)}
BETWEEN.update({164: ["sc"], 168: ["sps", "scT"], 171: ["sov", "ix1"], 174: ["ix2"]})


def ffn_items():
    items = []
    for grp in range(NGRP):
        for k in group_tiles(grp):
            items += [("g", k), ("u", k)]
        items += [("o", grp, m) for m in range(0, 8, 2)]
    return items


def group_tiles(grp):
    return range(grp * FG, min(NF, (grp + 1) * FG))


def residual_plan(n):
    order = []
    for i in range(NT + 2):
        if i <= NT:
            order.append((f"b{n}", i))
        if i >= 1:
            order.append((f"f{n}", i - 1))
    return order


def psum_plan():
    order = ["par"] + [("n1", i) for i in range(NT + 1)]
    for i in range(NT + 1):
        order += [("kv", i)] + ([("kT", i - 1)] if i else [])
    order += ["cproj"]
    order += [("in", m, c) for m in range(8) for c in range(2)]
    order += ["C", "h0", ("SA", 0)]
    for j in range(NPAIR):
        order += ([("SA", j + 1)] if j + 1 < NPAIR else []) + [("SB", j)]
    order += [("V", j) for j in range(NPAIR)]
    order += ["ys", "st"] + [("sst", q) for q in range(4)]
    order += [("bt", h) for h in range(NH)]
    n = len(attention_units())
    for a in range(n + AHEAD + 1):
        if a < n:
            order.append(("SC", a))
        if AHEAD <= a < n + AHEAD:
            order.append(("TR", a - AHEAD))
        if a > AHEAD:
            order.append(("PV", a - AHEAD - 1))
        order += BETWEEN.get(a, [])
    order += [("wT", b) for b in range(DB)] + ["wS", "wP", "wO"]
    order += [("gT", b, g) for b in range(DB) for g in range(NKV)] + ["gS", "gP", "gO"]
    order += ["oT0", "oT1"]
    order += [("glu", m, c) for m in range(4) for c in range(2)]
    order += [("ss", c) for c in range(2)]
    order += [("n0", i) for i in range(NT + 1)]
    order += [("wo", m, c) for m in range(8) for c in range(2)]
    order += residual_plan(1)
    order += [("mn", i) for i in range(2)] + [("mk", c) for c in range(8)] + ["mT"]
    order += [("xq", m, c) for m in range(4) for c in range(2)]
    order += [("xT", b) for b in range(DB)] + ["xS", "xP", "xO"]
    for i in range(NT + 1):
        if i < NT:
            order += [("XS", i)]
        if i >= 1:
            order += [("XT", i - 1), ("XO", i - 1)]
    order += [("xo", m, c) for m in range(8) for c in range(2)]
    order += residual_plan(2)
    for item in ffn_items():
        if item[0] == "o":
            order += [("wf", item[1], item[2] + n, c) for n in range(2) for c in range(2)]
        else:
            order += [item + (c,) for c in range(2)]
    order += [("b3", i) for i in range(NT + 1)]
    return {k: n for n, k in enumerate(order)}


def hymba_step(nc, x_prompt, x_sample, cache_kv_cmp, cache_kv_sel, cache_kv_win, state_ssm_re, state_ssm_im,
               cache_mem_kv, page_table, mem_prompt, w_in, w_out, norm_g, grp_norm_g, cmp_pos, cmp_proj,
               rel_bias, ssm_a_re, ssm_a_im, ssm_b_re, ssm_b_im, ssm_c_re, ssm_c_im, ssm_d, ssm_log_dt,
               glu_w, glu_b, mem_norm_g, xq, xkv, xo, ffn_wi, ffn_wo,
               y_prompt, y_sample, p_kv_cmp, p_kv_sel, p_kv_win, p_ssm_re, p_ssm_im, p_mem_kv,
               s_kv_cmp, s_kv_sel, s_kv_win, s_ssm_re, s_ssm_im):
    U = psum_plan()
    AT = attention_units()
    ctx = ExitStack()
    with ctx:
        def sb(name, shape, dt=F32):
            return ctx.enter_context(nc.sbuf_tensor(name, shape, dt))

        def sem(name):
            return ctx.enter_context(nc.semaphore(name))

        ident = sb("ident", [P, P])
        flip = sb("flip", [P, P])
        ones = sb("ones", [P, P])
        same = sb("same", [64, 64])
        spread = sb("spread", [SLOTS, SL])
        block_of = sb("block_of", [P, 4])
        dt2 = sb("dt2", [NPAIR, 2])
        cols = sb("cols", [P, 120])
        d_rows = sb("d_rows", [P, NPAIR])
        gates = sb("gates", [P, NT + 1, NG])
        tab = sb("tab", [NH, 32])
        eps_c = sb("eps_c", [P, 1])
        st = sb("st", [P, 64])
        kcT = sb("kcT", [P, NKV, 32])
        vc = sb("vc", [32, NKV * HD])
        csum = sb("csum", [P, 2, 32])
        pblk = sb("pblk", [P, 2, P])
        osT = sb("osT", [P, 3, 64])
        V64 = sb("V64", [64, WIN + 1])
        yS = sb("yS", [P, 4, DB])
        uS = sb("uS", [P, 4, DB])
        apow = sb("apow", [P, 6, 2, NPAIR])
        line = sb("line", [SL, 64], U32)
        pline = sb("pline", [P, 4, DB], U32)
        ptc = sb("ptc", [P, DB], I32)
        tiny = sb("tiny", [P, 16], I32)
        tinyf = sb("tinyf", [P, 16])
        jota_i = sb("jota_i", [64, 64], I32)
        jota = sb("jota", [64, 64])
        ptrow = sb("ptrow", [64, NPAGE], I32)
        co = sb("co", [P, 2, NPAIR])

        arena_at = -(-nc.sbuf_base // 32) * 32
        A = sb("A", [P, 49504])

        def at(first, *shape):
            n = int(np.prod(shape))
            v = A[:, first:first + n]
            if len(shape) == 2:
                v = v.rearrange("p (a b) -> p a b", b=shape[1])
            elif len(shape) == 3:
                v = v.rearrange("p (a b c) -> p a b c", b=shape[1], c=shape[2])
            elif len(shape) == 4:
                v = v.rearrange("p (a b c d) -> p a b c d", b=shape[1], c=shape[2], d=shape[3])
            return v

        def exact(name, first, *shape, dt=F32R):
            v = nc.alloc_sbuf_tensor_at(name, [P, int(np.prod(shape))], dt, offset=arena_at + 4 * first)[:, :]
            if len(shape) == 2:
                v = v.rearrange("p (a b) -> p a b", b=shape[1])
            return v

        qT = at(0, 4, TC)
        vkeep = at(4128, NT, 2 * P)
        kTd = exact("kTd", 6176, 2 * NKV, T, dt=F32)
        kH = exact("kH", 33056, 2 * NKV, T)
        kL = exact("kL", 6176, 2 * NKV, T)
        qS = exact("qS", 43296, QS, P)
        U2 = at(10272, NPAIR, NC)
        summ = at(14368, DB, 2 * P)
        kcTs = at(16416, DB, P)
        vcs = at(17440, DB, P)
        hT = at(18464, KD, TC)
        wkv = at(26720, KD, KVC + NG)
        gring = at(26720, 3, ROWS * 256)
        NS = 4
        wring = at(33056, NS, KD, P)
        xin = at(37152, 2, D)
        junk = at(39200, D)
        uTm = at(40224, 2, TC)
        kvst = at(42288, 2, KVC + NG)
        posP = at(43872, 256)
        cprod = at(44128, 2, 256)
        prow = at(44896, P)
        drow = at(45024, P)
        dtrow = at(49376, P)
        kvS = at(45152, KVC)
        H = at(18464, NC + 1, 2, NPAIR)
        CP = at(37152, 2, NPAIR, 5, 32)
        Tm = [at(42272, P), at(43296, P)]
        Wm = [at(42400, 2, P), at(43424, 2, P)]
        sTm = [at(26720, 2, P), at(26976, 2, P)]
        posB = at(43872, ROWS, P)
        WT = at(44896, 2, NPAIR, P)
        bb = at(18464, 2, NPAIR, 16)
        braw = at(18464 + 512, 2, NPAIR, 16)
        cc = at(18464 + 1024, 2, NPAIR, 16)
        q = at(18464 + 1536, 4, NPAIR, 16)
        craw = at(18464 + 2560, 8, HD)
        h0row = at(18464 + 3072, 2, 2048)
        V8 = at(46000, VL)
        prm = at(47200, 16, NPAIR)
        st_rows = at(44352, P)
        sst_rows = at(40224, 4 * D)
        r1 = at(44896, 16, 2, 2 * NPAIR)
        turn = A[:, 46912:46912 + 17 * 64].rearrange("p (n a b j) -> p n a b j", n=17, a=2, b=2)
        apw = at(44896 + 1024, 15, 2, NPAIR)
        us3 = at(42656, NPAIR, DB)
        h0T = at(42784, 2, NPAIR, DB)
        hs = at(49024, 2, NPAIR, DB)
        yF = at(44896, 4, TC)
        SQ = at(37152, 4, TC)
        RS = at(41280, TC)
        oF = at(26720, 4, TC)
        scr = at(17952, 512)
        junk2 = at(14368, D)
        BT = at(18464, NH, T)
        far = at(37152, NH, P)
        Pm = at(38176, NPM, T)
        PT = at(41248, 2, T)
        hank = at(38176, 2, T)
        oN = at(10272, NT, NH * HD)
        nbuf = at(18464, DB, 4, 256)
        kTw = at(37152, DB, 512)
        Pw = at(41248, 512)
        PTw = at(41760, 4, 64)
        Pc = at(14368, P)
        PcT = at(14496, 64)
        score = at(14560, 64)
        score2 = at(14624, 64)
        top = at(14688, 16)
        topi = at(14704, 16).bitcast(U32)
        pick = at(14720, 16)
        phys = at(14736, 16)
        is62 = at(14752, 16)
        p15 = at(14768, 64)
        cbias = at(14832, P)
        jphys = at(15024, 64)
        onehot = at(15152, SLOTS, 64)
        sbias = at(15152, ROWS, SK)
        sdiff = at(16128, PICK, LINES)
        kTs = at(37152, DB, ROWS, SK)
        Vs = at(18464, 2 * DB, ROWS, HD)
        Ps = at(10272 + 4096, ROWS, SK)
        PTs = at(10272 + 4096 + 1024, ROWS, 64)
        qz = sb("qz", [P, DB, 64])
        oS = at(16416, 3, NH * HD)
        mT = hT
        x1 = at(0, NT + 1, D)
        yT = at(37152, KD, TC)
        q2T = at(26720, XH, TC)
        mkv = at(30848, 2, D)
        mkT = at(46432, XH, NM)
        grow = at(45408, D)
        tb = at(47456, 2, D)
        Px = at(10272, 2, XH * NM)
        PTx = at(12320, 2, XH * NM)
        kst = at(14368, 2, 2, 512)
        qxz = at(16416, XH, DB, 32)
        mrow = at(10272, 2, D)
        memT = at(12320, KD, NM)
        Vm = at(18464, DB, 2, 512)
        kTm = at(37152, DB, XH, NM)
        Pxs = at(17440, NM)
        PTxs = at(17440 + 256, 2, 32)
        sT = at(17440 + 320, 1)

        hH = exact("hH", 18464, KD, TC)
        hL = exact("hL", 9216, KD, TC)
        hRaw = exact("hRaw", 9216, KD, TC, dt=F32)
        gH = exact("gH", 26720, FG, TC)
        gL = exact("gL", 26720 + FG * TC, FG, TC)
        gRaw = exact("gRaw", 26720 + FG * TC, FG, TC, dt=F32)
        wRaw = exact("wRaw", 33056, NS, KD * P, dt=F32)
        wH = [exact("wH0", 45408, KD * P), exact("wH1", 47456, KD * P)]
        wL = [exact("wL0", 46432, KD * P), exact("wL1", 48480, KD * P)]

        PS = ctx.enter_context(nc.psum_tensor("PS", [P, 8, 512], F32))

        def slot(key):
            s = U[key] % 4
            return PS[:, 2 * s:2 * s + 2, :].rearrange("p a b -> p (a b)")

        def chunked(key):
            s = U[key] % 4
            return PS[:, 2 * s:2 * s + 2, 0:CH]

        bias_dram = nc.dram_tensor("bias_by_distance", [NH, VL], F32, kind="Internal").ap()
        win_row = nc.dram_tensor("new_window_row", [DB, 256], F32, kind="Internal").ap()
        sel_row = nc.dram_tensor("new_selected_row", [DB, 256], F32, kind="Internal").ap()

        filled = sem("filled")
        emptied = [sem(f"emptied{s}") for s in range(4)]
        w_loaded = [sem(f"w_loaded{s}") for s in range(NS)]
        consts = sem("consts")
        params = sem("params")
        x_in = [sem(f"x_in{s}") for s in range(2)]
        wkv_in = sem("wkv_in")
        pos_in = sem("pos_in")
        pblk_zero = sem("pblk_zero")
        tab_in = sem("tab_in")
        s5_arg = sem("s5_arg")
        s5_fun = sem("s5_fun")
        win_stored = sem("win_stored")
        states_staged = sem("states_staged")
        res_stat2 = sem("res_stat2")
        mem_stat = sem("mem_stat")
        on_stat = sem("on_stat")
        pw_stat = sem("pw_stat")
        px_stat = sem("px_stat")
        oF_ready = sem("oF_ready")
        mkv_out = sem("mkv_out")
        qxz_zero = sem("qxz_zero")
        lanes = sem("lanes")
        b_in = sem("b_in")
        c_in = sem("c_in")
        xn_ready = sem("xn_ready")
        rt_ready = sem("rt_ready")
        kv_stored = [sem(f"kv_stored{s}") for s in range(2)]
        kv_ready = sem("kv_ready")
        prod_ready = sem("prod_ready")
        rows_saved = sem("rows_saved")
        gat = [sem(f"gat{s}") for s in range(3)]
        gat_used = sem("gat_used")
        posB_in = sem("posB_in")
        posB_used = sem("posB_used")
        summ_ready = sem("summ_ready")
        pline_ready = sem("pline_ready")
        pt_in = sem("pt_in")
        s5_built = sem("s5_built")
        s5_states = sem("s5_states")
        hs_ready = sem("hs_ready")
        u_moved = sem("u_moved")
        uT_ready = sem("uT_ready")
        qz_ready = sem("qz_ready")
        pc_ready = sem("pc_ready")
        phys_ready = sem("phys_ready")
        line_ready = sem("line_ready")
        v8_ready = sem("v8_ready")
        v8_out = sem("v8_out")
        V64_in = sem("V64_in")
        hank_in = [sem(f"hank_in{s}") for s in range(2)]
        far_ready = sem("far_ready")
        bt_ready = sem("bt_ready")
        k_hi = sem("k_hi")
        k_lo = sem("k_lo")
        q_hi = sem("q_hi")
        q_lo = sem("q_lo")
        dve_gate = sem("dve_gate")
        exp_ready = sem("exp_ready")
        branch_done = sem("branch_done")
        nbuf_in = sem("nbuf_in")
        nrow_in = sem("nrow_in")
        vs_ready = sem("vs_ready")
        pw_raw = sem("pw_raw")
        pw_exp = sem("pw_exp")
        pw_ready = sem("pw_ready")
        oS_ready = sem("oS_ready")
        y_ready = sem("y_ready")
        gelu_ready = sem("gelu_ready")
        sq_ready = sem("sq_ready")
        ssr_ready = sem("ssr_ready")
        m_ready = sem("m_ready")
        on_ready = sem("on_ready")
        x1_in = sem("x1_in")
        grow_in = sem("grow_in")
        tb_free = sem("tb_free")
        res_stat = sem("res_stat")
        res_sum = sem("res_sum")
        res_norm = sem("res_norm")
        mem_in = sem("mem_in")
        mem_norm = sem("mem_norm")
        vm_in = sem("vm_in")
        kst_in = [sem(f"kst_in{s}") for s in range(2)]
        qxz_ready = sem("qxz_ready")
        px_raw = sem("px_raw")
        px_exp = sem("px_exp")
        px_ready = sem("px_ready")
        h_hi = sem("h_hi")
        h_lo = sem("h_lo")
        w_hi = sem("w_hi")
        w_lo = sem("w_lo")
        g_prod = sem("g_prod")
        g_hi = sem("g_hi")
        g_lo = sem("g_lo")
        states_out = sem("states_out")
        out_ready = sem("out_ready")
        stored = sem("stored")
        dve_own = sem("dve_own")
        act_own = sem("act_own")
        pool_own = sem("pool_own")

        def full(eng, key):
            eng.wait_ge(filled, U[key] + 1)

        def read_out(eng, key):
            eng.wait_ge(emptied[U[key] % 4], U[key] // 4 + 1)

        def free(ins, key):
            ins.then_inc(emptied[U[key] % 4], 1)

        class Own:

            def __init__(self, eng, s):
                self.eng, self.sem, self.n = eng, s, 0

            def step(self, ins):
                ins.then_inc(self.sem, 1)
                self.n += 1

            def settle(self):
                self.eng.wait_ge(self.sem, self.n)

            def then(self, ins):
                self.step(ins)
                self.settle()

        stream = []
        wi_, wo_ = w_in[0], w_out[0]
        for m in range(8):
            c0 = m * P if m < 4 else OFF_U + (m - 4) * P
            stream.append((wi_[:, c0:c0 + P], KD, ("in", m, 1)))
        for m in range(4):
            stream.append((glu_w[0][:, m * P:(m + 1) * P], 4, ("glu", m, 1)))
        for m in range(8):
            stream.append((wo_[:, m * P:(m + 1) * P], KD, ("wo", m, 1)))
        for m in range(8):
            stream.append((xkv[0][:, m * P:(m + 1) * P], KD, ("mk", m)))
        for m in range(4):
            stream.append((xq[0][:, m * P:(m + 1) * P], KD, ("xq", m, 1)))
        for m in range(8):
            stream.append((xo[0][:, m * P:(m + 1) * P], 4, ("xo", m, 1)))
        ffn = ffn_items()
        first_ffn = len(stream)
        for item in ffn:
            if item[0] == "o":
                tiles = group_tiles(item[1])
                src = ffn_wo[0][tiles[0] * P:(tiles[-1] + 1) * P, item[2] * P:(item[2] + 2) * P]
                stream.append((src, len(tiles), None))
            else:
                c0 = item[1] * P + (DFF if item[0] == "u" else 0)
                stream.append((ffn_wi[0][:, c0:c0 + P], KD, None))

        def last_unit(item):
            return ("wf", item[1], item[2] + 1, 1) if item[0] == "o" else item + (1,)

        def group_size(item):
            return len(group_tiles(item[1])) * 2 * P if item[0] == "o" else KD * P

        block = ctx.enter_context(nc.Block())

        @block.sync
        def _(sp):
            for i in range(NT + 1):
                c0, n = token_tile(i)
                if i >= 2:
                    full(sp, ("n1", i - 2))
                src = x_prompt[0, c0:c0 + n, :] if i < NT else x_sample[:, 0, :]
                sp.dma_start(xin[0:n, i % 2, :], src).then_inc(x_in[i % 2], 16)
                if i == 1:
                    sp.dma_start(wkv, wi_[:, NH * HD:OFF_U].rearrange("(k p) n -> p k n", p=P)).then_inc(wkv_in, 16)
            for it, (src, kt, _) in enumerate(stream):
                if it >= NS + first_ffn:
                    sp.wait_ge(w_lo, it - NS - first_ffn + 1)
                elif it == 8:
                    full(sp, ("SC", len(AT) - 1))
                elif it >= NS and not 8 < it < 8 + NS:
                    full(sp, stream[it - NS][2])
                cols_ = src.shape[1]
                ring_slot = wRaw[:, it % NS] if it >= first_ffn else wring[:, it % NS].rearrange("p k n -> p (k n)")
                sp.dma_start(ring_slot[:, 0:kt * cols_]
                             .rearrange("p (k n) -> p k n", n=cols_),
                             src.rearrange("(k p) n -> p k n", p=P)).then_inc(w_loaded[it % NS], 16)

        @block.tensor
        def _(pe):
            item = [0]

            def open_(key):
                if U[key] >= 4:
                    pe.wait_ge(emptied[U[key] % 4], U[key] // 4)
                return slot(key)

            def mm(out, lhsT, rhs, start=True, stop=True):
                return nc.tensor.matmul(out, lhsT=lhsT, rhs=rhs, start=start, stop=stop, skip_group_check=True)

            def tr(out, in_):
                b, n = in_.base_partition(), in_.shape[0]
                return nc.tensor.transpose(out, in_, ident[b:b + n, b:b + n])

            def next_weights():
                it = item[0]
                item[0] += 1
                pe.wait_ge(w_loaded[it % NS], 16 * (it // NS + 1))
                return wring[:, it % NS]

            def dense(stage, tiles, kts, rhs, before=None):
                for m in range(tiles):
                    if before:
                        before(m)
                    a, b = (stage, m, 0), (stage, m, 1)
                    open_(a)
                    open_(b)
                    outs = [chunked(a)[:, 0], chunked(a)[:, 1], chunked(b)[:, 0]]
                    k, last = 0, sum(kts) - 1
                    for n, kt in enumerate(kts):
                        w = next_weights()
                        for kk in range(kt):
                            r = rhs(k)
                            for c in range(3):
                                ins = mm(outs[c], w[:, kk], r[:, c * CH:(c + 1) * CH], k == 0, k == last)
                                if k == last and c >= 1:
                                    ins.then_inc(filled, 1)
                            k += 1

            pe.wait_ge(consts, 5)
            pe.wait_ge(params, 16 * PARAM_DMAS)
            s = open_("par")
            tr(s[:, 0:104], prow[0:104])
            tr(s[:, 104:120], dtrow[0:NPAIR])
            tr(s[:, 128:128 + NPAIR], drow[0:NPAIR]).then_inc(filled, 1)

            for i in range(NT + 1):
                n = token_tile(i)[1]
                pe.wait_ge(xn_ready, i + 1)
                s = open_(("n1", i))
                for k in range(KD):
                    ins = tr(s[:, k * P:k * P + n], xin[0:n, i % 2, k * P:(k + 1) * P])
                ins.then_inc(filled, 1)

            def kv_transposes(i):
                pe.wait_ge(prod_ready, i + 1)
                s = open_(("kT", i))
                for br in range(2):
                    tr(s[:, br * P:(br + 1) * P], kvst[:, i % 2, 256 * (br + 1):256 * (br + 1) + P])
                for c in range(2):
                    ins = mm(s[:, 256 + 4 * c:260 + 4 * c], cprod[:, i % 2, c * P:(c + 1) * P], block_of[:, :])
                ins.then_inc(filled, 1)

            pe.wait_ge(wkv_in, 16)
            for i in range(NT + 1):
                c0, n = token_tile(i)
                read_out(pe, ("n1", i))
                s = open_(("kv", i))
                for k in range(KD):
                    mm(s[0:n, 0:512], hT[:, k, c0:c0 + n], wkv[:, k, 0:512], k == 0, k == KD - 1)
                    ins = mm(s[0:n, 512:KVC + NG], hT[:, k, c0:c0 + n], wkv[:, k, 512:KVC + NG], k == 0, k == KD - 1)
                ins.then_inc(filled, 1)
                if i:
                    kv_transposes(i - 1)
            read_out(pe, ("kT", NT - 1))
            s = open_("cproj")
            mm(s[:, 0:32], pblk[:, 0], csum[:, 0])
            mm(s[0:32, 32:32 + P], csum[:, 1], pblk[:, 1]).then_inc(filled, 1)

            dense("in", 8, [KD], lambda k: hT[:, k])

            pe.wait_ge(c_in, 64)
            s = open_("C")
            for n in range(8):
                ins = tr(s[0:HD, n * P:(n + 1) * P], craw[:, n])
            ins.then_inc(filled, 1)
            s = open_("h0")
            for part in range(2):
                for j in range(NPAIR):
                    c = (part * NPAIR + j) * DB
                    ins = tr(s[:, c:c + DB], h0row[0:DB, part, j * P:(j + 1) * P])
            ins.then_inc(filled, 1)

            def s5_matrices(j):
                s = open_(("SA", j))
                for part in range(2):
                    tr(s[:, part * P:(part + 1) * P], WT[:, part, j])
                for l in range(L4):
                    for part in range(2):
                        ins = mm(s[32 * l:32 * l + 32, 512 + 32 * l:640], WT[:, part, j, 96:P],
                                 CP[:, part, j, 0:L4 - l].rearrange("p k c -> p (k c)"), part == 0, part == 1)
                ins.then_inc(filled, 1)

            pe.wait_ge(s5_built, 1)
            pe.wait_ge(u_moved, 1)
            s5_matrices(0)
            for j in range(NPAIR):
                if j + 1 < NPAIR:
                    s5_matrices(j + 1)
                read_out(pe, ("SA", j))
                s = open_(("SB", j))
                for part in range(2):
                    mm(s[:, part * NC:(part + 1) * NC], Wm[j % 2][:, part], U2[:, j])
                for part in range(2):
                    mm(s[:, 512 + part * DB:512 + (part + 1) * DB], Wm[j % 2][96:P, part], us3[96:P, j])
                mm(s[:, 528:528 + NC], Tm[j % 2], U2[:, j]).then_inc(filled, 1)

            pe.wait_ge(s5_states, 1)
            for j in range(NPAIR):
                s = open_(("V", j))
                for part in range(2):
                    ins = mm(s[:, 0:NC], CP[:, part, j, 1:5].rearrange("p k c -> p (k c)"), H[:, 0:NC, part, j],
                             part == 0, part == 1)
                ins.then_inc(filled, 1)
            pe.wait_ge(hs_ready, 1)
            s = open_("ys")
            for j in range(NPAIR):
                q, m = j % 4, j // 4
                for part in range(2):
                    ins = mm(s[32 * q:32 * q + 32, m * DB:(m + 1) * DB], CP[:, part, j, 0], hs[:, part, j],
                             part == 0, part == 1)
            ins.then_inc(filled, 1)
            s = open_("st")
            tr(s[0:32, 0:P], H[:, NC].rearrange("p a j -> p (a j)")).then_inc(filled, 1)
            for q in range(4):
                s = open_(("sst", q))
                for n in range(8):
                    r = q * 8 + n
                    ins = tr(s[0:DB, n * P:(n + 1) * P], hs[:, r // NPAIR, r % NPAIR])
                ins.then_inc(filled, 1)

            for h in range(NH):
                pe.wait_ge(hank_in[h % 2], 16 * (h // 2 + 1))
                s = open_(("bt", h))
                for c in range(2):
                    ins = mm(s[:, c * 512:(c + 1) * 512], flip[:, :], hank[:, h % 2, c * 512:(c + 1) * 512])
                ins.then_inc(filled, 1)

            def compressed_branch(key):
                if key[0] == "sT":
                    b = key[1]
                    pe.wait_ge(summ_ready, b + 1)
                    s = open_(key)
                    for c in range(2):
                        ins = tr(s[:, c * P:(c + 1) * P], summ[:, b, c * P:(c + 1) * P])
                    ins.then_inc(filled, 1)
                elif key[0] == "sP":
                    b = key[1]
                    read_out(pe, ("sT", b))
                    s = open_(key)
                    mm(s[:, 0:P], pblk[:, 0], sTm[b % 2][:, 0])
                    mm(s[:, P:2 * P], sTm[b % 2][:, 1], pblk[:, 1]).then_inc(filled, 1)
                elif key == "sc":
                    read_out(pe, ("sP", DB - 1))
                    read_out(pe, ("sP", DB - 2))
                    pe.wait_ge(qz_ready, 1)
                    s = open_(key)
                    for b in range(DB):
                        ins = mm(s[0:64, 0:P], qz[:, b], kcTs[:, b], b == 0, b == DB - 1)
                    ins.then_inc(filled, 1)
                elif key == "sps":
                    pe.wait_ge(pc_ready, 1)
                    s = open_(key)
                    mm(s[0:64, 0:P], same[:, :], Pc[0:64]).then_inc(filled, 1)
                elif key == "scT":
                    s = open_(key)
                    tr(s[:, 0:64], Pc[0:64]).then_inc(filled, 1)
                elif key == "sov":
                    read_out(pe, "scT")
                    s = open_(key)
                    for b in range(DB):
                        ins = mm(s[:, b * 8:b * 8 + 8], vcs[:, b], PcT[:, b * 8:b * 8 + 8])
                    ins.then_inc(filled, 1)
                elif key == "ix1":
                    pe.wait_ge(phys_ready, 1)
                    s = open_(key)
                    tr(s[0:SLOTS, 0:64], phys[0:64, 0:SLOTS]).then_inc(filled, 1)
                elif key == "ix2":
                    read_out(pe, "ix1")
                    s = open_(key)
                    mm(s[0:SL, 0:64], spread[:, :], p15[0:SLOTS]).then_inc(filled, 1)

            n_at = len(AT)

            for a in range(n_at + AHEAD + 1):
                if a < n_at:
                    i, h, br, k0, nk = AT[a]
                    lo = 64 * (h % 2)
                    s = open_(("SC", a))
                    if br == 0:
                        ins = mm(s[:, 0:nk], qT[lo:lo + 64, h // 2, i * P:(i + 1) * P], kcT[lo:lo + 64, h // GQ, 0:nk])
                    else:
                        n = (br - 1) * NKV + h // GQ
                        if a == 1:
                            pe.wait_ge(k_lo, 1)
                        if br == 1:
                            pe.wait_ge(q_lo, a // 3 + 1)
                        for c in range(0, nk, 512):
                            w = min(512, nk - c)
                            mm(s[:, c:c + w], qS[:, a // 3 % QS], kL[:, n, k0 + c:k0 + c + w], True, False)
                            ins = mm(s[:, c:c + w], qS[:, a // 3 % QS], kH[:, n, k0 + c:k0 + c + w], False, True)
                    ins.then_inc(filled, 1)
                t = a - AHEAD
                if 0 <= t < n_at:
                    nk = AT[t][4]
                    pe.wait_ge(exp_ready, t + 1)
                    s = open_(("TR", t))
                    for c in range(0, nk, P):
                        w = min(P, nk - c)
                        ins = tr(s[0:w, c:c + P], Pm[:, t % NPM, c:c + w])
                    ins.then_inc(filled, 1)
                t -= 1
                if t >= 0:
                    i, h, br, k0, nk = AT[t]
                    g = h // GQ
                    read_out(pe, ("TR", t))
                    s = open_(("PV", t))
                    tiles = max(1, nk // P)
                    for n in range(tiles):
                        if br == 0:
                            v, rows = vc[0:nk, g * HD:(g + 1) * HD], nk
                        else:
                            c = (br - 1) * P + g * HD
                            v, rows = vkeep[:, k0 // P + n, c:c + HD], P
                        ins = mm(s[:, 0:HD], PT[0:rows, t % 2, n * P:(n + 1) * P], v, n == 0, n == tiles - 1)
                    ins.then_inc(filled, 1)
                for key in BETWEEN.get(a, []):
                    compressed_branch(key)

            pe.wait_ge(nbuf_in, 16 * 3 * DB)
            for b in range(DB):
                s = open_(("wT", b))
                for j in range(4):
                    ins = tr(s[:, j * P:(j + 1) * P], nbuf[:, b, j, 0:P])
                ins.then_inc(filled, 1)
            for b in range(DB - 4, DB):
                read_out(pe, ("wT", b))
            s = open_("wS")
            for b in range(DB):
                ins = mm(s[0:64, 0:512], qz[:, b], kTw[:, b], b == 0, b == DB - 1)
            ins.then_inc(filled, 1)
            pe.wait_ge(pw_ready, 1)
            s = open_("wP")
            for j in range(4):
                ins = tr(s[:, j * 64:(j + 1) * 64], Pw[0:64, j * P:(j + 1) * P])
            ins.then_inc(filled, 1)
            read_out(pe, "wP")
            s = open_("wO")
            for b in range(DB):
                for j in range(4):
                    ins = mm(s[:, b * 8:b * 8 + 8], nbuf[:, b, j, P:2 * P], PTw[:, j, b * 8:b * 8 + 8], j == 0, j == 3)
            ins.then_inc(filled, 1)

            for n in range(2 * DB):
                b, g = n // 2, n % 2
                pe.wait_ge(gat[n % 3], 16 * GAT0[n % 3] + 16 * 2 * (n // 3 + 1))
                s = open_(("gT", b, g))
                for r in range(ROWS):
                    c = r * SK if r < 4 else 512 + (r - 4) * SK
                    ins = tr(s[0:HD, c:c + SK], gring[0:SK, n % 3, r * 256 + g * HD:r * 256 + (g + 1) * HD])
                ins.then_inc(filled, 1)
            for n in range(2 * DB - 4, 2 * DB):
                read_out(pe, ("gT", n // 2, n % 2))
            s = open_("gS")
            for b in range(DB):
                for half in range(2):
                    ins = mm(s[0:64, half * 512:half * 512 + 4 * SK], qz[:, b],
                             kTs[:, b, 4 * half:4 * half + 4].rearrange("p r c -> p (r c)"), b == 0, b == DB - 1)
            ins.then_inc(filled, 1)
            pe.wait_ge(pw_ready, 2)
            s = open_("gP")
            for r in range(ROWS):
                ins = tr(s[0:SK, r * 64:(r + 1) * 64], Ps[0:64, r])
            ins.then_inc(filled, 1)
            read_out(pe, "gP")
            pe.wait_ge(vs_ready, 2 * DB)
            s = open_("gO")
            for n in range(2 * DB):
                b, g = n // 2, n % 2
                c = b * 8 + 4 * g
                for r in range(ROWS):
                    ins = mm(s[64 * g:64 * g + 64, c:c + 4], Vs[0:SK, n, r], PTs[0:SK, r, c:c + 4],
                             r == 0, r == ROWS - 1)
            ins.then_inc(filled, 1)
            read_out(pe, "sov")
            read_out(pe, "wO")
            read_out(pe, "gO")
            for key, brs in (("oT0", (0, 1)), ("oT1", (2,))):
                s = open_(key)
                for br in brs:
                    for h in range(NH):
                        g = h // GQ
                        c = g * 512 + (br % 2) * 256 + (h % GQ) * HD
                        ins = tr(s[0:DB, c:c + HD],
                                 osT[64 * g:64 * g + 64, br].rearrange("p (b h) -> p h b", h=NH)[:, h])
                ins.then_inc(filled, 1)

            pe.wait_ge(gelu_ready, 1)
            dense("glu", 4, [4], lambda k: yF[:, k])
            pe.wait_ge(sq_ready, 1)
            for c in range(2):
                s = open_(("ss", c))
                for n in range(2 - c):
                    for k in range(4):
                        c0 = (2 * c + n) * CH
                        ins = mm(chunked(("ss", c))[:, n], ones[:, :], SQ[:, k, c0:c0 + CH], k == 0, k == 3)
                ins.then_inc(filled, 1)
            for i in range(NT + 1):
                n = token_tile(i)[1]
                pe.wait_ge(on_ready, i + 1)
                s = open_(("n0", i))
                for k in range(4):
                    src = oN[:, i, k * P:(k + 1) * P] if i < NT else oS[0:DB, 0, k * P:(k + 1) * P]
                    ins = tr(s[:, k * P:k * P + n], src)
                ins.then_inc(filled, 1)
            pe.wait_ge(m_ready, 2)
            dense("wo", 8, [KD], lambda k: mT[:, k])

            def residual(n):
                for m in (6, 7):
                    for c in range(2):
                        read_out(pe, ("wf", NGRP - 1, m, c) if n == 3 else ({1: "wo", 2: "xo"}[n], m, c))
                for i in range(NT + 2):
                    if i <= NT:
                        c0, r = token_tile(i)
                        s = open_((f"b{n}", i))
                        for k in range(KD):
                            ins = tr(s[0:r, k * P:(k + 1) * P], yT[:, k, c0:c0 + r])
                        ins.then_inc(filled, 1)
                    if i >= 1 and n < 3:
                        c0, r = token_tile(i - 1)
                        pe.wait_ge(res_norm, (n - 1) * (NT + 1) + i)
                        s = open_((f"f{n}", i - 1))
                        for k in range(KD):
                            ins = tr(s[:, k * P:k * P + r], tb[0:r, (i - 1) % 2, k * P:(k + 1) * P])
                        ins.then_inc(filled, 1)

            residual(1)

            for i in range(2):
                pe.wait_ge(mem_norm, i + 1)
                s = open_(("mn", i))
                for k in range(KD):
                    ins = tr(s[:, k * P:(k + 1) * P], mrow[:, i, k * P:(k + 1) * P])
                ins.then_inc(filled, 1)
            read_out(pe, ("mn", 0))
            read_out(pe, ("mn", 1))
            for c in range(8):
                w = next_weights()
                s = open_(("mk", c))
                for i in range(2):
                    for k in range(KD):
                        ins = mm(s[:, i * P:(i + 1) * P], memT[:, k, i * P:(i + 1) * P], w[:, k], k == 0, k == KD - 1)
                ins.then_inc(filled, 1)
            for c in range(4):
                read_out(pe, ("mk", c))
            s = open_("mT")
            for h in range(XH):
                for i in range(2):
                    ins = tr(s[:, (2 * h + i) * P:(2 * h + i + 1) * P], mkv[:, i, h * P:(h + 1) * P])
            ins.then_inc(filled, 1)
            for i in range(NT - 3, NT + 1):
                read_out(pe, ("f1", i))
            dense("xq", 4, [KD], lambda k: hT[:, k])

            for b in range(DB):
                pe.wait_ge(kst_in[b % 2], 16 * (b // 2 + 1))
                s = open_(("xT", b))
                for h in range(XH):
                    for i in range(2):
                        ins = tr(s[:, (2 * h + i) * P:(2 * h + i + 1) * P], kst[:, b % 2, i, h * P:(h + 1) * P])
                ins.then_inc(filled, 1)
            for b in range(DB - 4, DB):
                read_out(pe, ("xT", b))
            pe.wait_ge(qxz_ready, 1)
            s = open_("xS")
            for b in range(DB):
                for h in range(XH):
                    ins = mm(s[0:32, 0:NM], qxz[:, h, b], kTm[:, b, h], b + h == 0, b + h == DB + XH - 2)
            ins.then_inc(filled, 1)
            pe.wait_ge(px_ready, 1)
            s = open_("xP")
            for i in range(2):
                ins = tr(s[:, i * 32:(i + 1) * 32], Pxs[0:32, i * P:(i + 1) * P])
            ins.then_inc(filled, 1)
            read_out(pe, "xP")
            pe.wait_ge(vm_in, 16 * DB)
            s = open_("xO")
            for b in range(DB):
                for h in range(XH):
                    for i in range(2):
                        ins = mm(s[:, h * DB + b:h * DB + b + 1], Vm[:, b, i, h * P:(h + 1) * P],
                                 PTxs[:, i, b * XH + h:b * XH + h + 1], i == 0, i == 1)
            ins.then_inc(filled, 1)

            read_out(pe, "mT")
            for i in range(NT + 1):
                if i < NT:
                    s = open_(("XS", i))
                    for h in range(XH):
                        ins = mm(s[:, h * NM:(h + 1) * NM], q2T[:, h, i * P:(i + 1) * P], mkT[:, h])
                    ins.then_inc(filled, 1)
                if i >= 1:
                    pe.wait_ge(px_ready, i + 1)
                    s = open_(("XT", i - 1))
                    for c in range(8):
                        ins = tr(s[:, c * P:(c + 1) * P], Px[:, (i - 1) % 2, c * P:(c + 1) * P])
                    ins.then_inc(filled, 1)
                    read_out(pe, ("XT", i - 1))
                    s = open_(("XO", i - 1))
                    for h in range(XH):
                        for c in range(2):
                            ins = mm(s[:, h * P:(h + 1) * P], mkv[:, c, 512 + h * P:512 + (h + 1) * P],
                                     PTx[:, (i - 1) % 2, (2 * h + c) * P:(2 * h + c + 1) * P], c == 0, c == 1)
                    ins.then_inc(filled, 1)
            read_out(pe, "xO")
            for i in range(NT - 2, NT):
                read_out(pe, ("XO", i))
            dense("xo", 8, [4], lambda k: q2T[:, k])
            residual(2)

            def exact_products(outs, wh, wl, xh, xl, first, last):
                for n, (w, x) in enumerate(((wl, xh), (wh, xl), (wh, xh))):
                    for c in range(3):
                        ins = mm(outs[c], w, x[:, c * CH:(c + 1) * CH], first and n == 0, last and n == 2)
                        if last and n == 2 and c >= 1:
                            ins.then_inc(filled, 1)

            pe.wait_ge(h_lo, NT + 1)
            for it, item in enumerate(ffn):
                pe.wait_ge(w_lo, it + 1)
                wh, wl = wH[it % 2], wL[it % 2]
                if item[0] != "o":
                    a, b = item + (0,), item + (1,)
                    open_(a)
                    open_(b)
                    outs = [chunked(a)[:, 0], chunked(a)[:, 1], chunked(b)[:, 0]]
                    for k in range(KD):
                        exact_products(outs, wh[:, k * P:(k + 1) * P], wl[:, k * P:(k + 1) * P],
                                       hH[:, k], hL[:, k], k == 0, k == KD - 1)
                    continue
                grp, m0 = item[1:]
                tiles = group_tiles(grp)
                outs = []
                for m in (m0, m0 + 1):
                    a, b = ("wf", grp, m, 0), ("wf", grp, m, 1)
                    open_(a)
                    open_(b)
                    outs.append([chunked(a)[:, 0], chunked(a)[:, 1], chunked(b)[:, 0]])
                    if m == m0 and len(tiles) > 1:
                        pe.wait_ge(g_lo, tiles[-1])
                    for n in range(len(tiles) - 1):
                        c = n * 2 * P + (m - m0) * P
                        exact_products(outs[-1], wh[:, c:c + P], wl[:, c:c + P], gH[:, n], gL[:, n], n == 0, False)
                pe.wait_ge(g_lo, tiles[-1] + 1)
                n = len(tiles) - 1
                for m in range(2):
                    c = n * 2 * P + m * P
                    exact_products(outs[m], wh[:, c:c + P], wl[:, c:c + P], gH[:, n], gL[:, n], n == 0, True)
            residual(3)

        @block.gpsimd
        def _(pool):
            own = Own(pool, pool_own)
            g = nc.gpsimd

            own.step(g.memset(ident[:, :], 0.0))
            own.step(g.memset(flip[:, :], 0.0))
            own.step(g.memset(same[:, :], 1.0))
            own.step(g.memset(block_of[:, :], 1.0))
            own.step(g.memset(spread[:, :], 0.0))
            own.step(g.memset(qz[:, :, :], 0.0))
            g.memset(pblk[:, :, :], 0.0).then_inc(pblk_zero, 1)
            own.settle()
            g.affine_select(out=ident[:, :], in_=ident[:, :], compare_op=ALU.not_equal, fill=1.0, base=0,
                            pattern=[[-1, P]], channel_multiplier=1).then_inc(consts, 1)
            own.step(g.memset(ones[:, :], 1.0))
            g.affine_select(out=flip[:, :], in_=flip[:, :], compare_op=ALU.not_equal, fill=1.0, base=1 - P,
                            pattern=[[1, P]], channel_multiplier=1).then_inc(consts, 1)
            own.step(g.affine_select(out=same[:, :], in_=same[:, :], compare_op=ALU.is_ge, fill=0.0, base=0,
                                     pattern=[[-4, 16], [0, 4]], channel_multiplier=1))
            own.step(g.affine_select(out=block_of[:, :], in_=block_of[:, :], compare_op=ALU.is_ge, fill=0.0, base=0,
                                     pattern=[[-CB, 4]], channel_multiplier=1))
            own.step(g.iota(tiny[:, 0:1], pattern=[[0, 1]], base=0, channel_multiplier=1))
            own.step(g.iota(jota_i[:, :], pattern=[[1, 64]], base=0, channel_multiplier=0))
            own.settle()
            own.step(g.affine_select(out=same[:, :], in_=same[:, :], compare_op=ALU.is_ge, fill=0.0, base=3,
                                     pattern=[[4, 16], [0, 4]], channel_multiplier=-1))
            own.step(g.affine_select(out=spread[:, :], in_=spread[:, :], compare_op=ALU.not_equal, fill=1.0, base=0,
                                     pattern=[[-1, SLOTS], [0, LINES]], channel_multiplier=1))
            g.affine_select(out=block_of[:, :], in_=block_of[:, :], compare_op=ALU.is_ge, fill=0.0, base=CB - 1,
                            pattern=[[CB, 4]], channel_multiplier=-1).then_inc(consts, 1)
            own.settle()
            g.memset(eps_c[:, :], EPS).then_inc(consts, 1)

            pool.wait_ge(params, 16 * PARAM_DMAS)
            g.tensor_copy(dtrow[0:NPAIR].rearrange("j (a p) -> j a p", a=2),
                          dt2[:, :].unsqueeze(2).to_broadcast([NPAIR, 2, 64])).then_inc(consts, 1)

            pool.wait_ge(tab_in, 16)
            own.then(g.tensor_scalar(tab[:, :], tab[:, :], 1.0 / SC, None, ALU.mult))
            for bucket, d0, d1 in bucket_ranges():
                own.step(g.tensor_copy(V8[0:NH, T - 1 - d1:T - d0],
                                       tab[:, bucket:bucket + 1].to_broadcast([NH, d1 - d0 + 1])))
            own.step(g.memset(V8[0:NH, T:VL], NEG))
            own.settle()
            pool.dma_start(bias_dram, V8[0:NH]).then_inc(v8_out, 16)
            pool.wait_ge(v8_out, 16)
            pool.dma_start(V64[:, :], bass.AP(bias_dram.tensor, T - 1 - WIN, [[0, DB], [VL, NH], [1, WIN + 1]]))\
                .then_inc(V64_in, 16)

            for i in range(NT + 1):
                pool.wait_ge(kv_ready, i + 1)
                if i < NT:
                    rows = slice(i * P, (i + 1) * P)
                    k = kvst[:, i % 2]
                    done = kv_stored[i % 2]
                    pool.dma_start(p_kv_cmp[0, 0, rows].rearrange("s c g d -> s (c g d)"), k[:, 0:256]).then_inc(done, 16)
                    pool.dma_start(p_kv_sel[0, 0, rows].rearrange("s c g d -> s (c g d)"), k[:, 256:512]).then_inc(done, 16)
                    if i >= NT - WIN // P:
                        w = slice(i * P - (T - WIN), (i + 1) * P - (T - WIN))
                        pool.dma_start(p_kv_win[0, 0, w].rearrange("s c g d -> s (c g d)"), k[:, 512:768]).then_inc(done, 16)
                else:
                    pool.dma_start(s_kv_cmp[0, :, 0].rearrange("b c g d -> b (c g d)"), kvS[0:DB, 0:256]).then_inc(rows_saved, 16)
                    pool.dma_start(s_kv_sel[0, :, 0].rearrange("b c g d -> b (c g d)"), kvS[0:DB, 256:512]).then_inc(rows_saved, 16)
                    pool.dma_start(sel_row, kvS[0:DB, 256:512]).then_inc(rows_saved, 16)
                    pool.dma_start(win_row, kvS[0:DB, 512:768]).then_inc(rows_saved, 16)

            pool.wait_ge(k_hi, 1)
            g.tensor_tensor(kL, kTd, kH, ALU.subtract).then_inc(k_lo, 1)

            full(pool, "ys")
            for h in range(NH):
                if h >= 2:
                    full(pool, ("bt", h - 2))
                pool.dma_start(hank[:, h % 2], bass.AP(bias_dram.tensor, h * VL, [[1, P], [1, T]]))\
                    .then_inc(hank_in[h % 2], 16)
            pool.wait_ge(states_staged, 1)
            pool.dma_start(p_ssm_re[0, 0].rearrange("(j a) p -> j (a p)", a=2), st_rows[0:NPAIR]).then_inc(states_out, 16)
            pool.dma_start(p_ssm_im[0, 0].rearrange("(j a) p -> j (a p)", a=2), st_rows[NPAIR:2 * NPAIR]).then_inc(states_out, 16)
            pool.wait_ge(states_staged, 2)
            pool.dma_start(s_ssm_re[0].rearrange("b g p -> b (g p)"), sst_rows[0:DB, 0:2048]).then_inc(states_out, 16)
            pool.dma_start(s_ssm_im[0].rearrange("b g p -> b (g p)"), sst_rows[0:DB, 2048:4096]).then_inc(states_out, 16)
            read_out(pool, ("bt", NH - 1))
            for h in range(NH):
                g.affine_select(out=far[:, h], in_=BT[:, h, T - P - WIN:T - WIN], compare_op=ALU.is_gt, fill=NEG,
                                base=0, pattern=[[1, P]], channel_multiplier=-1).then_inc(far_ready, 1)

            pool.wait_ge(pline_ready, 1)
            pool.wait_ge(states_out, 64)
            pool_c = cache_kv_cmp[0].rearrange("n (a r) c g d -> (n a) (r c g d)", r=ROWS)
            for n in range(4 * DB):
                k, b = n // DB, n % DB
                if n >= 3:
                    pool.wait_ge(gat_used, n - 2)
                if b == 0:
                    if k:
                        pool.wait_ge(gat_used, n)
                    for c in range(2):
                        pool.dma_start(posB[:, :, c * HD:(c + 1) * HD],
                                       bass.AP(cmp_pos.tensor, (c * CB + k * ROWS) * HD,
                                               [[0, P], [HD, ROWS], [1, HD]])).then_inc(posB_in, 16)
                pool.indirect_dma_start(out=gring[:, n % 3], out_offset=None, in_=pool_c,
                                        in_offset=bass.IndirectOffsetOnAxis(ap=pline[:, k, b:b + 1], axis=0))\
                    .then_inc(gat[n % 3], 16)

            pool_s = cache_kv_sel[0].rearrange("n (a r) c g d -> (n a) (r c g d)", r=ROWS)

            def gather(n):
                b, gg = n // 2, n % 2
                col = b * 8 + 4 * gg
                pool.indirect_dma_start(out=gring[0:SL, n % 3], out_offset=None, in_=pool_s,
                                        in_offset=bass.IndirectOffsetOnAxis(ap=line[:, col:col + 1], axis=0))\
                    .then_inc(gat[n % 3], 16)
                pool.dma_start(gring[SL:SK, n % 3, 0:256], sel_row[b:b + 1]).then_inc(gat[n % 3], 16)

            pool.wait_ge(line_ready, 1)
            pool.wait_ge(gat_used, 4 * DB)
            for n in range(3):
                gather(n)

            last = len(AT) - 1
            for a in range(last - 3, last + 1):
                read_out(pool, ("SC", a))
            pool.wait_ge(rows_saved, 64)
            for b in range(DB):
                pool.dma_start(nbuf[0:P - 1, b].rearrange("p r c -> p (r c)"),
                               bass.AP(cache_kv_win.tensor, (b * WIN + 1) * 256, [[1024, P - 1], [1, 1024]])).then_inc(nbuf_in, 16)
                pool.dma_start(nbuf[P - 1:P, b, 0:3].rearrange("p r c -> p (r c)"),
                               bass.AP(cache_kv_win.tensor, (b * WIN + WIN - 3) * 256, [[768, 1], [1, 768]])).then_inc(nbuf_in, 16)
                pool.dma_start(nbuf[P - 1:P, b, 3], win_row[b:b + 1]).then_inc(nbuf_in, 16)
            pool.wait_ge(nbuf_in, 16 * 3 * DB)
            for b in range(DB):
                pool.dma_start(s_kv_win[0, b].rearrange("(p r) c g d -> p (r c g d)", r=4),
                               nbuf[:, b].rearrange("p r c -> p (r c)")).then_inc(win_stored, 16)
            for n in range(3, 2 * DB):
                full(pool, ("gT", (n - 3) // 2, (n - 3) % 2))
                pool.wait_ge(vs_ready, n - 2)
                gather(n)

            full(pool, ("f1", NT))
            g.memset(qxz, 0.0).then_inc(qxz_zero, 1)
            for b in range(DB):
                if b >= 2:
                    full(pool, ("xT", b - 2))
                if b == 0:
                    full(pool, ("mn", 1))
                kv = cache_mem_kv[0, b].rearrange("(i p) c h d -> p i c (h d)", p=P)
                pool.dma_start(kst[:, b % 2], kv[:, :, 0]).then_inc(kst_in[b % 2], 16)
            full(pool, ("xq", XH - 1, 1))
            for b in range(DB):
                kv = cache_mem_kv[0, b].rearrange("(i p) c h d -> p i c (h d)", p=P)
                pool.dma_start(Vm[:, b], kv[:, :, 1]).then_inc(vm_in, 16)
            for c in range(4, 8):
                read_out(pool, ("mk", c))
            pool.dma_start(p_mem_kv[0, 0].rearrange("(i p) c h d -> p i (c h d)", p=P), mkv).then_inc(mkv_out, 16)

            for i in range(NT + 1):
                n = token_tile(i)[1]
                pool.wait_ge(out_ready, i + 1)
                dst = y_prompt[0, i * P:(i + 1) * P] if i < NT else y_sample[:, 0]
                pool.dma_start(dst, x1[0:n, i]).then_inc(stored, 16)
            pool.wait_ge(stored, 16 * (NT + 1))
            pool.wait_ge(mkv_out, 16)
            pool.wait_ge(win_stored, 16 * DB)
            pool.wait_ge(states_out, 64)
            pool.wait_ge(rows_saved, 64)
            pool.wait_ge(kv_stored[0], 16 * (2 * 4 + 2))
            pool.wait_ge(kv_stored[1], 16 * (2 * 4 + 2))

        @block.scalar
        def _(act):
            own = Own(act, act_own)
            a_ = nc.scalar

            def f(out, in_, func=ACT.Copy, **kw):
                return a_.activation(out, in_, func, **kw)

            ng = norm_g[0].rearrange("n (k p) -> (n k) p", p=P)
            act.dma_start(prow[0:48], ng).then_inc(params, 16)
            act.dma_start(prow[48:56], grp_norm_g[0].rearrange("(k p) -> k p", p=P)).then_inc(params, 16)
            act.dma_start(prow[56:64], mem_norm_g[0].rearrange("(k p) -> k p", p=P)).then_inc(params, 16)
            act.dma_start(prow[64:68], glu_b[0].rearrange("(k p) -> k p", p=P)).then_inc(params, 16)
            act.dma_start(prow[68:72], ssm_d[0].rearrange("(k p) -> k p", p=P)).then_inc(params, 16)
            act.dma_start(prow[72:88], ssm_a_re[0].rearrange("(j a) p -> j (a p)", a=2)).then_inc(params, 16)
            act.dma_start(prow[88:104], ssm_a_im[0].rearrange("(j a) p -> j (a p)", a=2)).then_inc(params, 16)
            act.dma_start(dt2[:, :], ssm_log_dt[0].rearrange("(j a) -> j a", a=2)).then_inc(params, 16)
            act.dma_start(drow[0:NPAIR].rearrange("j (l c) -> j l c", l=L4),
                          bass.AP(ssm_d.tensor, 0, [[32, NPAIR], [0, L4], [1, 32]])).then_inc(params, 16)
            with nc.allow_non_contiguous_dma(reason="a table of 32 by 8, transposed"):
                act.dma_start(tab[:, :], rel_bias.rearrange("b h -> h b")).then_inc(tab_in, 16)
            for n in range(4):
                for c in range(2):
                    act.dma_start(posP[32 * n:32 * n + 32, c * P:(c + 1) * P].rearrange("l (g d) -> l g d", g=2),
                                  bass.AP(cmp_pos.tensor, c * CB * HD, [[HD, CB], [0, NKV], [1, HD]])).then_inc(pos_in, 16)
            act.wait_ge(pblk_zero, 1)
            for c in range(2):
                for h in range(2):
                    act.dma_start(pblk[64 * h:64 * h + 64, c, 64 * h:64 * h + 64], cmp_proj[0, c]).then_inc(pos_in, 16)
            with nc.allow_non_contiguous_dma(reason="page numbers, one for each compressed block"):
                for b in range(DB):
                    act.dma_start(ptc[:, b:b + 1], bass.AP(page_table.tensor, b * NPAGE, [[1, NPAGE], [0, 4], [1, 1]])).then_inc(pt_in, 16)
            act.dma_start(ptrow[:, :], bass.AP(page_table.tensor, 0, [[NPAGE, DB], [0, NH], [1, NPAGE]])).then_inc(pt_in, 16)

            act.wait_ge(s5_arg, 1)
            f(prm[:, 0], cols[:, 104:120], ACT.Exp).then_inc(s5_fun, 1)
            act.wait_ge(s5_arg, 2)
            f(prm[:, 2], prm[:, 1], ACT.Exp).then_inc(s5_fun, 1)
            own.step(f(prm[:, 5], prm[:, 4], ACT.Sin))
            f(prm[:, 7], prm[:, 6], ACT.Sin).then_inc(s5_fun, 1)

            act.wait_ge(consts, 4)
            for i in range(NT + 1):
                n = token_tile(i)[1]
                act.wait_ge(x_in[i % 2], 16 * (i // 2 + 1))
                own.then(f(junk[0:n], xin[0:n, i % 2], ACT.Square, accum_out=st[0:n, i:i + 1]))
                f(st[0:n, 16 + i:17 + i], st[0:n, i:i + 1], ACT.Sqrt, scale=1.0 / D, bias=eps_c[0:n]).then_inc(rt_ready, 1)

            for i in range(NT + 1):
                n = token_tile(i)[1]
                full(act, ("kv", i))
                if i < NT:
                    if i >= 2:
                        u = i // 2
                        act.wait_ge(kv_stored[i % 2], 16 * (2 * u + max(0, u - 2)))
                        act.wait_ge(prod_ready, i - 1)
                        full(act, ("kT", i - 2))
                    dst = kvst[:, i % 2, 0:KVC]
                else:
                    dst = kvS[0:DB]
                f(dst, slot(("kv", i))[0:n, 0:KVC]).then_inc(kv_ready, 1)
                free(f(gates[0:n, i], slot(("kv", i))[0:n, KVC:KVC + NG], ACT.Sigmoid), ("kv", i))
                if i >= 1:
                    kt = i - 1
                    key = ("kT", kt)
                    full(act, key)
                    s = slot(key)[:, 0:256].rearrange("p (a t) -> p a t", a=2)
                    for half in range(2):
                        for g in range(NKV):
                            own.step(f(kTd[64 * half:64 * half + 64, g::NKV, kt * P:(kt + 1) * P], s[64 * g:64 * g + 64]))
                    free(f(csum[:, :, 4 * kt:4 * kt + 4], slot(key)[:, 256:264].rearrange("p (a t) -> p a t", a=2)), key)
            full(act, "cproj")
            for half in range(2):
                for g in range(NKV):
                    own.step(f(kcT[64 * half:64 * half + 64, g], slot("cproj")[64 * g:64 * g + 64, 0:32]))
            free(f(vc[:, :], slot("cproj")[0:32, 32:32 + P]), "cproj")

            def dense_out(stage, m, dst):
                for c in range(2):
                    key = (stage, m, c)
                    full(act, key)
                    if c == 0:
                        ins = f(dst[:, 0:2 * CH].rearrange("p (a n) -> p a n", a=2), chunked(key))
                    else:
                        ins = f(dst[:, 2 * CH:TC], chunked(key)[:, 0])
                    free(ins, key)

            for m in range(8):
                if m >= 6:
                    act.wait_ge(uT_ready, m - 5)
                dense_out("in", m, qT[:, m] if m < 4 else uTm[:, m % 2])

            full(act, ("in", 7, 1))
            own.settle()
            f(kH, kTd).then_inc(k_hi, 1)

            with nc.allow_non_contiguous_dma(reason="rows of 16 numbers"):
                for part, src in enumerate((ssm_b_re, ssm_b_im)):
                    act.dma_start(braw[:, part], src[0].rearrange("(j a) p i -> (a p) j i", a=2)).then_inc(b_in, 16)
            for part, src in enumerate((ssm_c_re, ssm_c_im)):
                act.dma_start(craw[:, 4 * part:4 * part + 4],
                              src[0].rearrange("(q g) i p -> (g i) q p", g=8)).then_inc(c_in, 16)
            for part, src in enumerate((state_ssm_re, state_ssm_im)):
                act.dma_start(h0row[0:DB, part], src[0].rearrange("b g p -> b (g p)")).then_inc(c_in, 16)
            full(act, "C")
            for half in range(2):
                for part in range(2):
                    s = slot("C")[0:HD, part * 512:part * 512 + 512]\
                        .rearrange("p (q g i) -> p q g i", g=2, i=16)[:, :, half]
                    ins = f(cc[64 * half:64 * half + 64, part], s)
                    free(ins, "C") if half and part else own.step(ins)
            full(act, "h0")
            free(f(h0T.rearrange("p a j b -> p (a j b)"), slot("h0")[:, 0:2 * NPAIR * DB]), "h0")

            def s5_out(j):
                key = ("SA", j)
                full(act, key)
                if j >= 2:
                    full(act, ("SB", j - 2))
                s = slot(key)
                own.step(f(Wm[j % 2].rearrange("p a c -> p (a c)"), s[:, 0:256]))
                for l in range(L4):
                    ins = f(Tm[j % 2][32 * l:32 * l + 32, 32 * l:P], s[32 * l:32 * l + 32, 512 + 32 * l:640])
                    free(ins, key) if l == L4 - 1 else own.step(ins)

            for j in range(NPAIR):
                s5_out(j)

            full(act, "st")
            own.step(f(st_rows[0:32], slot("st")[0:32, 0:P]))
            free(f(tinyf[0:32, 8:9], slot("st")[0:32, 0:1]), "st")
            act.wait_ge(own.sem, own.n)
            act.sem_inc(states_staged, 1)
            for q_ in range(4):
                key = ("sst", q_)
                full(act, key)
                free(f(sst_rows[0:DB, q_ * D:(q_ + 1) * D], slot(key)[0:DB]), key)
            for q_ in range(4):
                read_out(act, ("sst", q_))
            act.sem_inc(states_staged, 1)

            for h in range(NH):
                full(act, ("bt", h))
                free(f(BT[:, h], slot(("bt", h))), ("bt", h))

            def softmax_rows(n, src_ready, stat, x, s, scale=SC):
                act.wait_ge(src_ready, n)
                f(x, x, ACT.Exp, bias=st[0:s, 33:34], scale=scale, accum_out=st[0:s, 34:35]).then_inc(stat, 1)

            def compressed_branch(key):
                if key[0] == "sT":
                    b = key[1]
                    full(act, key)
                    if b >= 2:
                        full(act, ("sP", b - 2))
                    free(f(sTm[b % 2].rearrange("p a c -> p (a c)"), slot(key)[:, 0:256]), key)
                elif key[0] == "sP":
                    b = key[1]
                    full(act, key)
                    own.step(f(kcTs[:, b], slot(key)[:, 0:P]))
                    free(f(vcs[:, b], slot(key)[:, P:2 * P]), key)
                elif key == "sps":
                    softmax_rows(1, pw_raw, pw_exp, Pc[0:64], 64)
                elif key == "scT":
                    full(act, key)
                    free(f(PcT, slot(key)[:, 0:64]), key)
                elif key == "sov":
                    full(act, key)
                    free(f(osT[:, 0], slot(key)[:, 0:64]), key)
                elif key == "ix1":
                    full(act, key)
                    free(f(p15[0:SLOTS], slot(key)[0:SLOTS, 0:64]), key)

            act.wait_ge(states_out, 64)
            n_at = len(AT)
            def queries_hi(u):
                i, h = u // NH, u % NH
                lo = 64 * (h % 2)
                if u >= QS:
                    full(act, ("SC", 3 * (u - QS) + 2))
                f(qS[lo:lo + 64, u % QS], qT[lo:lo + 64, h // 2, i * P:(i + 1) * P]).then_inc(q_hi, 1)

            for u in range(2):
                queries_hi(u)
            for a in range(n_at + AHEAD + 1):
                if a % 3 == 0 and a // 3 + 2 < NT * NH:
                    queries_hi(a // 3 + 2)
                if a < n_at:
                    i, _, br, _, nk = AT[a]
                    r = a % 8 + (40 if br == 2 and i >= 4 else 0)
                    read_out(act, ("SC", a))
                    f(Pm[:, a % NPM, 0:nk], Pm[:, a % NPM, 0:nk], ACT.Exp, bias=st[:, r:r + 1], scale=-1.0,
                      accum_out=st[:, 16 + a % 8:17 + a % 8]).then_inc(exp_ready, 1)
                t = a - AHEAD
                if 0 <= t < n_at:
                    key, nk = ("TR", t), AT[t][4]
                    full(act, key)
                    if t >= 2:
                        full(act, ("PV", t - 2))
                    rows, w = (nk, P) if nk < P else (P, nk)
                    free(f(PT[0:rows, t % 2, 0:w], slot(key)[0:rows, 0:w]), key)
                for key in BETWEEN.get(a, []):
                    compressed_branch(key)

            for b in range(DB):
                full(act, ("wT", b))
                free(f(kTw[:, b], slot(("wT", b))[:, 0:512]), ("wT", b))
            softmax_rows(2, pw_raw, pw_exp, Pw[0:64], 64)
            full(act, "wP")
            free(f(PTw.rearrange("p a c -> p (a c)"), slot("wP")[:, 0:256]), "wP")
            full(act, "wO")
            free(f(osT[:, 2], slot("wO")[:, 0:64]), "wO")
            for n in range(2 * DB):
                b, g = n // 2, n % 2
                key = ("gT", b, g)
                full(act, key)
                s = slot(key)[0:HD].rearrange("p (a x) -> p a x", a=2)[:, :, 0:4 * SK]
                free(f(kTs[64 * g:64 * g + 64, b].rearrange("p (a r) c -> p a (r c)", a=2), s), key)
            softmax_rows(3, pw_raw, pw_exp, Ps[0:64].rearrange("p a c -> p (a c)"), 64)
            full(act, "gP")
            free(f(PTs[0:SK].rearrange("p a c -> p (a c)"), slot("gP")[0:SK, 0:512]), "gP")
            full(act, "gO")
            free(f(osT[:, 1], slot("gO")[:, 0:64]), "gO")

            act.wait_ge(y_ready, 1)
            f(yF, yF, ACT.Gelu_apprx_tanh).then_inc(gelu_ready, 1)
            for m in range(4):
                for c in range(2):
                    key = ("glu", m, c)
                    full(act, key)
                    if c == 0:
                        ins = f(oF[:, m, 0:2 * CH].rearrange("p (a n) -> p a n", a=2), chunked(key), ACT.Sigmoid,
                                bias=cols[:, 64 + m:65 + m])
                    else:
                        ins = f(oF[:, m, 2 * CH:TC], chunked(key)[:, 0], ACT.Sigmoid, bias=cols[:, 64 + m:65 + m])
                    free(ins, key)
            act.wait_ge(oF_ready, 1)
            f(SQ, oF, ACT.Square).then_inc(sq_ready, 1)
            for c in range(2):
                key = ("ss", c)
                full(act, key)
                if c == 0:
                    ins = f(RS[:, 0:2 * CH].rearrange("p (a n) -> p a n", a=2), chunked(key), ACT.Sqrt,
                            scale=1.0 / 512, bias=eps_c[:, :])
                else:
                    ins = f(RS[:, 2 * CH:TC], chunked(key)[:, 0], ACT.Sqrt, scale=1.0 / 512, bias=eps_c[:, :])
                free(ins, key)
            act.wait_ge(oS_ready, 1)
            for i in range(NT + 1):
                n = token_tile(i)[1]
                src = oN[:, i] if i < NT else oS[0:DB, 0]
                own.then(f(scr[0:n], src, ACT.Square, accum_out=st[0:n, i:i + 1]))
                f(st[0:n, 16 + i:17 + i], st[0:n, i:i + 1], ACT.Sqrt, scale=1.0 / 512, bias=eps_c[0:n]).then_inc(on_stat, 1)

            for i in range(NT + 1):
                c0, n = token_tile(i)
                src = x_prompt[0, c0:c0 + n] if i < NT else x_sample[:, 0]
                act.dma_start(x1[0:n, i], src).then_inc(x1_in, 16)

            def input_hi(i):
                c0, r = token_tile(i)
                read_out(act, ("f2", i))
                f(hH[:, :, c0:c0 + r], hRaw[:, :, c0:c0 + r]).then_inc(h_hi, 1)

            def residual(n):
                for m in range(8 if n < 3 else 0):
                    if m == 0 and n == 1:
                        act.wait_ge(m_ready, 2)
                    dense_out({1: "wo", 2: "xo"}[n], m, yT[:, m])
                if n == 3:
                    full(act, ("wf", NGRP - 1, 7, 1))
                if n == 1:
                    act.wait_ge(m_ready, 2)
                if n > 1:
                    act.wait_ge(res_sum, (n - 1) * (NT + 1))
                act.dma_start(grow, bass.AP(norm_g.tensor, (2 * n - 1) * D, [[0, P], [1, D]])).then_inc(grow_in, 16)
                base = (n - 1) * (NT + 1)

                def first(i):
                    r = token_tile(i)[1]
                    full(act, (f"b{n}", i))
                    if n < 3 and i >= 2:
                        full(act, (f"f{n}", i - 2))
                    if n == 3 and i >= 2:
                        act.wait_ge(out_ready, i - 1)
                    own.then(f(tb[0:r, i % 2], slot((f"b{n}", i))[0:r], ACT.Square, accum_out=st[0:r, i:i + 1]))
                    f(st[0:r, 16 + i:17 + i], st[0:r, i:i + 1], ACT.Sqrt, scale=1.0 / D, bias=eps_c[0:r]).then_inc(res_stat, 1)

                first(0)
                for i in range(NT + 1):
                    if i < NT:
                        first(i + 1)
                    if n < 3:
                        r = token_tile(i)[1]
                        act.wait_ge(res_sum, base + i + 1)
                        own.then(f(tb[0:r, i % 2], x1[0:r, i], ACT.Square, accum_out=st[0:r, 32 + i:33 + i]))
                        f(st[0:r, 48 + i:49 + i], st[0:r, 32 + i:33 + i], ACT.Sqrt, scale=1.0 / D,
                          bias=eps_c[0:r]).then_inc(res_stat2, 1)
                    if n == 2 and i >= 1:
                        input_hi(i - 1)
                if n == 2:
                    input_hi(NT)

            residual(1)

            act.dma_start(mrow, mem_prompt[0].rearrange("(i p) d -> p i d", p=P)).then_inc(mem_in, 16)
            act.wait_ge(mem_in, 16)
            for i in range(2):
                own.then(f(junk2, mrow[:, i], ACT.Square, accum_out=st[:, i:i + 1]))
                f(st[:, 16 + i:17 + i], st[:, i:i + 1], ACT.Sqrt, scale=1.0 / D, bias=eps_c[:, :]).then_inc(mem_stat, 1)
            for c in range(8):
                full(act, ("mk", c))
                free(f(mkv[:, :, c * P:(c + 1) * P], slot(("mk", c))[:, 0:256].rearrange("p (i n) -> p i n", i=2)), ("mk", c))
            full(act, "mT")
            free(f(mkT.rearrange("p h n -> p (h n)"), slot("mT")), "mT")
            for m in range(4):
                dense_out("xq", m, q2T[:, m])
            for b in range(DB):
                full(act, ("xT", b))
                free(f(kTm[:, b].rearrange("p h n -> p (h n)"), slot(("xT", b))), ("xT", b))
            act.wait_ge(px_raw, 1)
            free(f(Pxs[0:32], slot("xS")[0:32, 0:NM], ACT.Exp, bias=st[0:32, 33:34], scale=XSC,
                   accum_out=st[0:32, 34:35]), "xS")
            full(act, "xP")
            free(f(PTxs.rearrange("p a c -> p (a c)"), slot("xP")[:, 0:64]), "xP")
            for i in range(NT + 1):
                if i < NT:
                    act.wait_ge(px_raw, i + 2)
                    if i >= 2:
                        full(act, ("XT", i - 2))
                    b0 = 8 * (i % 2)
                    for h in range(XH):
                        ins = f(Px[:, i % 2, h * NM:(h + 1) * NM], slot(("XS", i))[:, h * NM:(h + 1) * NM], ACT.Exp,
                                bias=st[:, b0 + h:b0 + h + 1], scale=XSC, accum_out=st[:, 16 + b0 + h:17 + b0 + h])
                        free(ins, ("XS", i)) if h == XH - 1 else own.step(ins)
                if i >= 1:
                    full(act, ("XT", i - 1))
                    if i >= 3:
                        full(act, ("XO", i - 3))
                    free(f(PTx[:, (i - 1) % 2], slot(("XT", i - 1))), ("XT", i - 1))
            residual(2)

            act.wait_ge(mkv_out, 16)
            def weights_hi(it):
                n = first_ffn + it
                act.wait_ge(w_loaded[n % NS], 16 * (n // NS + 1))
                if it >= 2:
                    full(act, last_unit(ffn[it - 2]))
                size = group_size(ffn[it])
                f(wH[it % 2][:, 0:size], wRaw[:, n % NS, 0:size]).then_inc(w_hi, 1)

            weights_hi(0)
            for it, item in enumerate(ffn):
                if it + 1 < FFN_ITEMS:
                    weights_hi(it + 1)
                n = item[1] % FG
                if item[0] == "g":
                    full(act, item + (0,))
                    free(f(gRaw[:, n, 0:2 * CH].rearrange("p (a n) -> p a n", a=2), chunked(item + (0,)), ACT.Silu),
                         item + (0,))
                    full(act, item + (1,))
                    free(f(gRaw[:, n, 2 * CH:TC], chunked(item + (1,))[:, 0], ACT.Silu), item + (1,))
                elif item[0] == "u":
                    act.wait_ge(g_prod, item[1] + 1)
                    f(gH[:, n], gRaw[:, n]).then_inc(g_hi, 1)
            residual(3)

        @block.vector
        def _(dve):
            own = Own(dve, dve_own)
            v = nc.vector

            def tt(out, a, b, op=ALU.mult):
                return v.tensor_tensor(out, a, b, op)

            def cmul(out_re, out_im, a, b, t, neg_im=False):
                own.step(tt(t[0], a[0], b[0]))
                own.step(tt(t[1], a[1], b[1]))
                own.step(tt(t[2], a[0], b[1]))
                own.step(tt(t[3], a[1], b[0]))
                own.settle()
                for o in out_re:
                    own.step(tt(o[0], o[1](t[0]), o[1](t[1]), ALU.subtract))
                for o in out_im:
                    if neg_im:
                        own.step(v.scalar_tensor_tensor(o[0], o[1](t[2]), -1.0, o[1](t[3]), ALU.mult, ALU.subtract))
                    else:
                        own.step(tt(o[0], o[1](t[2]), o[1](t[3]), ALU.add))
                own.settle()

            def whole(o):
                return [(o, lambda x: x)]

            def bcast(col, shape, axis=-1):
                return col.unsqueeze(axis).to_broadcast(shape)

            full(dve, "par")
            own.step(v.tensor_copy(cols[:, :], slot("par")[:, 0:120]))
            free(v.tensor_copy(d_rows[:, :], slot("par")[:, 128:128 + NPAIR]), "par")
            read_out(dve, "par")
            v.tensor_copy(jota[:, :], jota_i[:, :]).then_inc(s5_arg, 1)
            dve.wait_ge(s5_fun, 1)
            a_re, a_im, dt = cols[:, 72:88], cols[:, 88:104], prm[:, 0]
            own.step(tt(prm[:, 1], a_re, dt))
            own.then(tt(prm[:, 8], a_im, dt))
            TWO_PI = [6.28125, 0.0019350051879882812, 3.0199159819567e-07]
            for shift, dst in ((0.0, 4), (0.25, 6)):
                own.then(v.tensor_scalar(prm[:, 9], prm[:, 8], 1.0 / (2 * pi), shift, ALU.mult, ALU.add))
                own.then(v.tensor_scalar(prm[:, 9], prm[:, 9], 12582912.0, None, ALU.add))
                own.then(v.tensor_scalar(prm[:, 9], prm[:, 9], -12582912.0, None, ALU.add))
                own.then(v.scalar_tensor_tensor(prm[:, dst], prm[:, 9], -TWO_PI[0], prm[:, 8], ALU.mult, ALU.add))
                own.then(v.scalar_tensor_tensor(prm[:, dst], prm[:, 9], -TWO_PI[1], prm[:, dst], ALU.mult, ALU.add))
                own.then(v.scalar_tensor_tensor(prm[:, dst], prm[:, 9], -TWO_PI[2], prm[:, dst], ALU.mult, ALU.add))
                if shift:
                    own.then(v.tensor_scalar(prm[:, dst], prm[:, dst], pi / 2, None, ALU.add))
                own.then(v.tensor_scalar(prm[:, dst], prm[:, dst], 3.1415925, -3.1415925, ALU.min, ALU.max))
            dve.sem_inc(s5_arg, 1)
            dve.wait_ge(s5_fun, 3)
            ab = apow[:, 1]
            own.step(tt(ab[:, 0], prm[:, 2], prm[:, 7]))
            own.step(tt(ab[:, 1], prm[:, 2], prm[:, 5]))
            own.step(v.memset(apow[:, 0, 0], 1.0))
            own.step(v.memset(apow[:, 0, 1], 0.0))
            own.step(tt(prm[:, 9], a_re, a_re))
            own.step(tt(prm[:, 10], a_im, a_im))
            own.settle()
            own.step(tt(prm[:, 9], prm[:, 9], prm[:, 10], ALU.add))
            own.step(v.tensor_scalar(prm[:, 11], ab[:, 0], -1.0, None, ALU.add))
            own.settle()
            own.step(v.reciprocal(prm[:, 9], prm[:, 9]))
            own.step(tt(prm[:, 12], prm[:, 11], a_re))
            own.step(tt(prm[:, 13], ab[:, 1], a_im))
            own.step(tt(prm[:, 14], ab[:, 1], a_re))
            own.step(tt(prm[:, 15], prm[:, 11], a_im))
            own.settle()
            own.step(tt(prm[:, 12], prm[:, 12], prm[:, 13], ALU.add))
            own.step(tt(prm[:, 14], prm[:, 14], prm[:, 15], ALU.subtract))
            own.settle()
            own.step(tt(co[:, 0], prm[:, 12], prm[:, 9]))
            own.step(tt(co[:, 1], prm[:, 14], prm[:, 9]))
            own.settle()
            sm = [prm[:, 12 + n] for n in range(4)]
            for k in range(2, 5):
                cmul(whole(apow[:, k, 0]), whole(apow[:, k, 1]), (apow[:, k - 1, 0], apow[:, k - 1, 1]),
                     (ab[:, 0], ab[:, 1]), sm)

            dve.wait_ge(pt_in, 16 * (DB + 1))
            own.step(v.tensor_copy(tinyf[:, 0:1], tiny[:, 0:1]))
            own.step(v.tensor_single_scalar(tiny[:, 1:2], tiny[:, 0:1], 3, ALU.bitwise_and))
            own.step(v.tensor_single_scalar(tiny[:, 2:3], tiny[:, 0:1], 7, ALU.bitwise_and))
            own.settle()
            own.step(v.tensor_copy(tinyf[:, 1:2], tiny[:, 1:2]))
            own.step(v.tensor_copy(tinyf[:, 2:3], tiny[:, 2:3]))
            own.settle()
            own.step(v.tensor_scalar(tinyf[:, 3:4], tinyf[:, 1:2], 4.0, None, ALU.mult))
            own.settle()
            for k in range(4):
                own.step(v.tensor_scalar(tinyf[:, 4 + k:5 + k], tinyf[:, 3:4], float(k), None, ALU.add))
            own.settle()
            for k in range(4):
                ins = v.tensor_scalar(pline[:, k], ptc[:, :], 16.0, tinyf[:, 4 + k:5 + k], ALU.mult, ALU.add)
                own.step(ins) if k < 3 else ins.then_inc(pline_ready, 1)

            for i in range(NT + 1):
                n = token_tile(i)[1]
                c0 = token_tile(i)[0]
                dve.wait_ge(rt_ready, i + 1)
                own.then(v.reciprocal(st[0:n, 32 + i:33 + i], st[0:n, 16 + i:17 + i]))
                v.tensor_scalar(xin[0:n, i % 2], xin[0:n, i % 2], st[0:n, 32 + i:33 + i], None, ALU.mult).then_inc(xn_ready, 1)
                full(dve, ("n1", i))
                s = slot(("n1", i)).rearrange("p (k t) -> p k t", k=KD)[:, :, 0:n]
                free(tt(hT[:, :, c0:c0 + n], s, bcast(cols[:, 0:8], [P, KD, n])), ("n1", i))

            dve.wait_ge(pos_in, 16 * 12)
            for i in range(NT):
                dve.wait_ge(kv_ready, i + 1)
                own.step(v.tensor_copy(vkeep[:, i].rearrange("p (a c) -> p a c", a=2),
                                       kvst[:, i % 2, 256:768].rearrange("p (a b c) -> p a b c", a=2, b=2)[:, :, 1]))
                if i >= 2:
                    full(dve, ("kT", i - 2))
                tt(cprod[:, i % 2], kvst[:, i % 2, 0:256], posP).then_inc(prod_ready, 1)

            dve.wait_ge(kv_stored[0], 16 * (2 * 4 + 2))
            dve.wait_ge(kv_stored[1], 16 * (2 * 4 + 2))
            for m in range(4):
                for c in range(2):
                    read_out(dve, ("in", 4 + m, c))
                for q_ in range(4):
                    src = uTm[32 * q_:32 * q_ + 32, m % 2]
                    for l in range(L4):
                        own.step(v.tensor_copy(U2[32 * l:32 * l + 32, 4 * m + q_], src[:, l:T:L4]))
                    own.step(v.tensor_copy(us3[96:P, 4 * m + q_], src[:, T:TC]))
                own.settle()
                v.tensor_copy(uS[:, m], uTm[:, m % 2, T:TC]).then_inc(uT_ready, 1)
            for h in range(NH):
                g = h // GQ
                lo = 64 * (h % 2)
                ins = v.tensor_copy(qz[64 * g:64 * g + 64].rearrange("p b c -> p (b c)")[:, h::72],
                                    qT[lo:lo + 64, h // 2, T:TC])
                own.step(ins) if h < NH - 1 else ins.then_inc(qz_ready, 1)
            dve.wait_ge(uT_ready, 4)
            dve.sem_inc(u_moved, 1)

            dve.wait_ge(b_in, 32)
            dve.wait_ge(rows_saved, 64)
            own.step(v.memset(WT, 0.0))
            own.step(v.memset(CP, 0.0))
            own.step(v.memset(Tm[0], 0.0))
            own.step(v.memset(Tm[1], 0.0))
            sh = [P, NPAIR, 16]
            qq = [q[:, n] for n in range(4)]
            cmul(whole(bb[:, 0]), whole(bb[:, 1]), (bcast(co[:, 0], sh), bcast(co[:, 1], sh)),
                 (braw[:, 0], braw[:, 1]), qq)

            def halves(dst):
                return [(dst(g)[64 * g:64 * g + 64], lambda x, g=g: x[64 * g:64 * g + 64]) for g in range(2)]

            for l in range(L4):
                pw = apow[:, L4 - 1 - l]
                cmul(halves(lambda g: WT[:, 0, :, 32 * l + 16 * g:32 * l + 16 * g + 16]),
                     halves(lambda g: WT[:, 1, :, 32 * l + 16 * g:32 * l + 16 * g + 16]),
                     (bcast(pw[:, 0], sh), bcast(pw[:, 1], sh)), (bb[:, 0], bb[:, 1]), qq)
            read_out(dve, "C")
            for k in range(5):
                pw = apow[:, k]
                cmul(halves(lambda g: CP[:, 0, :, k, 16 * g:16 * g + 16]),
                     halves(lambda g: CP[:, 1, :, k, 16 * g:16 * g + 16]),
                     (bcast(pw[:, 0], sh), bcast(pw[:, 1], sh)), (cc[:, 0], cc[:, 1]), qq, neg_im=True)
            read_out(dve, "h0")
            dve.sem_inc(s5_built, 1)
            own.then(v.memset(H[:, 0], 0.0))

            for j in range(NPAIR):
                key = ("SB", j)
                full(dve, key)
                s = slot(key)
                own.step(v.tensor_copy(H[:, 1:NC + 1, :, j].rearrange("p c a -> p a c"),
                                       s[:, 0:512].rearrange("p (a c) -> p a c", a=2)))
                own.step(v.tensor_copy(hs[:, :, j], s[:, 512:528].rearrange("p (a b) -> p a b", a=2)))
                free(v.scalar_tensor_tensor(U2[:, j], U2[:, j], d_rows[:, j:j + 1], s[:, 528:528 + NC],
                                            ALU.mult, ALU.add), key)
            read_out(dve, ("SB", NPAIR - 1))
            own.settle()

            sm2 = [r1[:, n, 0, 0:NPAIR] for n in range(4)]
            apw_ = lambda n: (apw[:, n, 0], apw[:, n, 1])
            own.step(v.tensor_copy(apw[:, 0], apow[:, 4]))
            own.settle()
            for n in range(1, 15):
                cmul(whole(apw[:, n, 0]), whole(apw[:, n, 1]), apw_(n - 1), (apow[:, 4, 0], apow[:, 4, 1]), sm2)
            cmul(whole(apow[:, 5, 0]), whole(apow[:, 5, 1]), apw_(14), (apow[:, 4, 0], apow[:, 4, 1]), sm2)
            Hm = H[:, 1:NC + 1].rearrange("p (m n) a j -> p m n a j", n=16)

            for n, power in enumerate([(apow[:, 4, 0], apow[:, 4, 1]), (apow[:, 5, 0], apow[:, 5, 1])]
                                      + [apw_(n) for n in range(15)]):
                own.step(v.tensor_copy(turn[:, n, 0, 0], power[0]))
                own.step(v.tensor_copy(turn[:, n, 1, 1], power[0]))
                own.step(v.tensor_copy(turn[:, n, 1, 0], power[1]))
                own.step(v.tensor_scalar(turn[:, n, 0, 1], power[1], -1.0, None, ALU.mult))
            own.settle()

            def advance(dst, src, n, m):
                shape = [P, m, 2, 2 * NPAIR]
                mat = turn[:, n].rearrange("p a b j -> p a (b j)").unsqueeze(1).to_broadcast(shape)
                own.then(tt(r1[:, 0:m],
                            src.rearrange("p m b j -> p m (b j)").unsqueeze(2).to_broadcast(shape), mat))
                own.then(tt(dst, dst, r1[:, 0:m, :, 0:NPAIR], ALU.add))
                own.then(tt(dst, dst, r1[:, 0:m, :, NPAIR:], ALU.add))

            for n in range(1, 16):
                advance(Hm[:, :, n], Hm[:, :, n - 1], 0, 16)
            for m in range(1, 16):
                advance(Hm[:, m:m + 1, 15], Hm[:, m - 1:m, 15], 1, 1)
            for n in range(15):
                advance(Hm[:, 1:16, n], Hm[:, 0:15, 15], 2 + n, 15)
            sb4 = [P, NPAIR, DB]
            t = [r1[:, 2 * n:2 * n + 2].rearrange("p m a j -> p (m a j)").rearrange("p (j b) -> p j b", b=DB)
                 for n in range(4)]
            abr, abi = bcast(ab[:, 0], sb4), bcast(ab[:, 1], sb4)
            own.step(tt(t[0], h0T[:, 0], abr))
            own.step(tt(t[1], h0T[:, 1], abi))
            own.step(tt(t[2], h0T[:, 1], abr))
            own.step(tt(t[3], h0T[:, 0], abi))
            own.settle()
            own.step(tt(t[0], t[0], t[1], ALU.subtract))
            own.step(tt(t[2], t[2], t[3], ALU.add))
            own.settle()
            own.step(tt(hs[:, 0], hs[:, 0], t[0], ALU.add))
            own.step(tt(hs[:, 1], hs[:, 1], t[2], ALU.add))
            own.settle()
            dve.sem_inc(s5_states, 1)
            dve.sem_inc(hs_ready, 1)

            for j in range(NPAIR):
                key = ("V", j)
                full(dve, key)
                q_, m = j % 4, j // 4
                for l in range(L4):
                    ins = tt(yF[32 * q_:32 * q_ + 32, m, l:T:L4], slot(key)[32 * l:32 * l + 32, 0:NC],
                             U2[32 * l:32 * l + 32, j], ALU.add)
                    free(ins, key) if l == L4 - 1 else own.step(ins)
            full(dve, "ys")
            for m in range(4):
                ins = v.scalar_tensor_tensor(yF[:, m, T:TC], uS[:, m], cols[:, 68 + m:69 + m],
                                             slot("ys")[:, m * DB:(m + 1) * DB], ALU.mult, ALU.add)
                free(ins, "ys") if m == 3 else own.step(ins)
            read_out(dve, "ys")
            dve.sem_inc(y_ready, 1)

            def softmax_in(out, x, bias, release=None):
                ins = v.tensor_tensor_reduce(out=out, in0=x, in1=bias, scale=1.0, scalar=FLOOR, op0=ALU.add,
                                             op1=ALU.max, accum_out=st[0:64, 32:33])
                if release:
                    free(ins, release)
                    read_out(dve, release)
                v.tensor_scalar(st[0:64, 33:34], st[0:64, 32:33], -SC, None, ALU.mult).then_inc(pw_raw, 1)

            def softmax_out(n, x):
                dve.wait_ge(pw_exp, n)
                own.then(v.tensor_scalar(st[0:64, 35:36], st[0:64, 34:35], TINY, None, ALU.max))
                own.then(v.reciprocal(st[0:64, 36:37], st[0:64, 35:36]))
                return v.tensor_scalar(x, x, st[0:64, 36:37], None, ALU.mult)

            def sum_lines(n, part):
                k, b = n // DB, n % DB
                r = gring[:, n % 3].rearrange("p (r c g d) -> p (r c) g d", r=ROWS, c=2, g=2)
                flat = gring[:, n % 3]
                if part == 0:
                    dve.wait_ge(gat[n % 3], 16 * (n // 3 + 1))
                    if b == 0:
                        dve.wait_ge(posB_in, 32 * (k + 1))
                    own.step(tt(r, r, posB.rearrange("p r (c d) -> p (r c) d", c=2).unsqueeze(2)
                                .to_broadcast([P, 2 * ROWS, NKV, HD])))
                elif part < 3:
                    half = 2048 >> part
                    own.settle()
                    own.step(tt(flat[:, 0:half], flat[:, 0:half], flat[:, half:2 * half], ALU.add))
                else:
                    own.settle()
                    if k == 0:
                        tt(summ[:, b], flat[:, 0:256], flat[:, 256:512], ALU.add).then_inc(gat_used, 1)
                    else:
                        own.then(tt(flat[:, 0:256], flat[:, 0:256], flat[:, 256:512], ALU.add))
                        tt(summ[:, b], summ[:, b], flat[:, 0:256], ALU.add).then_inc(gat_used, 1)
                    if k == 3:
                        dve.wait_ge(gat_used, n + 1)
                        dve.sem_inc(summ_ready, 1)

            def compressed_branch(key):
                if key == "sc":
                    full(dve, key)
                    dve.wait_ge(V64_in, 16)
                    own.step(v.tensor_copy(cbias[0:64, 0:112], V64[:, 0:1].to_broadcast([64, 112])))
                    own.step(v.tensor_copy(cbias[0:64, 112:P], V64[:, 31::CB][:, 0:16]))
                    own.settle()

                    softmax_in(Pc[0:64], slot("sc")[0:64, 0:P], cbias[0:64], "sc")
                elif key == "sps":
                    softmax_out(1, Pc[0:64]).then_inc(pc_ready, 1)
                    full(dve, "sps")
                    free(v.tensor_reduce(score[0:64], slot("sps")[0:64, 0:P].rearrange("p (j a) -> p j a", a=2), X, ALU.add), "sps")
                    read_out(dve, "sps")
                    own.step(v.memset(score[0:64, 0:1], -1.0))
                    own.then(v.memset(score[0:64, NSB - 1:NSB], -1.0))
                    own.then(v.max(top[0:64, 0:8], score[0:64]))
                    own.step(v.max_index(topi[0:64, 0:8], top[0:64, 0:8], score[0:64]))
                    own.step(v.match_replace(out=score2[0:64], in_to_replace=top[0:64, 0:8], in_values=score[0:64], imm_value=-1.0))
                    own.settle()
                    own.then(v.max(top[0:64, 8:16], score2[0:64]))
                    own.then(v.max_index(topi[0:64, 8:16], top[0:64, 8:16], score2[0:64]))
                    own.then(v.tensor_copy(pick[0:64], topi[0:64]))
                    own.step(v.memset(pick[0:64, PICK:PICK + 1], 0.0))
                    own.step(v.memset(pick[0:64, PICK + 1:PICK + 2], float(NSB - 1)))
                    own.step(v.tensor_scalar(jphys[0:64].rearrange("p (j a) -> p j a", a=2)[:, :, 0], ptrow[:, :], 2.0, None, ALU.mult))
                    own.step(v.tensor_scalar(jphys[0:64].rearrange("p (j a) -> p j a", a=2)[:, :, 1], ptrow[:, :], 2.0, 1.0, ALU.mult, ALU.add))
                    own.settle()
                    s3 = [64, SLOTS, 64]
                    own.step(tt(onehot[0:64], bcast(pick[0:64, 0:SLOTS], s3), jota[:, :].unsqueeze(1).to_broadcast(s3), ALU.is_equal))
                    own.step(v.tensor_scalar(is62[0:64, 0:PICK], pick[0:64, 0:PICK], float(NSB - 2), None, ALU.is_equal))
                    own.settle()
                    own.then(tt(onehot[0:64], onehot[0:64], jphys[0:64].unsqueeze(1).to_broadcast(s3)))
                    v.tensor_reduce(phys[0:64, 0:SLOTS], onehot[0:64], X, ALU.add).then_inc(phys_ready, 1)
                elif key == "ix2":
                    full(dve, "ix2")
                    free(v.tensor_scalar(line[:, :], slot("ix2")[0:SL, 0:64], 8.0, tinyf[0:SL, 2:3], ALU.mult, ALU.add), "ix2")
                    read_out(dve, "ix2")
                    dve.sem_inc(line_ready, 1)

            dve.wait_ge(far_ready, NH)
            n_at = len(AT)
            def queries_lo(u):
                i, h = u // NH, u % NH
                lo = 64 * (h % 2)
                dve.wait_ge(q_hi, u + 1)
                tt(qS[64 - lo:128 - lo, u % QS], qT[lo:lo + 64, h // 2, i * P:(i + 1) * P], qS[lo:lo + 64, u % QS],
                   ALU.subtract).then_inc(q_lo, 1)

            for u in range(2):
                queries_lo(u)
            for a in range(n_at + AHEAD + 1):
                if a % 3 == 0 and a // 3 + 2 < NT * NH:
                    queries_lo(a // 3 + 2)
                t = a - AHEAD - 1
                if t + 1 >= 0 and t + 1 < n_at:
                    rn = (t + 1) % 8
                    dve.wait_ge(exp_ready, t + 2)
                    own.step(v.tensor_scalar(st[:, 24 + rn:25 + rn], st[:, 16 + rn:17 + rn], TINY, None, ALU.max))
                if a < n_at:
                    i, h, br, k0, nk = AT[a]
                    r = a % 8
                    key = ("SC", a)
                    s = slot(key)
                    full(dve, key)
                    if a >= NPM:
                        full(dve, ("TR", a - NPM))
                    x0 = T - P - i * P
                    mx = st[:, r:r + 1]
                    start, done = -SC * FLOOR, 0
                    if br == 0:
                        bias = BT[:, h, x0 + CB - 1::CB][:, 0:nk]
                    else:
                        bias = BT[:, h, x0 + k0:x0 + k0 + nk]
                        if br == 2 and i >= 4:
                            own.then(v.tensor_tensor_reduce(out=Pm[:, a % NPM, 0:P], in0=s[:, 0:P], in1=far[:, h],
                                                            scale=-SC, scalar=start, op0=ALU.add, op1=ALU.min,
                                                            accum_out=mx))
                            start, done, bias = mx, P, bias[:, P:]
                    free(v.tensor_tensor_reduce(out=Pm[:, a % NPM, done:nk], in0=s[:, done:nk], in1=bias, scale=-SC,
                                                scalar=start, op0=ALU.add, op1=ALU.min,
                                                accum_out=mx if not done else st[:, 40 + r:41 + r]), key)
                if t + 1 >= 0 and t + 1 < n_at:
                    own.settle()
                    own.step(v.reciprocal(st[:, 48 + rn:49 + rn], st[:, 24 + rn:25 + rn]))
                if t >= 0:
                    i, h, br, k0, nk = AT[t]
                    key = ("PV", t)
                    r = t % 8
                    full(dve, key)
                    o = oN[:, i, h * HD:(h + 1) * HD]
                    p_ = slot(key)[:, 0:HD]
                    w = st[:, 56 + r:57 + r]
                    if br == 0:
                        dve.wait_ge(dve_gate, t + 1)
                        free(v.tensor_scalar(o, p_, w, None, ALU.mult), key)
                    else:
                        read_out(dve, ("PV", t - 1))
                        dve.wait_ge(dve_gate, t + 1)
                        free(v.scalar_tensor_tensor(o, p_, w, o, ALU.mult, ALU.add), key)
                if t + 1 >= 0 and t + 1 < n_at:
                    own.settle()
                    i, h, br = AT[t + 1][0:3]
                    tt(st[:, 56 + rn:57 + rn], st[:, 48 + rn:49 + rn], gates[:, i, 3 * h + br:3 * h + br + 1])\
                        .then_inc(dve_gate, 1)
                if a < 4 * 4 * DB:
                    sum_lines(a // 4, a % 4)
                for key in BETWEEN.get(a, []):
                    compressed_branch(key)

            far_bias = V64[:, 0:1]
            own.step(v.tensor_copy(sbias[0:64], far_bias.to_broadcast([64, ROWS * SK]).rearrange("p (r c) -> p r c", r=ROWS)))
            own.settle()
            last_block = V64[:, WIN - 64:WIN].rearrange("p (c r) -> p r c", r=ROWS)
            prev_block = V64[:, WIN - 128:WIN - 64]
            own.step(v.tensor_copy(sbias[0:64, :, (SLOTS - 1) * LINES:SL], last_block))
            own.step(v.tensor_scalar(score[0:64], prev_block, far_bias, None, ALU.subtract))
            own.step(v.tensor_copy(sbias[0:64, 0, SL:SK], V64[:, WIN:WIN + 1]))
            own.step(v.memset(sbias[0:64, 1:ROWS, SL:SK], NEG))
            own.settle()
            s4 = [64, PICK, LINES]
            for r in range(ROWS):
                diff = score[0:64].rearrange("p (c r) -> p r c", r=ROWS)[:, r].unsqueeze(1).to_broadcast(s4)
                own.then(tt(sdiff[0:64], bcast(is62[0:64, 0:PICK], s4), diff))
                own.then(tt(sbias[0:64, r, 0:PICK * LINES].rearrange("p (s c) -> p s c", c=LINES),
                            sbias[0:64, r, 0:PICK * LINES].rearrange("p (s c) -> p s c", c=LINES), sdiff[0:64], ALU.add))

            full(dve, "wS")
            softmax_in(Pw[0:64].rearrange("p (j c) -> p j c", j=4), slot("wS")[0:64, 0:512].rearrange("p (j c) -> p j c", j=4),
                       V64[:, 1:WIN + 1].rearrange("p (c j) -> p j c", j=4), "wS")
            softmax_out(2, Pw[0:64]).then_inc(pw_ready, 1)
            full(dve, "wO")
            dve.wait_ge(win_stored, 16 * DB)
            for n in range(2 * DB):
                g = n % 2
                dve.wait_ge(gat[n % 3], 16 * GAT0[n % 3] + 32 * (n // 3 + 1))
                v.tensor_copy(Vs[0:SK, n], gring[0:SK, n % 3].rearrange("p (r c) -> p r c", r=ROWS)
                              [:, :, P + g * HD:P + (g + 1) * HD]).then_inc(vs_ready, 1)
            full(dve, "gS")
            two = lambda x: x.rearrange("p (a c) -> p a c", a=2)
            flatS = Ps[0:64].rearrange("p a c -> p (a c)")
            softmax_in(two(flatS), two(slot("gS")[0:64])[:, :, 0:4 * SK],
                       two(sbias[0:64].rearrange("p a c -> p (a c)")), "gS")
            softmax_out(3, flatS).then_inc(pw_ready, 1)
            gt = gates[0:DB, NT].rearrange("b (h r) -> b h r", r=3)
            for br in range(3):
                key = "oT0" if br < 2 else "oT1"
                full(dve, key)
                ins = tt(oS[0:DB, br].rearrange("b (g h d) -> b g h d", g=NKV, h=GQ),
                         slot(key)[0:DB].rearrange("b (g r h d) -> b g r h d", g=NKV, r=2, h=GQ)[:, :, br % 2],
                         bcast(gt[:, :, br].rearrange("b (g h) -> b g h", g=NKV), [DB, NKV, GQ, HD]))
                own.step(ins) if br == 0 else free(ins, key)
            own.settle()
            read_out(dve, "oT0")
            read_out(dve, "oT1")
            own.then(tt(oS[0:DB, 0], oS[0:DB, 0], oS[0:DB, 1], ALU.add))
            tt(oS[0:DB, 0], oS[0:DB, 0], oS[0:DB, 2], ALU.add).then_inc(oS_ready, 1)

            for m in range(4):
                for c in range(2):
                    read_out(dve, ("glu", m, c))
            own.then(tt(oF, oF, yF))
            dve.sem_inc(oF_ready, 1)
            read_out(dve, ("ss", 0))
            read_out(dve, ("ss", 1))
            own.then(v.reciprocal(RS, RS))
            for k in range(4):
                ins = v.scalar_tensor_tensor(mT[:, 4 + k], oF[:, k], cols[:, 52 + k:53 + k], RS, ALU.mult, ALU.mult)
                own.step(ins)
            own.settle()
            dve.sem_inc(m_ready, 1)
            for i in range(NT + 1):
                c0, n = token_tile(i)
                src = oN[:, i] if i < NT else oS[0:DB, 0]
                dve.wait_ge(on_stat, i + 1)
                own.then(v.reciprocal(st[0:n, 32 + i:33 + i], st[0:n, 16 + i:17 + i]))
                v.tensor_scalar(src, src, st[0:n, 32 + i:33 + i], None, ALU.mult).then_inc(on_ready, 1)
                key = ("n0", i)
                full(dve, key)
                free(tt(mT[:, 0:4, c0:c0 + n], slot(key)[:, 0:512].rearrange("p (k t) -> p k t", k=4)[:, :, 0:n],
                        bcast(cols[:, 48:52], [P, 4, n])), key)
            for i in range(NT + 1):
                read_out(dve, ("n0", i))
            dve.sem_inc(m_ready, 1)

            def residual(n):
                base = (n - 1) * (NT + 1)
                dve.wait_ge(grow_in, 16 * n)
                if n == 1:
                    dve.wait_ge(x1_in, 16 * (NT + 1))

                def add(i):
                    r = token_tile(i)[1]
                    key = (f"b{n}", i)
                    dve.wait_ge(res_stat, base + i + 1)
                    own.then(v.reciprocal(st[0:r, 9 + i % 2:10 + i % 2], st[0:r, 16 + i:17 + i]))
                    free(v.scalar_tensor_tensor(tb[0:r, i % 2], slot(key)[0:r], st[0:r, 9 + i % 2:10 + i % 2], grow[0:r],
                                                ALU.mult, ALU.mult), key)
                    read_out(dve, key)
                    tt(x1[0:r, i], x1[0:r, i], tb[0:r, i % 2], ALU.add).then_inc(res_sum if n < 3 else out_ready, 1)

                def scale(i):
                    r = token_tile(i)[1]
                    dve.wait_ge(res_stat2, base + i + 1)
                    own.then(v.reciprocal(st[0:r, 11 + i % 2:12 + i % 2], st[0:r, 48 + i:49 + i]))
                    v.tensor_scalar(tb[0:r, i % 2], x1[0:r, i], st[0:r, 11 + i % 2:12 + i % 2], None, ALU.mult)\
                        .then_inc(res_norm, 1)

                def forward(i):
                    c0, r = token_tile(i)
                    key = (f"f{n}", i)
                    full(dve, key)
                    free(tt((hT if n == 1 else hRaw)[:, :, c0:c0 + r], slot(key).rearrange("p (k t) -> p k t", k=KD)[:, :, 0:r],
                            bcast(cols[:, 16 * n:16 * n + 8], [P, KD, r])), key)

                def input_lo(i):
                    c0, r = token_tile(i)
                    dve.wait_ge(h_hi, i + 1)
                    tt(hL[:, :, c0:c0 + r], hRaw[:, :, c0:c0 + r], hH[:, :, c0:c0 + r], ALU.subtract).then_inc(h_lo, 1)

                add(0)
                for i in range(NT + 1):
                    if i < NT:
                        add(i + 1)
                    if n < 3:
                        scale(i)
                        forward(i)
                    if n == 2 and i >= 1:
                        input_lo(i - 1)
                if n == 2:
                    input_lo(NT)

            residual(1)

            for i in range(2):
                dve.wait_ge(mem_stat, i + 1)
                own.then(v.reciprocal(st[:, 32 + i:33 + i], st[:, 16 + i:17 + i]))
                v.tensor_scalar(mrow[:, i], mrow[:, i], st[:, 32 + i:33 + i], None, ALU.mult).then_inc(mem_norm, 1)
            for i in range(2):
                full(dve, ("mn", i))
                free(tt(memT[:, :, i * P:(i + 1) * P], slot(("mn", i)).rearrange("p (k t) -> p k t", k=KD),
                        bcast(cols[:, 56:64], [P, KD, P])), ("mn", i))
            for m in range(4):
                for c in range(2):
                    read_out(dve, ("xq", m, c))
            dve.wait_ge(qxz_zero, 1)
            for h in range(XH):
                own.step(v.tensor_copy(qxz[:, h].rearrange("p b c -> p (b c)")[:, h::36], q2T[:, h, T:TC]))
            own.settle()
            dve.sem_inc(qxz_ready, 1)
            full(dve, "xS")
            own.then(v.tensor_reduce(st[0:32, 32:33], slot("xS")[0:32, 0:NM], X, ALU.max))
            v.tensor_scalar(st[0:32, 33:34], st[0:32, 32:33], -XSC, None, ALU.mult).then_inc(px_raw, 1)
            read_out(dve, "xS")
            own.then(v.reciprocal(st[0:32, 36:37], st[0:32, 34:35]))
            v.tensor_scalar(Pxs[0:32], Pxs[0:32], st[0:32, 36:37], None, ALU.mult).then_inc(px_ready, 1)
            full(dve, "xO")
            free(v.tensor_copy(q2T[:, :, T:TC], slot("xO")[:, 0:32].rearrange("p (h b) -> p h b", h=XH)), "xO")
            for i in range(NT + 1):
                if i < NT:
                    key = ("XS", i)
                    full(dve, key)
                    b0 = 8 * (i % 2)
                    own.then(v.tensor_reduce(st[:, 32 + b0:36 + b0], slot(key).rearrange("p (h n) -> p h n", h=XH), X, ALU.max))
                    v.tensor_scalar(st[:, b0:b0 + 4], st[:, 32 + b0:36 + b0], -XSC, None, ALU.mult).then_inc(px_raw, 1)
                    read_out(dve, key)
                    own.then(v.reciprocal(st[:, 48 + b0:52 + b0], st[:, 16 + b0:20 + b0]))
                    px = Px[:, i % 2].rearrange("p (h n) -> p h n", h=XH)
                    tt(px, px, bcast(st[:, 48 + b0:52 + b0], [P, XH, NM])).then_inc(px_ready, 1)
                if i >= 1:
                    key = ("XO", i - 1)
                    full(dve, key)
                    free(v.tensor_copy(q2T[:, :, (i - 1) * P:i * P], slot(key)[:, 0:512].rearrange("p (h n) -> p h n", h=XH)), key)
            residual(2)

            def weights_lo(it):
                n = first_ffn + it
                dve.wait_ge(w_hi, it + 1)
                size = group_size(ffn[it])
                tt(wL[it % 2][:, 0:size], wRaw[:, n % NS, 0:size],
                   wH[it % 2][:, 0:size], ALU.subtract).then_inc(w_lo, 1)

            weights_lo(0)
            for it, item in enumerate(ffn):
                if it + 1 < FFN_ITEMS:
                    weights_lo(it + 1)
                if item[0] == "u":
                    n = item[1] % FG
                    for c in range(2):
                        read_out(dve, ("g", item[1], c))
                        full(dve, item + (c,))
                        if c == 0:
                            w, s = gRaw[:, n, 0:2 * CH].rearrange("p (a n) -> p a n", a=2), chunked(item + (0,))
                        else:
                            w, s = gRaw[:, n, 2 * CH:TC], chunked(item + (1,))[:, 0]
                        free(tt(w, w, s), item + (c,))
                    read_out(dve, item + (0,))
                    read_out(dve, item + (1,))
                    dve.sem_inc(g_prod, 1)
                    dve.wait_ge(g_hi, item[1] + 1)
                    tt(gL[:, n], gRaw[:, n], gH[:, n], ALU.subtract).then_inc(g_lo, 1)
                elif item[0] == "o":
                    grp = item[1]
                    for m in (item[2], item[2] + 1):
                        for c in range(2):
                            key = ("wf", grp, m, c)
                            full(dve, key)
                            if c == 0:
                                y, s = yT[:, m, 0:2 * CH].rearrange("p (a n) -> p a n", a=2), chunked(key)
                            else:
                                y, s = yT[:, m, 2 * CH:TC], chunked(key)[:, 0]
                            if grp == 0:
                                free(v.tensor_copy(y, s), key)
                            else:
                                read_out(dve, ("wf", grp - 1, m, c))
                                free(tt(y, y, s, ALU.add), key)
            residual(3)


_INPUTS = ["x_prompt", "x_sample", "cache_kv_cmp", "cache_kv_sel", "cache_kv_win", "state_ssm_re", "state_ssm_im",
           "cache_mem_kv", "page_table", "mem_prompt", "w_in", "w_out", "norm_g", "grp_norm_g", "cmp_pos", "cmp_proj",
           "rel_bias", "ssm_a_re", "ssm_a_im", "ssm_b_re", "ssm_b_im", "ssm_c_re", "ssm_c_im", "ssm_d", "ssm_log_dt",
           "glu_w", "glu_b", "mem_norm_g", "xq", "xkv", "xo", "ffn_wi", "ffn_wo"]
_OUTPUTS = [(1, T, D), (DB, 1, D), (1, 1, T, 2, NKV, HD), (1, 1, T, 2, NKV, HD), (1, 1, WIN, 2, NKV, HD),
            (1, 1, 32, 64), (1, 1, 32, 64), (1, 1, NM, 2, XH, P), (1, DB, 1, 2, NKV, HD), (1, DB, 1, 2, NKV, HD),
            (1, DB, WIN, 2, NKV, HD), (1, DB, 32, 64), (1, DB, 32, 64)]


def kernel(**inputs):
    import concourse.bacc as bacc
    from concourse.bass_utils import run_bass_kernel_spmd

    nc = bacc.Bacc("TRN2", target_bir_lowering=False, num_devices=1)
    arrays, args = {}, []
    for name in _INPUTS:
        a = np.ascontiguousarray(inputs[name])
        arrays[f"in_{name}"] = a
        args.append(nc.dram_tensor(f"in_{name}", a.shape, mybir.dt.from_np(a.dtype), kind="ExternalInput").ap())
    for i, shape in enumerate(_OUTPUTS):
        args.append(nc.dram_tensor(f"out_{i}", shape, F32, kind="ExternalOutput").ap())
    hymba_step(nc, *args)
    r = run_bass_kernel_spmd(nc, [arrays], core_ids=[0])
    return tuple(r.results[0][f"out_{i}"] for i in range(len(_OUTPUTS)))
```

```python
from contextlib import ExitStack
from math import log, pi

import numpy as np

import concourse.bass as bass
from concourse import mybir

F32 = mybir.dt.float32
F32R = mybir.dt.float32r
I32 = mybir.dt.int32
U32 = mybir.dt.uint32
ALU = mybir.AluOpType
ACT = mybir.ActivationFunctionType
X = mybir.AxisListType.X

P = 128
D = 1024
KD = D // P
T = 1024
NT = T // P
DB = 8
TC = T + DB
CH = TC // 3
HD = 64
NH = 8
NKV = 2
GQ = NH // NKV
KVC = 3 * 2 * NKV * HD
NG = 3 * NH
OFF_U = NH * HD + KVC + NG
CB = 32
WIN = 512
PAST = 4096
PAGE = 128
NPAGE = PAST // PAGE
NSB = PAST // 64
PICK = 13
SLOTS = PICK + 2
PARAM_DMAS = 9
ROWS = 8
LINES = 64 // ROWS
SL = SLOTS * LINES
SK = SL + 1
GAT0 = [11, 11, 10]
NPAIR = 16
L4 = 4
NC = T // L4
NF = 22
DFF = NF * P
FG = 3
NGRP = -(-NF // FG)
FFN_ITEMS = 2 * NF + 4 * NGRP
XH = 4
NM = 256
EPS = 1e-6
TINY = 1e-30
SC = HD ** -0.5
NEG = -1e30 / SC
FLOOR = -1e20 / SC
XSC = P ** -0.5
QS = 4
AHEAD = 2
NPM = AHEAD + 1
VL = T + P - 1


def bucket_ranges():
    n = np.arange(T)
    big = 16 + (np.log(np.maximum(n, 16).astype(np.float32) / 16) / log(8) * 16).astype(np.int32)
    b = np.where(n < 16, n, np.minimum(big, 31))
    return [(int(v), int(np.argmax(b == v)), int(T - 1 - np.argmax(b[::-1] == v))) for v in np.unique(b)]


def token_tile(i):
    return (i * P, P) if i < NT else (T, DB)


def attention_units():
    out = []
    for i in range(NT):
        out.append((i, 0, 0, 0, 4 * (i + 1)))
        for h in range(NH):
            out.append((i, h, 1, 0, P * (i + 1)))
            k0 = max(0, i - 4) * P
            out.append((i, h, 2, k0, P * (i + 1) - k0))
    return out


SUMS_AT = 2
BETWEEN = {SUMS_AT + 3 * 4 * DB + 1 + 2 * b: [("sT", b), ("sP", b)] for b in range(DB)}
BETWEEN.update({122: ["sc"], 124: ["sps", "scT"], 127: ["sov", "ix1"], 130: ["ix2"]})


def ffn_items():
    items = []
    for grp in range(NGRP):
        for k in group_tiles(grp):
            items += [("g", k), ("u", k)]
        items += [("o", grp, m) for m in range(0, 8, 2)]
    return items


def group_tiles(grp):
    return range(grp * FG, min(NF, (grp + 1) * FG))


GLU_AFTER = {4: 2, 9: 3}


def unit_number(i, h, br):
    return i * (2 * NH + 1) + (2 * h + br if br else 0)


def residual_plan(n):
    order = []
    for i in range(NT + 3):
        if i <= NT:
            order.append((f"b{n}", i))
        if i >= 2:
            order.append((f"f{n}", i - 2))
    return order


def psum_plan():
    order = ["par", ("n1", 0), ("n1", 1)]
    for i in range(NT + 1):
        order += [("kv", i)] + ([("n1", i + 2)] if i + 2 <= NT else []) + ([("kT", i - 1)] if i else [])
    order += ["cproj", "C", "h0"]
    order += [("in", m, c) for m in range(8) for c in range(2)]
    order += [("SA", 0)]
    for j in range(NPAIR):
        order += ([("SA", j + 1)] if j + 1 < NPAIR else []) + [("SB", j)]
    order += [("mn", i) for i in range(2)] + [("mk", c) for c in range(8)]
    order += [("V", j) for j in range(NPAIR)]
    order += ["ys", "st"] + [("sst", q) for q in range(4)]
    order += [("bt", h) for h in range(NH)]
    n = len(attention_units())
    for a in range(n + AHEAD + 1):
        if a < n:
            order.append(("SC", a))
        if AHEAD <= a < n + AHEAD:
            order.append(("TR", a - AHEAD))
        if a > AHEAD:
            order.append(("PV", a - AHEAD - 1))
        order += BETWEEN.get(a, [])
    order += [("glu", m, c) for m in range(2) for c in range(2)]
    order += [("wT", b) for b in range(DB)] + ["wS", "wP", "wO"]
    for n in range(2 * DB):
        order += [("gT", n // 2, n % 2)]
        if n in GLU_AFTER:
            order += [("glu", GLU_AFTER[n], c) for c in range(2)]
    order += ["gS", "gP", "gO", "oT0", "oT1"]
    order += [("n0", i) for i in range(NT + 1)]
    order += [("ss", c) for c in range(2)]
    order += [("wo", m, c) for m in range(8) for c in range(2)]
    order += residual_plan(1)
    order += ["mT"]
    order += [("xq", m, c) for m in range(4) for c in range(2)]
    order += [("xT", b) for b in range(DB)] + ["xS", "xP", "xO"]
    for i in range(NT + 3):
        order += [("XS", i)] if i < NT else []
        order += [("XT", i - 2)] if 2 <= i < NT + 2 else []
        order += [("XO", i - 3)] if i >= 3 else []
    order += [("xo", m, c) for m in range(8) for c in range(2)]
    order += residual_plan(2)
    for item in ffn_items():
        if item[0] == "o":
            order += [("wf", item[1], item[2] + n, c) for n in range(2) for c in range(2)]
        else:
            order += [item + (c,) for c in range(2)]
    order += [("b3", i) for i in range(NT + 1)]
    return {k: n for n, k in enumerate(order)}


def hymba_step(nc, x_prompt, x_sample, cache_kv_cmp, cache_kv_sel, cache_kv_win, state_ssm_re, state_ssm_im,
               cache_mem_kv, page_table, mem_prompt, w_in, w_out, norm_g, grp_norm_g, cmp_pos, cmp_proj,
               rel_bias, ssm_a_re, ssm_a_im, ssm_b_re, ssm_b_im, ssm_c_re, ssm_c_im, ssm_d, ssm_log_dt,
               glu_w, glu_b, mem_norm_g, xq, xkv, xo, ffn_wi, ffn_wo,
               y_prompt, y_sample, p_kv_cmp, p_kv_sel, p_kv_win, p_ssm_re, p_ssm_im, p_mem_kv,
               s_kv_cmp, s_kv_sel, s_kv_win, s_ssm_re, s_ssm_im):
    U = psum_plan()
    AT = attention_units()
    ctx = ExitStack()
    with ctx:
        def sb(name, shape, dt=F32):
            return ctx.enter_context(nc.sbuf_tensor(name, shape, dt))

        def sem(name):
            return ctx.enter_context(nc.semaphore(name))

        ident = sb("ident", [P, P])
        flip = sb("flip", [P, P])
        ones = sb("ones", [P, P])
        same = sb("same", [64, 64])
        spread = sb("spread", [SLOTS, SL])
        block_of = sb("block_of", [P, 4])
        dt2 = sb("dt2", [NPAIR, 2])
        cols = sb("cols", [P, 120])
        d_rows = sb("d_rows", [P, NPAIR])
        gates = sb("gates", [P, NT + 1, NG])
        tab = sb("tab", [NH, 32])
        eps_c = sb("eps_c", [P, 1])
        st = sb("st", [P, 64])
        kcT = sb("kcT", [P, NKV, 32])
        vc = sb("vc", [32, NKV * HD])
        csum = sb("csum", [P, 2, 32])
        pblk = sb("pblk", [P, 2, P])
        osT = sb("osT", [P, 3, 64])
        V64 = sb("V64", [64, WIN + 1])
        uS = sb("uS", [P, 4, DB])
        apow = sb("apow", [P, 6, 2, NPAIR])
        line = sb("line", [SL, 64], U32)
        pline = sb("pline", [P, 4, DB], U32)
        ptc = sb("ptc", [P, DB], I32)
        tiny = sb("tiny", [P, 16], I32)
        tinyf = sb("tinyf", [P, 16])
        jota_i = sb("jota_i", [64, 64], I32)
        jota = sb("jota", [64, 64])
        ptrow = sb("ptrow", [64, NPAGE], I32)
        co = sb("co", [P, 2, NPAIR])
        cst = sb("cst", [P, 3, NH])

        arena_at = -(-nc.sbuf_base // 32) * 32
        A = sb("A", [P, 49504])

        def at(first, *shape):
            n = int(np.prod(shape))
            v = A[:, first:first + n]
            if len(shape) == 2:
                v = v.rearrange("p (a b) -> p a b", b=shape[1])
            elif len(shape) == 3:
                v = v.rearrange("p (a b c) -> p a b c", b=shape[1], c=shape[2])
            elif len(shape) == 4:
                v = v.rearrange("p (a b c d) -> p a b c d", b=shape[1], c=shape[2], d=shape[3])
            return v

        def exact(name, first, *shape, dt=F32R):
            v = nc.alloc_sbuf_tensor_at(name, [P, int(np.prod(shape))], dt, offset=arena_at + 4 * first)[:, :]
            if len(shape) == 2:
                v = v.rearrange("p (a b) -> p a b", b=shape[1])
            return v

        qT = at(0, 4, TC)
        vkeep = at(4128, NT, 2 * P)
        kTd = exact("kTd", 6176, 2 * NKV, T, dt=F32)
        kH = exact("kH", 33056, 2 * NKV, T)
        kL = exact("kL", 6176, 2 * NKV, T)
        qS = exact("qS", 43296, QS, P)
        U2 = at(10272, NPAIR, NC)
        summ = at(14368, DB, 2 * P)
        kcTs = at(16416, DB, P)
        vcs = at(17440, DB, P)
        hT = at(18464, KD, TC)
        wkv = at(26720, KD, KVC + NG)
        gring = at(26720, 3, ROWS * 256)
        NS = 4
        wring = at(33056, NS, KD, P)
        xin = at(37152, 2, D)
        junk = at(39200, D)
        uTm = at(29792, 2, TC)
        kvst = at(42288, 2, KVC + NG)
        posP = at(43872, 256)
        cprod = at(44128, 2, 256)
        prow = at(44896, P)
        drow = at(45024, P)
        dtrow = at(49376, P)
        kvS = at(45152, KVC)
        H = at(18464, NC + 1, 2, NPAIR)
        CP = at(37152, 2, NPAIR, 5, 32)
        Tm = [at(42272, P), at(43296, P)]
        Wm = [at(42400, 2, P), at(43424, 2, P)]
        sTm = [at(26720, 2, P), at(26976, 2, P)]
        posB = at(43872, ROWS, P)
        WT = at(44896, 2, NPAIR, P)
        bb = at(26720, 2, NPAIR, 16)
        braw = at(26720 + 512, 2, NPAIR, 16)
        cc = at(26720 + 1024, 2, NPAIR, 16)
        q = at(26720 + 1536, 4, NPAIR, 16)
        craw = at(26720 + 2560, 8, HD)
        h0row = at(14368, 2, 2048)
        V8 = at(46000, VL)
        prm = at(47200, 16, NPAIR)
        st_rows = at(49280, P)
        sst_rows = at(14368, 4 * D)
        r1 = at(44896, 16, 2, 2 * NPAIR)
        turn = A[:, 46912:46912 + 17 * 64].rearrange("p (n a b j) -> p n a b j", n=17, a=2, b=2)
        apw = at(44896 + 1024, 15, 2, NPAIR)
        us3 = at(42656, NPAIR, DB)
        h0T = at(42784, 2, NPAIR, DB)
        hs = at(49024, 2, NPAIR, DB)
        yF = at(44896, 4, TC)
        SQ = at(37152, 4, TC)
        RS = at(41280, TC)
        oF = at(0, 4, TC)
        junkR = at(26720, D)
        dtmp = at(26720 + D, 2, D)
        scr = at(42400, 512)
        junk2 = at(14368, D)
        BT = at(18464, NH, T)
        far = at(37152, NH, P)
        Pm = at(38176, NPM, T)
        PT = at(41248, 2, T)
        hank = at(38176, 2, T)
        oN = at(10272, NT, NH * HD)
        nbuf = at(18464, DB, 4, 256)
        kTw = at(37152, DB, 512)
        Pw = at(41248, 512)
        PTw = at(41760, 4, 64)
        Pc = at(14368, P)
        PcT = at(14496, 64)
        score = at(14560, 64)
        score2 = at(14624, 64)
        top = at(14688, 16)
        topi = at(14704, 16).bitcast(U32)
        pick = at(14720, 16)
        phys = at(14736, 16)
        is62 = at(14752, 16)
        p15 = at(14768, 64)
        cbias = at(14832, P)
        jphys = at(15024, 64)
        onehot = at(15152, SLOTS, 64)
        sbias = at(15152, ROWS, SK)
        sdiff = at(16128, PICK, LINES)
        kTs = at(37152, DB, ROWS, SK)
        Vs = at(18464, 2 * DB, ROWS, HD)
        Ps = at(10272 + 4096, ROWS, SK)
        PTs = at(10272 + 4096 + 1024, ROWS, 64)
        qz = sb("qz", [P, DB, 64])
        oS = at(43360, 3, NH * HD)
        x1 = at(0, NT + 1, D)
        yT = at(37152, KD, TC)
        q2T = at(26720, XH, TC)
        mkv = at(30848, 2, D)
        mkT = at(46432, XH, NM)
        grow = at(45408, D)
        tb = at(47456, 2, D)
        Px = at(10272, 3, XH * NM)
        PTx = at(13344, 2, XH * NM)
        kst = at(14368, 2, 2, 512)
        qxz = at(16416, XH, DB, 32)
        mrow = at(26720, 2, D)
        memT = at(28768, KD, NM)
        mkv_new = at(30816, 2, D)
        Vm = at(18464, DB, 2, 512)
        kTm = at(37152, DB, XH, NM)
        Pxs = at(17440, NM)
        PTxs = at(17440 + 256, 2, 32)

        hH = exact("hH", 18464, KD, TC)
        hL = exact("hL", 9216, KD, TC)
        hRaw = exact("hRaw", 9216, KD, TC, dt=F32)
        gH = exact("gH", 26720, FG, TC)
        gL = exact("gL", 26720 + FG * TC, FG, TC)
        gRaw = exact("gRaw", 26720 + FG * TC, FG, TC, dt=F32)
        wRaw = exact("wRaw", 33056, NS, KD * P, dt=F32)
        mH = exact("mH", 18496, KD, TC)
        mRaw = [exact("mA", 14368, 4, TC, dt=F32)] + [exact(f"mS{k}", 10208 + k * TC, TC, dt=F32) for k in range(4)]
        mAL = exact("mAL", 14368, 4, TC)
        mL = [mAL[:, k] for k in range(4)] + [exact(f"mSL{k}", 10208 + k * TC, TC) for k in range(4)]
        wHm = [exact("wHm0", 26752, KD * P), exact("wHm1", 28800, KD * P)]
        wLm = [exact("wLm0", 27776, KD * P), exact("wLm1", 29824, KD * P)]
        wH = [exact("wH0", 45408, KD * P), exact("wH1", 47456, KD * P)]
        wL = [exact("wL0", 46432, KD * P), exact("wL1", 48480, KD * P)]

        PS = ctx.enter_context(nc.psum_tensor("PS", [P, 8, 512], F32))

        def slot(key):
            s = U[key] % 4
            return PS[:, 2 * s:2 * s + 2, :].rearrange("p a b -> p (a b)")

        def chunked(key):
            s = U[key] % 4
            return PS[:, 2 * s:2 * s + 2, 0:CH]

        bias_dram = nc.dram_tensor("bias_by_distance", [NH, VL], F32, kind="Internal").ap()
        win_row = nc.dram_tensor("new_window_row", [DB, 256], F32, kind="Internal").ap()
        sel_row = nc.dram_tensor("new_selected_row", [DB, 256], F32, kind="Internal").ap()

        filled = sem("filled")
        emptied = [sem(f"emptied{s}") for s in range(4)]
        w_loaded = [sem(f"w_loaded{s}") for s in range(NS)]
        consts = sem("consts")
        params = sem("params")
        x_in = [sem(f"x_in{s}") for s in range(2)]
        wkv_in = sem("wkv_in")
        pos_in = sem("pos_in")
        pblk_zero = sem("pblk_zero")
        tab_in = sem("tab_in")
        s5_arg = sem("s5_arg")
        s5_fun = sem("s5_fun")
        win_stored = sem("win_stored")
        states_staged = sem("states_staged")
        res_stat2 = sem("res_stat2")
        mem_stat = sem("mem_stat")
        on_stat = sem("on_stat")
        oF_ready = sem("oF_ready")
        mkv_out = sem("mkv_out")
        mkv_in = sem("mkv_in")
        weighted = sem("weighted")
        qxz_zero = sem("qxz_zero")
        b_in = sem("b_in")
        c_in = sem("c_in")
        xn_ready = sem("xn_ready")
        rt_ready = sem("rt_ready")
        kv_stored = [sem(f"kv_stored{s}") for s in range(2)]
        kv_ready = sem("kv_ready")
        prod_ready = sem("prod_ready")
        rows_saved = sem("rows_saved")
        gat = [sem(f"gat{s}") for s in range(3)]
        gat_used = sem("gat_used")
        posB_in = sem("posB_in")
        summ_ready = sem("summ_ready")
        pline_ready = sem("pline_ready")
        pt_in = sem("pt_in")
        s5_built = sem("s5_built")
        s5_states = sem("s5_states")
        hs_ready = sem("hs_ready")
        u_moved = sem("u_moved")
        uT_ready = sem("uT_ready")
        qz_ready = sem("qz_ready")
        pc_ready = sem("pc_ready")
        phys_ready = sem("phys_ready")
        line_ready = sem("line_ready")
        v8_out = sem("v8_out")
        V64_in = sem("V64_in")
        hank_in = [sem(f"hank_in{s}") for s in range(2)]
        far_ready = sem("far_ready")
        k_hi = sem("k_hi")
        k_lo = sem("k_lo")
        q_hi = sem("q_hi")
        q_lo = sem("q_lo")
        c_raw = sem("c_raw")
        dve_gate = sem("dve_gate")
        exp_ready = sem("exp_ready")
        nbuf_in = sem("nbuf_in")
        vs_ready = sem("vs_ready")
        pw_raw = sem("pw_raw")
        pw_exp = sem("pw_exp")
        pw_ready = sem("pw_ready")
        oS_ready = sem("oS_ready")
        y_ready = sem("y_ready")
        gelu_ready = sem("gelu_ready")
        sq_ready = sem("sq_ready")
        m_ready = sem("m_ready")
        on_ready = sem("on_ready")
        x1_in = sem("x1_in")
        grow_in = sem("grow_in")
        res_stat = sem("res_stat")
        res_sum = sem("res_sum")
        res_norm = sem("res_norm")
        mem_in = sem("mem_in")
        mem_norm = sem("mem_norm")
        vm_in = sem("vm_in")
        kst_in = [sem(f"kst_in{s}") for s in range(2)]
        qxz_ready = sem("qxz_ready")
        px_raw = sem("px_raw")
        px_ready = sem("px_ready")
        m_hi = sem("m_hi")
        m_lo = sem("m_lo")
        h_hi = sem("h_hi")
        h_lo = sem("h_lo")
        w_hi = sem("w_hi")
        w_lo = sem("w_lo")
        g_prod = sem("g_prod")
        g_hi = sem("g_hi")
        g_lo = sem("g_lo")
        states_out = sem("states_out")
        out_ready = sem("out_ready")
        stored = sem("stored")
        dve_own = sem("dve_own")
        act_own = sem("act_own")
        pool_own = sem("pool_own")

        def full(eng, key):
            eng.wait_ge(filled, U[key] + 1)

        def read_out(eng, key):
            eng.wait_ge(emptied[U[key] % 4], U[key] // 4 + 1)

        def free(ins, key):
            ins.then_inc(emptied[U[key] % 4], 1)

        class Own:

            def __init__(self, eng, s):
                self.eng, self.sem, self.n = eng, s, 0

            def step(self, ins):
                ins.then_inc(self.sem, 1)
                self.n += 1

            def settle(self):
                self.eng.wait_ge(self.sem, self.n)

            def then(self, ins):
                self.step(ins)
                self.settle()

        stream = []
        wi_, wo_ = w_in[0], w_out[0]
        for m in range(8):
            c0 = m * P if m < 4 else OFF_U + (m - 4) * P
            stream.append((wi_[:, c0:c0 + P], KD, ("in", m, 1)))
        for m in range(8):
            stream.append((xkv[0][:, m * P:(m + 1) * P], KD, ("mk", m)))
        first_glu = len(stream)
        for m in range(4):
            stream.append((glu_w[0][:, m * P:(m + 1) * P], 4, ("glu", m, 1)))
        first_wo = len(stream)
        for m in range(8):
            stream.append((wo_[:, m * P:(m + 1) * P], KD, ("wo", m, 1)))
        for m in range(4):
            stream.append((xq[0][:, m * P:(m + 1) * P], KD, ("xq", m, 1)))
        for m in range(8):
            stream.append((xo[0][:, m * P:(m + 1) * P], 4, ("xo", m, 1)))
        ffn = ffn_items()
        first_ffn = len(stream)
        for item in ffn:
            if item[0] == "o":
                tiles = group_tiles(item[1])
                src = ffn_wo[0][tiles[0] * P:(tiles[-1] + 1) * P, item[2] * P:(item[2] + 2) * P]
                stream.append((src, len(tiles), None))
            else:
                c0 = item[1] * P + (DFF if item[0] == "u" else 0)
                stream.append((ffn_wi[0][:, c0:c0 + P], KD, None))

        split = [(("wo", m), first_wo + m) for m in range(8)] + [(item, first_ffn + n) for n, item in enumerate(ffn)]
        split_number = {n: i for i, (_, n) in enumerate(split)}
        NWO = 8

        def parts_at(n):
            return (wHm[n % 2], wLm[n % 2]) if n < NWO else (wH[n % 2], wL[n % 2])

        def last_unit(item):
            return ("wf", item[1], item[2] + 1, 1) if item[0] == "o" else item + (1,)

        def group_size(item):
            return len(group_tiles(item[1])) * 2 * P if item[0] == "o" else KD * P

        block = ctx.enter_context(nc.Block())

        @block.sync
        def _(sp):
            for i in range(NT + 1):
                c0, n = token_tile(i)
                if i >= 2:
                    full(sp, ("n1", i - 2))
                src = x_prompt[0, c0:c0 + n, :] if i < NT else x_sample[:, 0, :]
                sp.dma_start(xin[0:n, i % 2, :], src).then_inc(x_in[i % 2], 16)
                if i == 1:
                    sp.dma_start(wkv, wi_[:, NH * HD:OFF_U].rearrange("(k p) n -> p k n", p=P)).then_inc(wkv_in, 16)
            for it, (src, kt, _) in enumerate(stream):
                if it - NS in split_number:
                    sp.wait_ge(w_lo, split_number[it - NS] + 1)
                elif it == first_glu:
                    full(sp, ("SC", len(AT) - 1))
                elif it >= NS and not first_glu < it < first_glu + NS:
                    full(sp, stream[it - NS][2])
                cols_ = src.shape[1]
                ring_slot = wRaw[:, it % NS] if it in split_number else wring[:, it % NS].rearrange("p k n -> p (k n)")
                sp.dma_start(ring_slot[:, 0:kt * cols_]
                             .rearrange("p (k n) -> p k n", n=cols_),
                             src.rearrange("(k p) n -> p k n", p=P)).then_inc(w_loaded[it % NS], 16)

        @block.tensor
        def _(pe):
            item = [0]

            def open_(key):
                if U[key] >= 4:
                    pe.wait_ge(emptied[U[key] % 4], U[key] // 4)
                return slot(key)

            def mm(out, lhsT, rhs, start=True, stop=True):
                return nc.tensor.matmul(out, lhsT=lhsT, rhs=rhs, start=start, stop=stop, skip_group_check=True)

            def tr(out, in_):
                b, n = in_.base_partition(), in_.shape[0]
                return nc.tensor.transpose(out, in_, ident[b:b + n, b:b + n])

            def next_weights():
                it = item[0]
                item[0] += 1
                pe.wait_ge(w_loaded[it % NS], 16 * (it // NS + 1))
                return wring[:, it % NS]

            def dense(stage, tiles, kts, rhs):
                for m in tiles:
                    a, b = (stage, m, 0), (stage, m, 1)
                    open_(a)
                    open_(b)
                    outs = [chunked(a)[:, 0], chunked(a)[:, 1], chunked(b)[:, 0]]
                    k, last = 0, sum(kts) - 1
                    for n, kt in enumerate(kts):
                        w = next_weights()
                        for kk in range(kt):
                            r = rhs(k)
                            for c in range(3):
                                ins = mm(outs[c], w[:, kk], r[:, c * CH:(c + 1) * CH], k == 0, k == last)
                                if k == last and c >= 1:
                                    ins.then_inc(filled, 1)
                            k += 1

            def exact_products(outs, wh, wl, xh, xl, first, last):
                for n, (w, x) in enumerate(((wl, xh), (wh, xl), (wh, xh))):
                    for c in range(3):
                        ins = mm(outs[c], w, x[:, c * CH:(c + 1) * CH], first and n == 0, last and n == 2)
                        if last and n == 2 and c >= 1:
                            ins.then_inc(filled, 1)

            pe.wait_ge(consts, 5)
            pe.wait_ge(params, 16 * PARAM_DMAS)
            s = open_("par")
            tr(s[:, 0:104], prow[0:104])
            tr(s[:, 104:120], dtrow[0:NPAIR])
            tr(s[:, 128:128 + NPAIR], drow[0:NPAIR]).then_inc(filled, 1)

            def norm_transposes(i):
                n = token_tile(i)[1]
                pe.wait_ge(xn_ready, i + 1)
                s = open_(("n1", i))
                for k in range(KD):
                    ins = tr(s[:, k * P:k * P + n], xin[0:n, i % 2, k * P:(k + 1) * P])
                ins.then_inc(filled, 1)

            def kv_transposes(i):
                pe.wait_ge(prod_ready, i + 1)
                s = open_(("kT", i))
                for br in range(2):
                    tr(s[:, br * P:(br + 1) * P], kvst[:, i % 2, 256 * (br + 1):256 * (br + 1) + P])
                for c in range(2):
                    ins = mm(s[:, 256 + 4 * c:260 + 4 * c], cprod[:, i % 2, c * P:(c + 1) * P], block_of[:, :])
                ins.then_inc(filled, 1)

            norm_transposes(0)
            norm_transposes(1)
            pe.wait_ge(wkv_in, 16)
            for i in range(NT + 1):
                c0, n = token_tile(i)
                read_out(pe, ("n1", i))
                s = open_(("kv", i))
                for k in range(KD):
                    mm(s[0:n, 0:512], hT[:, k, c0:c0 + n], wkv[:, k, 0:512], k == 0, k == KD - 1)
                    ins = mm(s[0:n, 512:KVC + NG], hT[:, k, c0:c0 + n], wkv[:, k, 512:KVC + NG], k == 0, k == KD - 1)
                ins.then_inc(filled, 1)
                if i + 2 <= NT:
                    norm_transposes(i + 2)
                if i:
                    kv_transposes(i - 1)
            read_out(pe, ("kT", NT - 1))
            s = open_("cproj")
            mm(s[:, 0:32], pblk[:, 0], csum[:, 0])
            mm(s[0:32, 32:32 + P], csum[:, 1], pblk[:, 1]).then_inc(filled, 1)

            pe.wait_ge(c_in, 64)
            s = open_("C")
            for n in range(8):
                ins = tr(s[0:HD, n * P:(n + 1) * P], craw[:, n])
            ins.then_inc(filled, 1)
            s = open_("h0")
            for part in range(2):
                for j in range(NPAIR):
                    c = (part * NPAIR + j) * DB
                    ins = tr(s[:, c:c + DB], h0row[0:DB, part, j * P:(j + 1) * P])
            ins.then_inc(filled, 1)

            dense("in", range(8), [KD], lambda k: hT[:, k])

            def s5_matrices(j):
                s = open_(("SA", j))
                for part in range(2):
                    tr(s[:, part * P:(part + 1) * P], WT[:, part, j])
                for l in range(L4):
                    for part in range(2):
                        ins = mm(s[32 * l:32 * l + 32, 512 + 32 * l:640], WT[:, part, j, 96:P],
                                 CP[:, part, j, 0:L4 - l].rearrange("p k c -> p (k c)"), part == 0, part == 1)
                ins.then_inc(filled, 1)

            pe.wait_ge(s5_built, 1)
            pe.wait_ge(u_moved, 1)
            s5_matrices(0)
            for j in range(NPAIR):
                if j + 1 < NPAIR:
                    s5_matrices(j + 1)
                read_out(pe, ("SA", j))
                s = open_(("SB", j))
                for part in range(2):
                    mm(s[:, part * NC:(part + 1) * NC], Wm[j % 2][:, part], U2[:, j])
                for part in range(2):
                    mm(s[:, 512 + part * DB:512 + (part + 1) * DB], Wm[j % 2][96:P, part], us3[96:P, j])
                mm(s[:, 528:528 + NC], Tm[j % 2], U2[:, j]).then_inc(filled, 1)

            for i in range(2):
                pe.wait_ge(mem_norm, i + 1)
                s = open_(("mn", i))
                for k in range(KD):
                    ins = tr(s[:, k * P:(k + 1) * P], mrow[:, i, k * P:(k + 1) * P])
                ins.then_inc(filled, 1)
            read_out(pe, ("mn", 0))
            read_out(pe, ("mn", 1))
            for c in range(8):
                w = next_weights()
                s = open_(("mk", c))
                for i in range(2):
                    for k in range(KD):
                        ins = mm(s[:, i * P:(i + 1) * P], memT[:, k, i * P:(i + 1) * P], w[:, k], k == 0, k == KD - 1)
                ins.then_inc(filled, 1)
            pe.wait_ge(s5_states, 1)
            for j in range(NPAIR):
                s = open_(("V", j))
                for part in range(2):
                    ins = mm(s[:, 0:NC], CP[:, part, j, 1:5].rearrange("p k c -> p (k c)"), H[:, 0:NC, part, j],
                             part == 0, part == 1)
                ins.then_inc(filled, 1)
            pe.wait_ge(hs_ready, 1)
            s = open_("ys")
            for j in range(NPAIR):
                q, m = j % 4, j // 4
                for part in range(2):
                    ins = mm(s[32 * q:32 * q + 32, m * DB:(m + 1) * DB], CP[:, part, j, 0], hs[:, part, j],
                             part == 0, part == 1)
            ins.then_inc(filled, 1)
            s = open_("st")
            tr(s[0:32, 0:P], H[:, NC].rearrange("p a j -> p (a j)")).then_inc(filled, 1)
            for q in range(4):
                s = open_(("sst", q))
                for n in range(8):
                    r = q * 8 + n
                    ins = tr(s[0:DB, n * P:(n + 1) * P], hs[:, r // NPAIR, r % NPAIR])
                ins.then_inc(filled, 1)

            for h in range(NH):
                pe.wait_ge(hank_in[h % 2], 16 * (h // 2 + 1))
                s = open_(("bt", h))
                for c in range(2):
                    ins = mm(s[:, c * 512:(c + 1) * 512], flip[:, :], hank[:, h % 2, c * 512:(c + 1) * 512])
                ins.then_inc(filled, 1)

            def compressed_branch(key):
                if key[0] == "sT":
                    b = key[1]
                    pe.wait_ge(summ_ready, b + 1)
                    s = open_(key)
                    for c in range(2):
                        ins = tr(s[:, c * P:(c + 1) * P], summ[:, b, c * P:(c + 1) * P])
                    ins.then_inc(filled, 1)
                elif key[0] == "sP":
                    b = key[1]
                    read_out(pe, ("sT", b))
                    s = open_(key)
                    mm(s[:, 0:P], pblk[:, 0], sTm[b % 2][:, 0])
                    mm(s[:, P:2 * P], sTm[b % 2][:, 1], pblk[:, 1]).then_inc(filled, 1)
                elif key == "sc":
                    read_out(pe, ("sP", DB - 1))
                    read_out(pe, ("sP", DB - 2))
                    pe.wait_ge(qz_ready, 1)
                    s = open_(key)
                    for b in range(DB):
                        ins = mm(s[0:64, 0:P], qz[:, b], kcTs[:, b], b == 0, b == DB - 1)
                    ins.then_inc(filled, 1)
                elif key == "sps":
                    pe.wait_ge(pc_ready, 1)
                    s = open_(key)
                    mm(s[0:64, 0:P], same[:, :], Pc[0:64]).then_inc(filled, 1)
                elif key == "scT":
                    s = open_(key)
                    tr(s[:, 0:64], Pc[0:64]).then_inc(filled, 1)
                elif key == "sov":
                    read_out(pe, "scT")
                    s = open_(key)
                    for b in range(DB):
                        ins = mm(s[:, b * 8:b * 8 + 8], vcs[:, b], PcT[:, b * 8:b * 8 + 8])
                    ins.then_inc(filled, 1)
                elif key == "ix1":
                    pe.wait_ge(phys_ready, 1)
                    s = open_(key)
                    tr(s[0:SLOTS, 0:64], phys[0:64, 0:SLOTS]).then_inc(filled, 1)
                elif key == "ix2":
                    read_out(pe, "ix1")
                    s = open_(key)
                    mm(s[0:SL, 0:64], spread[:, :], p15[0:SLOTS]).then_inc(filled, 1)

            n_at = len(AT)

            for a in range(n_at + AHEAD + 1):
                if a < n_at:
                    i, h, br, k0, nk = AT[a]
                    lo = 64 * (h % 2)
                    s = open_(("SC", a))
                    if br == 0:
                        for h in range(NH):
                            lo, c = 64 * (h % 2), 512 * (h % 2) + h // 2 * CB
                            ins = mm(s[:, c:c + nk], qT[lo:lo + 64, h // 2, i * P:(i + 1) * P],
                                     kcT[lo:lo + 64, h // GQ, 0:nk])
                    else:
                        n = (br - 1) * NKV + h // GQ
                        if a == 1:
                            pe.wait_ge(k_lo, 1)
                        u = i * NH + h
                        if br == 1:
                            pe.wait_ge(q_lo, u + 1)
                        for c in range(0, nk, 512):
                            w = min(512, nk - c)
                            mm(s[:, c:c + w], qS[:, u % QS], kL[:, n, k0 + c:k0 + c + w], True, False)
                            ins = mm(s[:, c:c + w], qS[:, u % QS], kH[:, n, k0 + c:k0 + c + w], False, True)
                    ins.then_inc(filled, 1)
                t = a - AHEAD
                if 0 <= t < n_at:
                    nk = AT[t][4]
                    pe.wait_ge(exp_ready, t + 1)
                    s = open_(("TR", t))
                    if AT[t][2] == 0:
                        for h in range(NH):
                            c = (h % 2 * 4 + h // 2) * nk
                            ins = tr(s[0:nk, h * P:(h + 1) * P], Pm[:, t % NPM, c:c + nk])
                    else:
                        for c in range(0, nk, P):
                            ins = tr(s[:, c:c + P], Pm[:, t % NPM, c:c + P])
                    ins.then_inc(filled, 1)
                t -= 1
                if t >= 0:
                    i, h, br, k0, nk = AT[t]
                    g = h // GQ
                    read_out(pe, ("TR", t))
                    s = open_(("PV", t))
                    if br == 0:
                        for h in range(NH):
                            g = h // GQ
                            ins = mm(s[:, h * HD:(h + 1) * HD], PT[0:nk, t % 2, h * P:(h + 1) * P],
                                     vc[0:nk, g * HD:(g + 1) * HD])
                    else:
                        tiles, c = nk // P, (br - 1) * P + g * HD
                        for n in range(tiles):
                            ins = mm(s[:, 0:HD], PT[:, t % 2, n * P:(n + 1) * P], vkeep[:, k0 // P + n, c:c + HD],
                                     n == 0, n == tiles - 1)
                    ins.then_inc(filled, 1)
                for key in BETWEEN.get(a, []):
                    compressed_branch(key)

            pe.wait_ge(gelu_ready, 1)
            dense("glu", range(2), [4], lambda k: yF[:, k])

            pe.wait_ge(nbuf_in, 16 * 3 * DB)
            for b in range(DB):
                s = open_(("wT", b))
                for j in range(4):
                    ins = tr(s[:, j * P:(j + 1) * P], nbuf[:, b, j, 0:P])
                ins.then_inc(filled, 1)
            for b in range(DB - 4, DB):
                read_out(pe, ("wT", b))
            s = open_("wS")
            for b in range(DB):
                ins = mm(s[0:64, 0:512], qz[:, b], kTw[:, b], b == 0, b == DB - 1)
            ins.then_inc(filled, 1)
            pe.wait_ge(pw_ready, 1)
            s = open_("wP")
            for j in range(4):
                ins = tr(s[:, j * 64:(j + 1) * 64], Pw[0:64, j * P:(j + 1) * P])
            ins.then_inc(filled, 1)
            read_out(pe, "wP")
            s = open_("wO")
            for b in range(DB):
                for j in range(4):
                    ins = mm(s[:, b * 8:b * 8 + 8], nbuf[:, b, j, P:2 * P], PTw[:, j, b * 8:b * 8 + 8], j == 0, j == 3)
            ins.then_inc(filled, 1)

            for n in range(2 * DB):
                b, g = n // 2, n % 2
                pe.wait_ge(gat[n % 3], 16 * GAT0[n % 3] + 16 * 2 * (n // 3 + 1))
                s = open_(("gT", b, g))
                for r in range(ROWS):
                    c = r * SK if r < 4 else 512 + (r - 4) * SK
                    ins = tr(s[0:HD, c:c + SK], gring[0:SK, n % 3, r * 256 + g * HD:r * 256 + (g + 1) * HD])
                ins.then_inc(filled, 1)
                if n in GLU_AFTER:
                    dense("glu", [GLU_AFTER[n]], [4], lambda k: yF[:, k])
            for n in range(2 * DB - 4, 2 * DB):
                read_out(pe, ("gT", n // 2, n % 2))
            s = open_("gS")
            for b in range(DB):
                for half in range(2):
                    ins = mm(s[0:64, half * 512:half * 512 + 4 * SK], qz[:, b],
                             kTs[:, b, 4 * half:4 * half + 4].rearrange("p r c -> p (r c)"), b == 0, b == DB - 1)
            ins.then_inc(filled, 1)
            pe.wait_ge(pw_ready, 2)
            s = open_("gP")
            for r in range(ROWS):
                ins = tr(s[0:SK, r * 64:(r + 1) * 64], Ps[0:64, r])
            ins.then_inc(filled, 1)
            read_out(pe, "gP")
            pe.wait_ge(vs_ready, 2 * DB)
            s = open_("gO")
            for n in range(2 * DB):
                b, g = n // 2, n % 2
                c = b * 8 + 4 * g
                for r in range(ROWS):
                    ins = mm(s[64 * g:64 * g + 64, c:c + 4], Vs[0:SK, n, r], PTs[0:SK, r, c:c + 4],
                             r == 0, r == ROWS - 1)
            ins.then_inc(filled, 1)
            read_out(pe, "sov")
            read_out(pe, "wO")
            read_out(pe, "gO")
            for key, brs in (("oT0", (0, 1)), ("oT1", (2,))):
                s = open_(key)
                for br in brs:
                    for h in range(NH):
                        g = h // GQ
                        c = g * 512 + (br % 2) * 256 + (h % GQ) * HD
                        ins = tr(s[0:DB, c:c + HD],
                                 osT[64 * g:64 * g + 64, br].rearrange("p (b h) -> p h b", h=NH)[:, h])
                ins.then_inc(filled, 1)

            for i in range(NT + 1):
                n = token_tile(i)[1]
                pe.wait_ge(on_ready, i + 1)
                s = open_(("n0", i))
                for k in range(4):
                    src = oN[:, i, k * P:(k + 1) * P] if i < NT else oS[0:DB, 0, k * P:(k + 1) * P]
                    ins = tr(s[:, k * P:k * P + n], src)
                ins.then_inc(filled, 1)
            pe.wait_ge(sq_ready, 1)
            for c in range(2):
                s = open_(("ss", c))
                for n in range(2 - c):
                    for k in range(4):
                        c0 = (2 * c + n) * CH
                        ins = mm(chunked(("ss", c))[:, n], ones[:, :], SQ[:, k, c0:c0 + CH], k == 0, k == 3)
                ins.then_inc(filled, 1)
            for m in range(8):
                item[0] += 1
                pe.wait_ge(w_lo, m + 1)
                a, b = ("wo", m, 0), ("wo", m, 1)
                open_(a)
                open_(b)
                outs = [chunked(a)[:, 0], chunked(a)[:, 1], chunked(b)[:, 0]]
                for k in range(KD):
                    if m == 0 and (k == 0 or k >= 4):
                        pe.wait_ge(m_lo, 1 if k == 0 else k - 2)
                    exact_products(outs, wHm[m % 2][:, k * P:(k + 1) * P], wLm[m % 2][:, k * P:(k + 1) * P],
                                   mH[:, k], mL[k], k == 0, k == KD - 1)

            def residual(n):
                for m in (6, 7):
                    for c in range(2):
                        read_out(pe, ("wf", NGRP - 1, m, c) if n == 3 else ({1: "wo", 2: "xo"}[n], m, c))
                for i in range(NT + 3 if n < 3 else NT + 1):
                    if i <= NT:
                        c0, r = token_tile(i)
                        s = open_((f"b{n}", i))
                        for k in range(KD):
                            ins = tr(s[0:r, k * P:(k + 1) * P], yT[:, k, c0:c0 + r])
                        ins.then_inc(filled, 1)
                    if i >= 2 and n < 3:
                        c0, r = token_tile(i - 2)
                        pe.wait_ge(res_norm, (n - 1) * (NT + 1) + i - 1)
                        s = open_((f"f{n}", i - 2))
                        for k in range(KD):
                            ins = tr(s[:, k * P:k * P + r], tb[0:r, i % 2, k * P:(k + 1) * P])
                        ins.then_inc(filled, 1)

            residual(1)

            pe.wait_ge(mkv_in, 16)
            s = open_("mT")
            for h in range(XH):
                for i in range(2):
                    ins = tr(s[:, (2 * h + i) * P:(2 * h + i + 1) * P], mkv[:, i, h * P:(h + 1) * P])
            ins.then_inc(filled, 1)
            for i in range(NT - 3, NT + 1):
                read_out(pe, ("f1", i))
            dense("xq", range(4), [KD], lambda k: hT[:, k])

            for b in range(DB):
                pe.wait_ge(kst_in[b % 2], 16 * (b // 2 + 1))
                s = open_(("xT", b))
                for h in range(XH):
                    for i in range(2):
                        ins = tr(s[:, (2 * h + i) * P:(2 * h + i + 1) * P], kst[:, b % 2, i, h * P:(h + 1) * P])
                ins.then_inc(filled, 1)
            for b in range(DB - 4, DB):
                read_out(pe, ("xT", b))
            pe.wait_ge(qxz_ready, 1)
            s = open_("xS")
            for b in range(DB):
                for h in range(XH):
                    ins = mm(s[0:32, 0:NM], qxz[:, h, b], kTm[:, b, h], b + h == 0, b + h == DB + XH - 2)
            ins.then_inc(filled, 1)
            pe.wait_ge(px_ready, 1)
            s = open_("xP")
            for i in range(2):
                ins = tr(s[:, i * 32:(i + 1) * 32], Pxs[0:32, i * P:(i + 1) * P])
            ins.then_inc(filled, 1)
            read_out(pe, "xP")
            pe.wait_ge(vm_in, 16 * DB)
            s = open_("xO")
            for b in range(DB):
                for h in range(XH):
                    for i in range(2):
                        ins = mm(s[:, h * DB + b:h * DB + b + 1], Vm[:, b, i, h * P:(h + 1) * P],
                                 PTxs[:, i, b * XH + h:b * XH + h + 1], i == 0, i == 1)
            ins.then_inc(filled, 1)

            read_out(pe, "mT")
            for i in range(NT + 3):
                if i < NT:
                    s = open_(("XS", i))
                    for h in range(XH):
                        ins = mm(s[:, h * NM:(h + 1) * NM], q2T[:, h, i * P:(i + 1) * P], mkT[:, h])
                    ins.then_inc(filled, 1)
                if 2 <= i < NT + 2:
                    t = i - 2
                    pe.wait_ge(px_ready, t + 2)
                    s = open_(("XT", t))
                    for c in range(8):
                        ins = tr(s[:, c * P:(c + 1) * P], Px[:, t % 3, c * P:(c + 1) * P])
                    ins.then_inc(filled, 1)
                if i >= 3:
                    t = i - 3
                    read_out(pe, ("XT", t))
                    s = open_(("XO", t))
                    for h in range(XH):
                        for c in range(2):
                            ins = mm(s[:, h * P:(h + 1) * P], mkv[:, c, 512 + h * P:512 + (h + 1) * P],
                                     PTx[:, t % 2, (2 * h + c) * P:(2 * h + c + 1) * P], c == 0, c == 1)
                    ins.then_inc(filled, 1)
            read_out(pe, "xO")
            for i in range(NT - 2, NT):
                read_out(pe, ("XO", i))
            dense("xo", range(8), [4], lambda k: q2T[:, k])
            residual(2)

            pe.wait_ge(h_lo, NT + 1)
            for it, tile in enumerate(ffn):
                pe.wait_ge(w_lo, NWO + it + 1)
                wh, wl = wH[it % 2], wL[it % 2]
                if tile[0] != "o":
                    a, b = tile + (0,), tile + (1,)
                    open_(a)
                    open_(b)
                    outs = [chunked(a)[:, 0], chunked(a)[:, 1], chunked(b)[:, 0]]
                    for k in range(KD):
                        exact_products(outs, wh[:, k * P:(k + 1) * P], wl[:, k * P:(k + 1) * P],
                                       hH[:, k], hL[:, k], k == 0, k == KD - 1)
                    continue
                grp, m0 = tile[1:]
                tiles = group_tiles(grp)
                outs = []
                for m in (m0, m0 + 1):
                    a, b = ("wf", grp, m, 0), ("wf", grp, m, 1)
                    open_(a)
                    open_(b)
                    outs.append([chunked(a)[:, 0], chunked(a)[:, 1], chunked(b)[:, 0]])
                    if m == m0 and len(tiles) > 1:
                        pe.wait_ge(g_lo, tiles[-1])
                    for n in range(len(tiles) - 1):
                        c = n * 2 * P + (m - m0) * P
                        exact_products(outs[-1], wh[:, c:c + P], wl[:, c:c + P], gH[:, n], gL[:, n], n == 0, False)
                pe.wait_ge(g_lo, tiles[-1] + 1)
                n = len(tiles) - 1
                for m in range(2):
                    c = n * 2 * P + m * P
                    exact_products(outs[m], wh[:, c:c + P], wl[:, c:c + P], gH[:, n], gL[:, n], n == 0, True)
            residual(3)

        @block.gpsimd
        def _(pool):
            own = Own(pool, pool_own)
            g = nc.gpsimd

            own.step(g.memset(ident[:, :], 0.0))
            own.step(g.memset(flip[:, :], 0.0))
            own.step(g.memset(same[:, :], 1.0))
            own.step(g.memset(block_of[:, :], 1.0))
            own.step(g.memset(spread[:, :], 0.0))
            own.step(g.memset(qz[:, :, :], 0.0))
            g.memset(pblk[:, :, :], 0.0).then_inc(pblk_zero, 1)
            own.settle()
            g.affine_select(out=ident[:, :], in_=ident[:, :], compare_op=ALU.not_equal, fill=1.0, base=0,
                            pattern=[[-1, P]], channel_multiplier=1).then_inc(consts, 1)
            own.step(g.memset(ones[:, :], 1.0))
            g.affine_select(out=flip[:, :], in_=flip[:, :], compare_op=ALU.not_equal, fill=1.0, base=1 - P,
                            pattern=[[1, P]], channel_multiplier=1).then_inc(consts, 1)
            own.step(g.affine_select(out=same[:, :], in_=same[:, :], compare_op=ALU.is_ge, fill=0.0, base=0,
                                     pattern=[[-4, 16], [0, 4]], channel_multiplier=1))
            own.step(g.affine_select(out=block_of[:, :], in_=block_of[:, :], compare_op=ALU.is_ge, fill=0.0, base=0,
                                     pattern=[[-CB, 4]], channel_multiplier=1))
            own.step(g.iota(tiny[:, 0:1], pattern=[[0, 1]], base=0, channel_multiplier=1))
            own.step(g.iota(jota_i[:, :], pattern=[[1, 64]], base=0, channel_multiplier=0))
            own.settle()
            own.step(g.affine_select(out=same[:, :], in_=same[:, :], compare_op=ALU.is_ge, fill=0.0, base=3,
                                     pattern=[[4, 16], [0, 4]], channel_multiplier=-1))
            own.step(g.affine_select(out=spread[:, :], in_=spread[:, :], compare_op=ALU.not_equal, fill=1.0, base=0,
                                     pattern=[[-1, SLOTS], [0, LINES]], channel_multiplier=1))
            g.affine_select(out=block_of[:, :], in_=block_of[:, :], compare_op=ALU.is_ge, fill=0.0, base=CB - 1,
                            pattern=[[CB, 4]], channel_multiplier=-1).then_inc(consts, 1)
            own.settle()
            g.memset(eps_c[:, :], EPS).then_inc(consts, 1)

            pool.wait_ge(params, 16 * PARAM_DMAS)
            g.tensor_copy(dtrow[0:NPAIR].rearrange("j (a p) -> j a p", a=2),
                          dt2[:, :].unsqueeze(2).to_broadcast([NPAIR, 2, 64])).then_inc(consts, 1)

            pool.wait_ge(tab_in, 16)
            own.then(g.tensor_scalar(tab[:, :], tab[:, :], 1.0 / SC, None, ALU.mult))
            for bucket, d0, d1 in bucket_ranges():
                own.step(g.tensor_copy(V8[0:NH, T - 1 - d1:T - d0],
                                       tab[:, bucket:bucket + 1].to_broadcast([NH, d1 - d0 + 1])))
            own.step(g.memset(V8[0:NH, T:VL], NEG))
            own.settle()
            pool.dma_start(bias_dram, V8[0:NH]).then_inc(v8_out, 16)
            pool.wait_ge(v8_out, 16)
            pool.dma_start(V64[:, :], bass.AP(bias_dram.tensor, T - 1 - WIN, [[0, DB], [VL, NH], [1, WIN + 1]]))\
                .then_inc(V64_in, 16)

            for i in range(NT + 1):
                pool.wait_ge(kv_ready, i + 1)
                if i < NT:
                    rows = slice(i * P, (i + 1) * P)
                    k = kvst[:, i % 2]
                    done = kv_stored[i % 2]
                    pool.dma_start(p_kv_cmp[0, 0, rows].rearrange("s c g d -> s (c g d)"), k[:, 0:256]).then_inc(done, 16)
                    pool.dma_start(p_kv_sel[0, 0, rows].rearrange("s c g d -> s (c g d)"), k[:, 256:512]).then_inc(done, 16)
                    if i >= NT - WIN // P:
                        w = slice(i * P - (T - WIN), (i + 1) * P - (T - WIN))
                        pool.dma_start(p_kv_win[0, 0, w].rearrange("s c g d -> s (c g d)"), k[:, 512:768]).then_inc(done, 16)
                else:
                    pool.dma_start(s_kv_cmp[0, :, 0].rearrange("b c g d -> b (c g d)"), kvS[0:DB, 0:256]).then_inc(rows_saved, 16)
                    pool.dma_start(s_kv_sel[0, :, 0].rearrange("b c g d -> b (c g d)"), kvS[0:DB, 256:512]).then_inc(rows_saved, 16)
                    pool.dma_start(sel_row, kvS[0:DB, 256:512]).then_inc(rows_saved, 16)
                    pool.dma_start(win_row, kvS[0:DB, 512:768]).then_inc(rows_saved, 16)

            for c in range(4, 8):
                read_out(pool, ("mk", c))
            pool.dma_start(p_mem_kv[0, 0].rearrange("(i p) c h d -> p i (c h d)", p=P), mkv_new).then_inc(mkv_out, 16)

            pool.wait_ge(k_hi, 1)
            g.tensor_tensor(kL, kTd, kH, ALU.subtract).then_inc(k_lo, 1)

            pool.wait_ge(pline_ready, 1)
            pool_c = cache_kv_cmp[0].rearrange("n (a r) c g d -> (n a) (r c g d)", r=ROWS)
            pool.wait_ge(mkv_out, 16)

            def past_line(n):
                if n >= 3:
                    pool.wait_ge(gat_used, n - 2)
                pool.indirect_dma_start(out=gring[:, n % 3], out_offset=None, in_=pool_c,
                                        in_offset=bass.IndirectOffsetOnAxis(ap=pline[:, n // DB, n % DB:n % DB + 1], axis=0))\
                    .then_inc(gat[n % 3], 16)

            def weigh_line(n):
                k, b = n // DB, n % DB
                if n + 1 < 4 * DB:
                    past_line(n + 1)
                if b == 0:
                    if k:
                        pool.wait_ge(weighted, n)
                    for c in range(2):
                        pool.dma_start(posB[:, :, c * HD:(c + 1) * HD],
                                       bass.AP(cmp_pos.tensor, (c * CB + k * ROWS) * HD,
                                               [[0, P], [HD, ROWS], [1, HD]])).then_inc(posB_in, 16)
                    pool.wait_ge(posB_in, 32 * (k + 1))
                pool.wait_ge(gat[n % 3], 16 * (n // 3 + 1))
                r = gring[:, n % 3].rearrange("p (r c g d) -> p (r c) g d", r=ROWS, c=2, g=2)
                g.tensor_tensor(r, r, posB.rearrange("p r (c d) -> p (r c) d", c=2).unsqueeze(2)
                                .to_broadcast([P, 2 * ROWS, NKV, HD]), ALU.mult).then_inc(weighted, 1)

            past_line(0)
            for n in range(2):
                weigh_line(n)

            full(pool, "ys")
            for h in range(NH):
                if h >= 2:
                    full(pool, ("bt", h - 2))
                pool.dma_start(hank[:, h % 2], bass.AP(bias_dram.tensor, h * VL, [[1, P], [1, T]]))\
                    .then_inc(hank_in[h % 2], 16)
            pool.wait_ge(states_staged, 1)
            pool.dma_start(p_ssm_re[0, 0].rearrange("(j a) p -> j (a p)", a=2), st_rows[0:NPAIR]).then_inc(states_out, 16)
            pool.dma_start(p_ssm_im[0, 0].rearrange("(j a) p -> j (a p)", a=2), st_rows[NPAIR:2 * NPAIR]).then_inc(states_out, 16)
            pool.wait_ge(states_staged, 2)
            pool.dma_start(s_ssm_re[0].rearrange("b g p -> b (g p)"), sst_rows[0:DB, 0:2048]).then_inc(states_out, 16)
            pool.dma_start(s_ssm_im[0].rearrange("b g p -> b (g p)"), sst_rows[0:DB, 2048:4096]).then_inc(states_out, 16)
            read_out(pool, ("bt", NH - 1))
            for h in range(NH):
                g.affine_select(out=far[:, h], in_=BT[:, h, T - P - WIN:T - WIN], compare_op=ALU.is_gt, fill=NEG,
                                base=0, pattern=[[1, P]], channel_multiplier=-1).then_inc(far_ready, 1)

            for n in range(2, 4 * DB):
                weigh_line(n)

            pool_s = cache_kv_sel[0].rearrange("n (a r) c g d -> (n a) (r c g d)", r=ROWS)

            def gather(n):
                b, gg = n // 2, n % 2
                col = b * 8 + 4 * gg
                pool.indirect_dma_start(out=gring[0:SL, n % 3], out_offset=None, in_=pool_s,
                                        in_offset=bass.IndirectOffsetOnAxis(ap=line[:, col:col + 1], axis=0))\
                    .then_inc(gat[n % 3], 16)
                pool.dma_start(gring[SL:SK, n % 3, 0:256], sel_row[b:b + 1]).then_inc(gat[n % 3], 16)

            pool.wait_ge(line_ready, 1)
            pool.wait_ge(gat_used, 4 * DB)
            for n in range(3):
                gather(n)

            last = len(AT) - 1
            for a in range(last - 3, last + 1):
                read_out(pool, ("SC", a))
            pool.wait_ge(rows_saved, 64)
            for b in range(DB):
                pool.dma_start(nbuf[0:P - 1, b].rearrange("p r c -> p (r c)"),
                               bass.AP(cache_kv_win.tensor, (b * WIN + 1) * 256, [[1024, P - 1], [1, 1024]])).then_inc(nbuf_in, 16)
                pool.dma_start(nbuf[P - 1:P, b, 0:3].rearrange("p r c -> p (r c)"),
                               bass.AP(cache_kv_win.tensor, (b * WIN + WIN - 3) * 256, [[768, 1], [1, 768]])).then_inc(nbuf_in, 16)
                pool.dma_start(nbuf[P - 1:P, b, 3], win_row[b:b + 1]).then_inc(nbuf_in, 16)
            pool.wait_ge(nbuf_in, 16 * 3 * DB)
            for b in range(DB):
                pool.dma_start(s_kv_win[0, b].rearrange("(p r) c g d -> p (r c g d)", r=4),
                               nbuf[:, b].rearrange("p r c -> p (r c)")).then_inc(win_stored, 16)
            for n in range(3, 2 * DB):
                full(pool, ("gT", (n - 3) // 2, (n - 3) % 2))
                pool.wait_ge(vs_ready, n - 2)
                gather(n)

            full(pool, ("gT", DB - 1, 1))
            pool.wait_ge(vs_ready, 2 * DB)
            pool.wait_ge(mkv_out, 16)
            pool.dma_start(mkv, p_mem_kv[0, 0].rearrange("(i p) c h d -> p i (c h d)", p=P)).then_inc(mkv_in, 16)
            full(pool, ("f1", NT))
            g.memset(qxz, 0.0).then_inc(qxz_zero, 1)
            for b in range(DB):
                if b >= 2:
                    full(pool, ("xT", b - 2))
                kv = cache_mem_kv[0, b].rearrange("(i p) c h d -> p i c (h d)", p=P)
                pool.dma_start(kst[:, b % 2], kv[:, :, 0]).then_inc(kst_in[b % 2], 16)
            full(pool, ("xq", XH - 1, 1))
            for b in range(DB):
                kv = cache_mem_kv[0, b].rearrange("(i p) c h d -> p i c (h d)", p=P)
                pool.dma_start(Vm[:, b], kv[:, :, 1]).then_inc(vm_in, 16)
            for i in range(NT + 1):
                n = token_tile(i)[1]
                pool.wait_ge(out_ready, i + 1)
                dst = y_prompt[0, i * P:(i + 1) * P] if i < NT else y_sample[:, 0]
                pool.dma_start(dst, x1[0:n, i]).then_inc(stored, 16)
            pool.wait_ge(stored, 16 * (NT + 1))
            pool.wait_ge(mkv_out, 16)
            pool.wait_ge(win_stored, 16 * DB)
            pool.wait_ge(states_out, 64)
            pool.wait_ge(rows_saved, 64)
            pool.wait_ge(kv_stored[0], 16 * (2 * 4 + 2))
            pool.wait_ge(kv_stored[1], 16 * (2 * 4 + 2))

        @block.scalar
        def _(act):
            own = Own(act, act_own)
            a_ = nc.scalar

            def f(out, in_, func=ACT.Copy, **kw):
                return a_.activation(out, in_, func, **kw)

            ng = norm_g[0].rearrange("n (k p) -> (n k) p", p=P)
            act.dma_start(prow[0:48], ng).then_inc(params, 16)
            act.dma_start(prow[48:56], grp_norm_g[0].rearrange("(k p) -> k p", p=P)).then_inc(params, 16)
            act.dma_start(prow[56:64], mem_norm_g[0].rearrange("(k p) -> k p", p=P)).then_inc(params, 16)
            act.dma_start(prow[64:68], glu_b[0].rearrange("(k p) -> k p", p=P)).then_inc(params, 16)
            act.dma_start(prow[68:72], ssm_d[0].rearrange("(k p) -> k p", p=P)).then_inc(params, 16)
            act.dma_start(prow[72:88], ssm_a_re[0].rearrange("(j a) p -> j (a p)", a=2)).then_inc(params, 16)
            act.dma_start(prow[88:104], ssm_a_im[0].rearrange("(j a) p -> j (a p)", a=2)).then_inc(params, 16)
            act.dma_start(dt2[:, :], ssm_log_dt[0].rearrange("(j a) -> j a", a=2)).then_inc(params, 16)
            act.dma_start(drow[0:NPAIR].rearrange("j (l c) -> j l c", l=L4),
                          bass.AP(ssm_d.tensor, 0, [[32, NPAIR], [0, L4], [1, 32]])).then_inc(params, 16)
            with nc.allow_non_contiguous_dma(reason="a table of 32 by 8, transposed"):
                act.dma_start(tab[:, :], rel_bias.rearrange("b h -> h b")).then_inc(tab_in, 16)
            for n in range(4):
                for c in range(2):
                    act.dma_start(posP[32 * n:32 * n + 32, c * P:(c + 1) * P].rearrange("l (g d) -> l g d", g=2),
                                  bass.AP(cmp_pos.tensor, c * CB * HD, [[HD, CB], [0, NKV], [1, HD]])).then_inc(pos_in, 16)
            act.wait_ge(pblk_zero, 1)
            for c in range(2):
                for h in range(2):
                    act.dma_start(pblk[64 * h:64 * h + 64, c, 64 * h:64 * h + 64], cmp_proj[0, c]).then_inc(pos_in, 16)
            with nc.allow_non_contiguous_dma(reason="page numbers, one for each compressed block"):
                for b in range(DB):
                    act.dma_start(ptc[:, b:b + 1], bass.AP(page_table.tensor, b * NPAGE, [[1, NPAGE], [0, 4], [1, 1]])).then_inc(pt_in, 16)
            act.dma_start(ptrow[:, :], bass.AP(page_table.tensor, 0, [[NPAGE, DB], [0, NH], [1, NPAGE]])).then_inc(pt_in, 16)

            act.wait_ge(consts, 4)

            def mean_square(i):
                n = token_tile(i)[1]
                act.wait_ge(x_in[i % 2], 16 * (i // 2 + 1))
                own.then(f(junk[0:n], xin[0:n, i % 2], ACT.Square, accum_out=st[0:n, i:i + 1]))
                f(st[0:n, 16 + i:17 + i], st[0:n, i:i + 1], ACT.Sqrt, scale=1.0 / D, bias=eps_c[0:n]).then_inc(rt_ready, 1)

            for i in range(3):
                mean_square(i)
            act.wait_ge(s5_arg, 1)
            f(prm[:, 0], cols[:, 104:120], ACT.Exp).then_inc(s5_fun, 1)
            act.wait_ge(s5_arg, 2)
            f(prm[:, 2], prm[:, 1], ACT.Exp).then_inc(s5_fun, 1)
            own.step(f(prm[:, 5], prm[:, 4], ACT.Sin))
            f(prm[:, 7], prm[:, 6], ACT.Sin).then_inc(s5_fun, 1)


            for i in range(NT + 1):
                n = token_tile(i)[1]
                full(act, ("kv", i))
                if i < NT:
                    if i >= 2:
                        u = i // 2
                        act.wait_ge(kv_stored[i % 2], 16 * (2 * u + max(0, u - 2)))
                        act.wait_ge(prod_ready, i - 1)
                        full(act, ("kT", i - 2))
                    dst = kvst[:, i % 2, 0:KVC]
                else:
                    dst = kvS[0:DB]
                f(dst, slot(("kv", i))[0:n, 0:KVC]).then_inc(kv_ready, 1)
                free(f(gates[0:n, i], slot(("kv", i))[0:n, KVC:KVC + NG], ACT.Sigmoid), ("kv", i))
                if i + 3 <= NT:
                    mean_square(i + 3)
                if i >= 1:
                    kt = i - 1
                    key = ("kT", kt)
                    full(act, key)
                    s = slot(key)[:, 0:256].rearrange("p (a t) -> p a t", a=2)
                    for half in range(2):
                        for g in range(NKV):
                            own.step(f(kTd[64 * half:64 * half + 64, g::NKV, kt * P:(kt + 1) * P], s[64 * g:64 * g + 64]))
                    free(f(csum[:, :, 4 * kt:4 * kt + 4], slot(key)[:, 256:264].rearrange("p (a t) -> p a t", a=2)), key)
            full(act, "cproj")
            for half in range(2):
                for g in range(NKV):
                    own.step(f(kcT[64 * half:64 * half + 64, g], slot("cproj")[64 * g:64 * g + 64, 0:32]))
            free(f(vc[:, :], slot("cproj")[0:32, 32:32 + P]), "cproj")

            with nc.allow_non_contiguous_dma(reason="rows of 16 numbers"):
                for part, src in enumerate((ssm_b_re, ssm_b_im)):
                    act.dma_start(braw[:, part], src[0].rearrange("(j a) p i -> (a p) j i", a=2)).then_inc(b_in, 16)
            for part, src in enumerate((ssm_c_re, ssm_c_im)):
                act.dma_start(craw[:, 4 * part:4 * part + 4],
                              src[0].rearrange("(q g) i p -> (g i) q p", g=8)).then_inc(c_in, 16)
            for part, src in enumerate((state_ssm_re, state_ssm_im)):
                act.dma_start(h0row[0:DB, part], src[0].rearrange("b g p -> b (g p)")).then_inc(c_in, 16)
            full(act, "C")
            for half in range(2):
                for part in range(2):
                    s = slot("C")[0:HD, part * 512:part * 512 + 512]\
                        .rearrange("p (q g i) -> p q g i", g=2, i=16)[:, :, half]
                    ins = f(cc[64 * half:64 * half + 64, part], s)
                    free(ins, "C") if half and part else own.step(ins)
            full(act, "h0")
            act.wait_ge(kv_stored[0], 16 * (2 * 4 + 2))
            act.wait_ge(kv_stored[1], 16 * (2 * 4 + 2))
            free(f(h0T.rearrange("p a j b -> p (a j b)"), slot("h0")[:, 0:2 * NPAIR * DB]), "h0")

            def dense_out(stage, m, dst):
                for c in range(2):
                    key = (stage, m, c)
                    full(act, key)
                    if c == 0:
                        ins = f(dst[:, 0:2 * CH].rearrange("p (a n) -> p a n", a=2), chunked(key))
                    else:
                        ins = f(dst[:, 2 * CH:TC], chunked(key)[:, 0])
                    free(ins, key)

            for m in range(8):
                if m >= 6:
                    act.wait_ge(uT_ready, m - 5)
                dense_out("in", m, qT[:, m] if m < 4 else uTm[:, m % 2])

            def s5_out(j):
                key = ("SA", j)
                full(act, key)
                if j >= 2:
                    full(act, ("SB", j - 2))
                s = slot(key)
                own.step(f(Wm[j % 2].rearrange("p a c -> p (a c)"), s[:, 0:256]))
                for l in range(L4):
                    ins = f(Tm[j % 2][32 * l:32 * l + 32, 32 * l:P], s[32 * l:32 * l + 32, 512 + 32 * l:640])
                    free(ins, key) if l == L4 - 1 else own.step(ins)

            act.wait_ge(s5_built, 1)
            act.dma_start(mrow, mem_prompt[0].rearrange("(i p) d -> p i d", p=P)).then_inc(mem_in, 16)
            for j in range(NPAIR):
                s5_out(j)
                if j == 8:
                    act.wait_ge(mem_in, 16)
                    for i in range(2):
                        own.then(f(junk2, mrow[:, i], ACT.Square, accum_out=st[:, i:i + 1]))
                        f(st[:, 16 + i:17 + i], st[:, i:i + 1], ACT.Sqrt, scale=1.0 / D, bias=eps_c[:, :]).then_inc(mem_stat, 1)
            for c in range(8):
                full(act, ("mk", c))
                free(f(mkv_new[:, :, c * P:(c + 1) * P], slot(("mk", c))[:, 0:256].rearrange("p (i n) -> p i n", i=2)), ("mk", c))
            full(act, ("mk", 7))
            own.settle()
            f(kH, kTd).then_inc(k_hi, 1)


            full(act, "st")
            own.step(f(st_rows[0:32], slot("st")[0:32, 0:P]))
            free(f(tinyf[0:32, 8:9], slot("st")[0:32, 0:1]), "st")
            act.wait_ge(own.sem, own.n)
            act.sem_inc(states_staged, 1)
            for q_ in range(4):
                key = ("sst", q_)
                full(act, key)
                free(f(sst_rows[0:DB, q_ * D:(q_ + 1) * D], slot(key)[0:DB]), key)
            for q_ in range(4):
                read_out(act, ("sst", q_))
            act.sem_inc(states_staged, 1)

            for h in range(NH):
                full(act, ("bt", h))
                free(f(BT[:, h], slot(("bt", h))), ("bt", h))

            def softmax_rows(n, src_ready, stat, x, s, scale=SC):
                act.wait_ge(src_ready, n)
                f(x, x, ACT.Exp, bias=st[0:s, 33:34], scale=scale, accum_out=st[0:s, 34:35]).then_inc(stat, 1)

            def compressed_branch(key):
                if key[0] == "sT":
                    b = key[1]
                    full(act, key)
                    if b >= 2:
                        full(act, ("sP", b - 2))
                    free(f(sTm[b % 2].rearrange("p a c -> p (a c)"), slot(key)[:, 0:256]), key)
                elif key[0] == "sP":
                    b = key[1]
                    full(act, key)
                    own.step(f(kcTs[:, b], slot(key)[:, 0:P]))
                    free(f(vcs[:, b], slot(key)[:, P:2 * P]), key)
                elif key == "sps":
                    softmax_rows(1, pw_raw, pw_exp, Pc[0:64], 64)
                elif key == "scT":
                    full(act, key)
                    free(f(PcT, slot(key)[:, 0:64]), key)
                elif key == "sov":
                    full(act, key)
                    free(f(osT[:, 0], slot(key)[:, 0:64]), key)
                elif key == "ix1":
                    full(act, key)
                    free(f(p15[0:SLOTS], slot(key)[0:SLOTS, 0:64]), key)

            def weights_hi(n):
                item, it = split[n]
                act.wait_ge(w_loaded[it % NS], 16 * (it // NS + 1))
                if n >= 2:
                    full(act, last_unit(split[n - 2][0]))
                size = group_size(item)
                f(parts_at(n)[0][:, 0:size], wRaw[:, it % NS, 0:size]).then_inc(w_hi, 1)

            act.wait_ge(y_ready, 1)
            f(yF, yF, ACT.Gelu_apprx_tanh).then_inc(gelu_ready, 1)

            act.wait_ge(states_out, 64)
            n_at = len(AT)
            def queries_hi(u):
                i, h = u // NH, u % NH
                lo = 64 * (h % 2)
                if u >= QS:
                    full(act, ("SC", unit_number((u - QS) // NH, (u - QS) % NH, 2)))
                f(qS[lo:lo + 64, u % QS], qT[lo:lo + 64, h // 2, i * P:(i + 1) * P]).then_inc(q_hi, 1)

            for u in range(2):
                queries_hi(u)
            for a in range(n_at + AHEAD + 1):
                if a < n_at:
                    i, h, br, _, nk = AT[a]
                    if br == 1 and i * NH + h + 2 < NT * NH:
                        queries_hi(i * NH + h + 2)
                if a < n_at and br == 0:
                    act.wait_ge(c_raw, i + 1)
                    f(Pm[:, a % NPM, 0:NH * nk], Pm[:, a % NPM, 0:NH * nk], ACT.Exp, scale=SC).then_inc(exp_ready, 1)
                elif a < n_at:
                    r = a % 8 + (40 if br == 2 and i >= 4 else 0)
                    read_out(act, ("SC", a))
                    f(Pm[:, a % NPM, 0:nk], Pm[:, a % NPM, 0:nk], ACT.Exp, bias=st[:, r:r + 1], scale=-1.0,
                      accum_out=st[:, 16 + a % 8:17 + a % 8]).then_inc(exp_ready, 1)
                t = a - AHEAD
                if 0 <= t < n_at:
                    key, nk = ("TR", t), AT[t][4]
                    full(act, key)
                    if t >= 2:
                        full(act, ("PV", t - 2))
                    rows, w = (nk, NH * P) if AT[t][2] == 0 else (P, nk)
                    free(f(PT[0:rows, t % 2, 0:w], slot(key)[0:rows, 0:w]), key)
                for key in BETWEEN.get(a, []):
                    compressed_branch(key)


            def glu_out(m):
                for c in range(2):
                    key = ("glu", m, c)
                    full(act, key)
                    if c == 0:
                        ins = f(oF[:, m, 0:2 * CH].rearrange("p (a n) -> p a n", a=2), chunked(key), ACT.Sigmoid,
                                bias=cols[:, 64 + m:65 + m])
                    else:
                        ins = f(oF[:, m, 2 * CH:TC], chunked(key)[:, 0], ACT.Sigmoid, bias=cols[:, 64 + m:65 + m])
                    free(ins, key)

            for m in range(2):
                glu_out(m)

            for b in range(DB):
                full(act, ("wT", b))
                free(f(kTw[:, b], slot(("wT", b))[:, 0:512]), ("wT", b))
            softmax_rows(2, pw_raw, pw_exp, Pw[0:64], 64)
            full(act, "wP")
            free(f(PTw.rearrange("p a c -> p (a c)"), slot("wP")[:, 0:256]), "wP")
            full(act, "wO")
            free(f(osT[:, 2], slot("wO")[:, 0:64]), "wO")
            for n in range(2 * DB):
                b, g = n // 2, n % 2
                key = ("gT", b, g)
                full(act, key)
                s = slot(key)[0:HD].rearrange("p (a x) -> p a x", a=2)[:, :, 0:4 * SK]
                free(f(kTs[64 * g:64 * g + 64, b].rearrange("p (a r) c -> p a (r c)", a=2), s), key)
                if n in GLU_AFTER:
                    glu_out(GLU_AFTER[n])
            softmax_rows(3, pw_raw, pw_exp, Ps[0:64].rearrange("p a c -> p (a c)"), 64)
            full(act, "gP")
            free(f(PTs[0:SK].rearrange("p a c -> p (a c)"), slot("gP")[0:SK, 0:512]), "gP")
            full(act, "gO")
            free(f(osT[:, 1], slot("gO")[:, 0:64]), "gO")

            act.wait_ge(oS_ready, 1)
            for i in range(NT + 1):
                n = token_tile(i)[1]
                src = oN[:, i] if i < NT else oS[0:DB, 0]
                own.then(f(scr[0:n], src, ACT.Square, accum_out=st[0:n, i:i + 1]))
                f(st[0:n, 16 + i:17 + i], st[0:n, i:i + 1], ACT.Sqrt, scale=1.0 / 512, bias=eps_c[0:n]).then_inc(on_stat, 1)

            act.wait_ge(oF_ready, 1)
            f(SQ, oF, ACT.Square).then_inc(sq_ready, 1)
            for i in range(NT + 1):
                read_out(act, ("n0", i))
            f(mH[:, 0:4], mRaw[0]).then_inc(m_hi, 1)
            weights_hi(0)
            for c in range(2):
                key = ("ss", c)
                full(act, key)
                if c == 0:
                    ins = f(RS[:, 0:2 * CH].rearrange("p (a n) -> p a n", a=2), chunked(key), ACT.Sqrt,
                            scale=1.0 / 512, bias=eps_c[:, :])
                else:
                    ins = f(RS[:, 2 * CH:TC], chunked(key)[:, 0], ACT.Sqrt, scale=1.0 / 512, bias=eps_c[:, :])
                free(ins, key)
            def input_hi(i):
                c0, r = token_tile(i)
                read_out(act, ("f2", i))
                f(hH[:, :, c0:c0 + r], hRaw[:, :, c0:c0 + r]).then_inc(h_hi, 1)

            def residual(n):
                for m in range(8 if n < 3 else 0):
                    if n == 1 and m + 1 < NWO:
                        weights_hi(m + 1)
                    if m == 0 and n == 1:
                        for k in range(4):
                            act.wait_ge(m_ready, 1 + k)
                            f(mH[:, 4 + k], mRaw[1 + k]).then_inc(m_hi, 1)
                    dense_out({1: "wo", 2: "xo"}[n], m, yT[:, m])
                    if m == 1 and n == 1:
                        for i in range(NT + 1):
                            c0, r = token_tile(i)
                            src = x_prompt[0, c0:c0 + r] if i < NT else x_sample[:, 0]
                            act.dma_start(x1[0:r, i], src).then_inc(x1_in, 16)
                if n == 3:
                    full(act, ("wf", NGRP - 1, 7, 1))
                if n > 1:
                    act.wait_ge(res_sum, (n - 1) * (NT + 1))
                act.dma_start(grow, bass.AP(norm_g.tensor, (2 * n - 1) * D, [[0, P], [1, D]])).then_inc(grow_in, 16)
                base = (n - 1) * (NT + 1)

                def first(i):
                    r = token_tile(i)[1]
                    full(act, (f"b{n}", i))
                    own.then(f(junkR[0:r], slot((f"b{n}", i))[0:r], ACT.Square, accum_out=st[0:r, i:i + 1]))
                    f(st[0:r, 16 + i:17 + i], st[0:r, i:i + 1], ACT.Sqrt, scale=1.0 / D, bias=eps_c[0:r]).then_inc(res_stat, 1)

                first(0)
                first(1)
                for i in range(NT + 1):
                    if n < 3:
                        r = token_tile(i)[1]
                        act.wait_ge(res_sum, base + i + 1)
                        own.then(f(junkR[0:r], x1[0:r, i], ACT.Square, accum_out=st[0:r, 32 + i:33 + i]))
                        f(st[0:r, 48 + i:49 + i], st[0:r, 32 + i:33 + i], ACT.Sqrt, scale=1.0 / D,
                          bias=eps_c[0:r]).then_inc(res_stat2, 1)
                    if i + 2 <= NT:
                        first(i + 2)
                    if n == 2 and i >= 1:
                        input_hi(i - 1)
                if n == 2:
                    input_hi(NT)

            residual(1)

            full(act, "mT")
            free(f(mkT.rearrange("p h n -> p (h n)"), slot("mT")), "mT")
            for m in range(4):
                dense_out("xq", m, q2T[:, m])
            for b in range(DB):
                full(act, ("xT", b))
                free(f(kTm[:, b].rearrange("p h n -> p (h n)"), slot(("xT", b))), ("xT", b))
            act.wait_ge(px_raw, 1)
            free(f(Pxs[0:32], slot("xS")[0:32, 0:NM], ACT.Exp, bias=st[0:32, 33:34], scale=XSC,
                   accum_out=st[0:32, 34:35]), "xS")
            full(act, "xP")
            free(f(PTxs.rearrange("p a c -> p (a c)"), slot("xP")[:, 0:64]), "xP")
            for i in range(NT + 2):
                if i < NT:
                    act.wait_ge(px_raw, i + 2)
                    if i >= 3:
                        full(act, ("XT", i - 3))
                    b0 = 4 * (i % 3)
                    for h in range(XH):
                        ins = f(Px[:, i % 3, h * NM:(h + 1) * NM], slot(("XS", i))[:, h * NM:(h + 1) * NM], ACT.Exp,
                                bias=st[:, b0 + h:b0 + h + 1], scale=XSC, accum_out=st[:, 16 + b0 + h:17 + b0 + h])
                        free(ins, ("XS", i)) if h == XH - 1 else own.step(ins)
                if i >= 2:
                    t = i - 2
                    full(act, ("XT", t))
                    if t >= 2:
                        full(act, ("XO", t - 2))
                    free(f(PTx[:, t % 2], slot(("XT", t))), ("XT", t))
            residual(2)

            act.wait_ge(mkv_out, 16)
            weights_hi(NWO)
            for it, item in enumerate(ffn):
                if it + 1 < FFN_ITEMS:
                    weights_hi(NWO + it + 1)
                n = item[1] % FG
                if item[0] == "g":
                    full(act, item + (0,))
                    free(f(gRaw[:, n, 0:2 * CH].rearrange("p (a n) -> p a n", a=2), chunked(item + (0,)), ACT.Silu),
                         item + (0,))
                    full(act, item + (1,))
                    free(f(gRaw[:, n, 2 * CH:TC], chunked(item + (1,))[:, 0], ACT.Silu), item + (1,))
                elif item[0] == "u":
                    act.wait_ge(g_prod, item[1] + 1)
                    f(gH[:, n], gRaw[:, n]).then_inc(g_hi, 1)
            residual(3)

        @block.vector
        def _(dve):
            own = Own(dve, dve_own)
            v = nc.vector

            def tt(out, a, b, op=ALU.mult):
                return v.tensor_tensor(out, a, b, op)

            def cmul(out_re, out_im, a, b, t, neg_im=False):
                own.step(tt(t[0], a[0], b[0]))
                own.step(tt(t[1], a[1], b[1]))
                own.step(tt(t[2], a[0], b[1]))
                own.step(tt(t[3], a[1], b[0]))
                own.settle()
                for o in out_re:
                    own.step(tt(o[0], o[1](t[0]), o[1](t[1]), ALU.subtract))
                for o in out_im:
                    if neg_im:
                        own.step(v.scalar_tensor_tensor(o[0], o[1](t[2]), -1.0, o[1](t[3]), ALU.mult, ALU.subtract))
                    else:
                        own.step(tt(o[0], o[1](t[2]), o[1](t[3]), ALU.add))
                own.settle()

            def whole(o):
                return [(o, lambda x: x)]

            def bcast(col, shape, axis=-1):
                return col.unsqueeze(axis).to_broadcast(shape)

            full(dve, "par")
            own.step(v.tensor_copy(cols[:, :], slot("par")[:, 0:120]))
            free(v.tensor_copy(d_rows[:, :], slot("par")[:, 128:128 + NPAIR]), "par")
            read_out(dve, "par")
            def normalise(i):
                n = token_tile(i)[1]
                c0 = token_tile(i)[0]
                dve.wait_ge(rt_ready, i + 1)
                own.then(v.reciprocal(st[0:n, 32 + i:33 + i], st[0:n, 16 + i:17 + i]))
                v.tensor_scalar(xin[0:n, i % 2], xin[0:n, i % 2], st[0:n, 32 + i:33 + i], None, ALU.mult).then_inc(xn_ready, 1)
                full(dve, ("n1", i))
                s = slot(("n1", i)).rearrange("p (k t) -> p k t", k=KD)[:, :, 0:n]
                free(tt(hT[:, :, c0:c0 + n], s, bcast(cols[:, 0:8], [P, KD, n])), ("n1", i))

            for i in range(3):
                normalise(i)
            v.tensor_copy(jota[:, :], jota_i[:, :]).then_inc(s5_arg, 1)
            dve.wait_ge(s5_fun, 1)
            a_re, a_im, dt = cols[:, 72:88], cols[:, 88:104], prm[:, 0]
            own.step(tt(prm[:, 1], a_re, dt))
            own.then(tt(prm[:, 8], a_im, dt))
            TWO_PI = [6.28125, 0.0019350051879882812, 3.0199159819567e-07]
            for shift, dst in ((0.0, 4), (0.25, 6)):
                own.then(v.tensor_scalar(prm[:, 9], prm[:, 8], 1.0 / (2 * pi), shift, ALU.mult, ALU.add))
                own.then(v.tensor_scalar(prm[:, 9], prm[:, 9], 12582912.0, None, ALU.add))
                own.then(v.tensor_scalar(prm[:, 9], prm[:, 9], -12582912.0, None, ALU.add))
                own.then(v.scalar_tensor_tensor(prm[:, dst], prm[:, 9], -TWO_PI[0], prm[:, 8], ALU.mult, ALU.add))
                own.then(v.scalar_tensor_tensor(prm[:, dst], prm[:, 9], -TWO_PI[1], prm[:, dst], ALU.mult, ALU.add))
                own.then(v.scalar_tensor_tensor(prm[:, dst], prm[:, 9], -TWO_PI[2], prm[:, dst], ALU.mult, ALU.add))
                if shift:
                    own.then(v.tensor_scalar(prm[:, dst], prm[:, dst], pi / 2, None, ALU.add))
                own.then(v.tensor_scalar(prm[:, dst], prm[:, dst], 3.1415925, -3.1415925, ALU.min, ALU.max))
            dve.sem_inc(s5_arg, 1)
            dve.wait_ge(s5_fun, 3)
            ab = apow[:, 1]
            own.step(tt(ab[:, 0], prm[:, 2], prm[:, 7]))
            own.step(tt(ab[:, 1], prm[:, 2], prm[:, 5]))
            own.step(v.memset(apow[:, 0, 0], 1.0))
            own.step(v.memset(apow[:, 0, 1], 0.0))
            own.step(tt(prm[:, 9], a_re, a_re))
            own.step(tt(prm[:, 10], a_im, a_im))
            own.settle()
            own.step(tt(prm[:, 9], prm[:, 9], prm[:, 10], ALU.add))
            own.step(v.tensor_scalar(prm[:, 11], ab[:, 0], -1.0, None, ALU.add))
            own.settle()
            own.step(v.reciprocal(prm[:, 9], prm[:, 9]))
            own.step(tt(prm[:, 12], prm[:, 11], a_re))
            own.step(tt(prm[:, 13], ab[:, 1], a_im))
            own.step(tt(prm[:, 14], ab[:, 1], a_re))
            own.step(tt(prm[:, 15], prm[:, 11], a_im))
            own.settle()
            own.step(tt(prm[:, 12], prm[:, 12], prm[:, 13], ALU.add))
            own.step(tt(prm[:, 14], prm[:, 14], prm[:, 15], ALU.subtract))
            own.settle()
            own.step(tt(co[:, 0], prm[:, 12], prm[:, 9]))
            own.step(tt(co[:, 1], prm[:, 14], prm[:, 9]))
            own.settle()
            sm = [prm[:, 12 + n] for n in range(4)]
            for k in range(2, 5):
                cmul(whole(apow[:, k, 0]), whole(apow[:, k, 1]), (apow[:, k - 1, 0], apow[:, k - 1, 1]),
                     (ab[:, 0], ab[:, 1]), sm)

            dve.wait_ge(pt_in, 16 * (DB + 1))
            own.step(v.tensor_copy(tinyf[:, 0:1], tiny[:, 0:1]))
            own.step(v.tensor_single_scalar(tiny[:, 1:2], tiny[:, 0:1], 3, ALU.bitwise_and))
            own.step(v.tensor_single_scalar(tiny[:, 2:3], tiny[:, 0:1], 7, ALU.bitwise_and))
            own.settle()
            own.step(v.tensor_copy(tinyf[:, 1:2], tiny[:, 1:2]))
            own.step(v.tensor_copy(tinyf[:, 2:3], tiny[:, 2:3]))
            own.settle()
            own.step(v.tensor_scalar(tinyf[:, 3:4], tinyf[:, 1:2], 4.0, None, ALU.mult))
            own.settle()
            for k in range(4):
                own.step(v.tensor_scalar(tinyf[:, 4 + k:5 + k], tinyf[:, 3:4], float(k), None, ALU.add))
            own.settle()
            for k in range(4):
                ins = v.tensor_scalar(pline[:, k], ptc[:, :], 16.0, tinyf[:, 4 + k:5 + k], ALU.mult, ALU.add)
                own.step(ins) if k < 3 else ins.then_inc(pline_ready, 1)

            dve.wait_ge(pos_in, 16 * 12)
            for i in range(NT):
                dve.wait_ge(kv_ready, i + 1)
                own.step(v.tensor_copy(vkeep[:, i].rearrange("p (a c) -> p a c", a=2),
                                       kvst[:, i % 2, 256:768].rearrange("p (a b c) -> p a b c", a=2, b=2)[:, :, 1]))
                if i >= 2:
                    full(dve, ("kT", i - 2))
                tt(cprod[:, i % 2], kvst[:, i % 2, 0:256], posP).then_inc(prod_ready, 1)
                if i + 3 <= NT:
                    normalise(i + 3)

            dve.wait_ge(kv_stored[0], 16 * (2 * 4 + 2))
            dve.wait_ge(kv_stored[1], 16 * (2 * 4 + 2))
            dve.wait_ge(prod_ready, NT)
            full(dve, ("kT", NT - 1))
            dve.wait_ge(b_in, 32)
            dve.wait_ge(rows_saved, 64)
            own.step(v.memset(WT, 0.0))
            own.step(v.memset(CP, 0.0))
            own.step(v.memset(Tm[0], 0.0))
            own.step(v.memset(Tm[1], 0.0))
            sh = [P, NPAIR, 16]
            qq = [q[:, n] for n in range(4)]
            cmul(whole(bb[:, 0]), whole(bb[:, 1]), (bcast(co[:, 0], sh), bcast(co[:, 1], sh)),
                 (braw[:, 0], braw[:, 1]), qq)

            def halves(dst):
                return [(dst(g)[64 * g:64 * g + 64], lambda x, g=g: x[64 * g:64 * g + 64]) for g in range(2)]

            for l in range(L4):
                pw = apow[:, L4 - 1 - l]
                cmul(halves(lambda g: WT[:, 0, :, 32 * l + 16 * g:32 * l + 16 * g + 16]),
                     halves(lambda g: WT[:, 1, :, 32 * l + 16 * g:32 * l + 16 * g + 16]),
                     (bcast(pw[:, 0], sh), bcast(pw[:, 1], sh)), (bb[:, 0], bb[:, 1]), qq)
            read_out(dve, "C")
            for k in range(5):
                pw = apow[:, k]
                cmul(halves(lambda g: CP[:, 0, :, k, 16 * g:16 * g + 16]),
                     halves(lambda g: CP[:, 1, :, k, 16 * g:16 * g + 16]),
                     (bcast(pw[:, 0], sh), bcast(pw[:, 1], sh)), (cc[:, 0], cc[:, 1]), qq, neg_im=True)
            read_out(dve, "h0")
            dve.sem_inc(s5_built, 1)

            for m in range(4):
                for c in range(2):
                    read_out(dve, ("in", 4 + m, c))
                for q_ in range(4):
                    src = uTm[32 * q_:32 * q_ + 32, m % 2]
                    for l in range(L4):
                        own.step(v.tensor_copy(U2[32 * l:32 * l + 32, 4 * m + q_], src[:, l:T:L4]))
                    own.step(v.tensor_copy(us3[96:P, 4 * m + q_], src[:, T:TC]))
                own.settle()
                v.tensor_copy(uS[:, m], uTm[:, m % 2, T:TC]).then_inc(uT_ready, 1)
            for h in range(NH):
                g = h // GQ
                lo = 64 * (h % 2)
                ins = v.tensor_copy(qz[64 * g:64 * g + 64].rearrange("p b c -> p (b c)")[:, h::72],
                                    qT[lo:lo + 64, h // 2, T:TC])
                own.step(ins) if h < NH - 1 else ins.then_inc(qz_ready, 1)
            dve.wait_ge(uT_ready, 4)
            dve.sem_inc(u_moved, 1)

            own.then(v.memset(H[:, 0], 0.0))

            for j in range(NPAIR):
                key = ("SB", j)
                full(dve, key)
                s = slot(key)
                own.step(v.tensor_copy(H[:, 1:NC + 1, :, j].rearrange("p c a -> p a c"),
                                       s[:, 0:512].rearrange("p (a c) -> p a c", a=2)))
                own.step(v.tensor_copy(hs[:, :, j], s[:, 512:528].rearrange("p (a b) -> p a b", a=2)))
                free(v.scalar_tensor_tensor(U2[:, j], U2[:, j], d_rows[:, j:j + 1], s[:, 528:528 + NC],
                                            ALU.mult, ALU.add), key)
            read_out(dve, ("SB", NPAIR - 1))
            own.settle()

            for i in range(2):
                dve.wait_ge(mem_stat, i + 1)
                own.then(v.reciprocal(st[:, 32 + i:33 + i], st[:, 16 + i:17 + i]))
                v.tensor_scalar(mrow[:, i], mrow[:, i], st[:, 32 + i:33 + i], None, ALU.mult).then_inc(mem_norm, 1)
            for i in range(2):
                full(dve, ("mn", i))
                free(tt(memT[:, :, i * P:(i + 1) * P], slot(("mn", i)).rearrange("p (k t) -> p k t", k=KD),
                        bcast(cols[:, 56:64], [P, KD, P])), ("mn", i))
            sm2 = [r1[:, n, 0, 0:NPAIR] for n in range(4)]
            apw_ = lambda n: (apw[:, n, 0], apw[:, n, 1])
            own.step(v.tensor_copy(apw[:, 0], apow[:, 4]))
            own.settle()
            for n in range(1, 15):
                cmul(whole(apw[:, n, 0]), whole(apw[:, n, 1]), apw_(n - 1), (apow[:, 4, 0], apow[:, 4, 1]), sm2)
            cmul(whole(apow[:, 5, 0]), whole(apow[:, 5, 1]), apw_(14), (apow[:, 4, 0], apow[:, 4, 1]), sm2)
            Hm = H[:, 1:NC + 1].rearrange("p (m n) a j -> p m n a j", n=16)

            for n, power in enumerate([(apow[:, 4, 0], apow[:, 4, 1]), (apow[:, 5, 0], apow[:, 5, 1])]
                                      + [apw_(n) for n in range(15)]):
                own.step(v.tensor_copy(turn[:, n, 0, 0], power[0]))
                own.step(v.tensor_copy(turn[:, n, 1, 1], power[0]))
                own.step(v.tensor_copy(turn[:, n, 1, 0], power[1]))
                own.step(v.tensor_scalar(turn[:, n, 0, 1], power[1], -1.0, None, ALU.mult))
            own.settle()

            def advance(dst, src, n, m):
                shape = [P, m, 2, 2 * NPAIR]
                mat = turn[:, n].rearrange("p a b j -> p a (b j)").unsqueeze(1).to_broadcast(shape)
                own.then(tt(r1[:, 0:m],
                            src.rearrange("p m b j -> p m (b j)").unsqueeze(2).to_broadcast(shape), mat))
                own.then(tt(dst, dst, r1[:, 0:m, :, 0:NPAIR], ALU.add))
                own.then(tt(dst, dst, r1[:, 0:m, :, NPAIR:], ALU.add))

            for n in range(1, 16):
                advance(Hm[:, :, n], Hm[:, :, n - 1], 0, 16)
            for m in range(1, 16):
                advance(Hm[:, m:m + 1, 15], Hm[:, m - 1:m, 15], 1, 1)
            for n in range(15):
                advance(Hm[:, 1:16, n], Hm[:, 0:15, 15], 2 + n, 15)
            sb4 = [P, NPAIR, DB]
            t = [r1[:, 2 * n:2 * n + 2].rearrange("p m a j -> p (m a j)").rearrange("p (j b) -> p j b", b=DB)
                 for n in range(4)]
            abr, abi = bcast(ab[:, 0], sb4), bcast(ab[:, 1], sb4)
            own.step(tt(t[0], h0T[:, 0], abr))
            own.step(tt(t[1], h0T[:, 1], abi))
            own.step(tt(t[2], h0T[:, 1], abr))
            own.step(tt(t[3], h0T[:, 0], abi))
            own.settle()
            own.step(tt(t[0], t[0], t[1], ALU.subtract))
            own.step(tt(t[2], t[2], t[3], ALU.add))
            own.settle()
            own.step(tt(hs[:, 0], hs[:, 0], t[0], ALU.add))
            own.step(tt(hs[:, 1], hs[:, 1], t[2], ALU.add))
            own.settle()
            dve.sem_inc(s5_states, 1)
            dve.sem_inc(hs_ready, 1)

            for j in range(NPAIR):
                key = ("V", j)
                full(dve, key)
                q_, m = j % 4, j // 4
                for l in range(L4):
                    ins = tt(yF[32 * q_:32 * q_ + 32, m, l:T:L4], slot(key)[32 * l:32 * l + 32, 0:NC],
                             U2[32 * l:32 * l + 32, j], ALU.add)
                    free(ins, key) if l == L4 - 1 else own.step(ins)
            full(dve, "ys")
            for m in range(4):
                ins = v.scalar_tensor_tensor(yF[:, m, T:TC], uS[:, m], cols[:, 68 + m:69 + m],
                                             slot("ys")[:, m * DB:(m + 1) * DB], ALU.mult, ALU.add)
                free(ins, "ys") if m == 3 else own.step(ins)
            read_out(dve, "ys")
            dve.sem_inc(y_ready, 1)

            def softmax_in(out, x, bias, release=None):
                ins = v.tensor_tensor_reduce(out=out, in0=x, in1=bias, scale=1.0, scalar=FLOOR, op0=ALU.add,
                                             op1=ALU.max, accum_out=st[0:64, 32:33])
                if release:
                    free(ins, release)
                    read_out(dve, release)
                v.tensor_scalar(st[0:64, 33:34], st[0:64, 32:33], -SC, None, ALU.mult).then_inc(pw_raw, 1)

            def softmax_out(n, x):
                dve.wait_ge(pw_exp, n)
                own.then(v.tensor_scalar(st[0:64, 35:36], st[0:64, 34:35], TINY, None, ALU.max))
                own.then(v.reciprocal(st[0:64, 36:37], st[0:64, 35:36]))
                return v.tensor_scalar(x, x, st[0:64, 36:37], None, ALU.mult)

            def sum_lines(n, part):
                k, b = n // DB, n % DB
                flat = gring[:, n % 3]
                if part == 0:
                    dve.wait_ge(weighted, n + 1)
                    own.step(tt(flat[:, 0:1024], flat[:, 0:1024], flat[:, 1024:2048], ALU.add))
                elif part == 1:
                    own.settle()
                    own.step(tt(flat[:, 0:512], flat[:, 0:512], flat[:, 512:1024], ALU.add))
                else:
                    own.settle()
                    if k == 0:
                        tt(summ[:, b], flat[:, 0:256], flat[:, 256:512], ALU.add).then_inc(gat_used, 1)
                    else:
                        own.then(tt(flat[:, 0:256], flat[:, 0:256], flat[:, 256:512], ALU.add))
                        tt(summ[:, b], summ[:, b], flat[:, 0:256], ALU.add).then_inc(gat_used, 1)
                    if k == 3:
                        dve.wait_ge(gat_used, n + 1)
                        dve.sem_inc(summ_ready, 1)

            def compressed_branch(key):
                if key == "sc":
                    full(dve, key)
                    dve.wait_ge(V64_in, 16)
                    own.step(v.tensor_copy(cbias[0:64, 0:112], V64[:, 0:1].to_broadcast([64, 112])))
                    own.step(v.tensor_copy(cbias[0:64, 112:P], V64[:, 31::CB][:, 0:16]))
                    own.settle()

                    softmax_in(Pc[0:64], slot("sc")[0:64, 0:P], cbias[0:64], "sc")
                elif key == "sps":
                    softmax_out(1, Pc[0:64]).then_inc(pc_ready, 1)
                    full(dve, "sps")
                    free(v.tensor_reduce(score[0:64], slot("sps")[0:64, 0:P].rearrange("p (j a) -> p j a", a=2), X, ALU.add), "sps")
                    read_out(dve, "sps")
                    own.step(v.memset(score[0:64, 0:1], -1.0))
                    own.then(v.memset(score[0:64, NSB - 1:NSB], -1.0))
                    own.then(v.max(top[0:64, 0:8], score[0:64]))
                    own.step(v.max_index(topi[0:64, 0:8], top[0:64, 0:8], score[0:64]))
                    own.step(v.match_replace(out=score2[0:64], in_to_replace=top[0:64, 0:8], in_values=score[0:64], imm_value=-1.0))
                    own.settle()
                    own.then(v.max(top[0:64, 8:16], score2[0:64]))
                    own.then(v.max_index(topi[0:64, 8:16], top[0:64, 8:16], score2[0:64]))
                    own.then(v.tensor_copy(pick[0:64], topi[0:64]))
                    own.step(v.memset(pick[0:64, PICK:PICK + 1], 0.0))
                    own.step(v.memset(pick[0:64, PICK + 1:PICK + 2], float(NSB - 1)))
                    own.step(v.tensor_scalar(jphys[0:64].rearrange("p (j a) -> p j a", a=2)[:, :, 0], ptrow[:, :], 2.0, None, ALU.mult))
                    own.step(v.tensor_scalar(jphys[0:64].rearrange("p (j a) -> p j a", a=2)[:, :, 1], ptrow[:, :], 2.0, 1.0, ALU.mult, ALU.add))
                    own.settle()
                    s3 = [64, SLOTS, 64]
                    own.step(tt(onehot[0:64], bcast(pick[0:64, 0:SLOTS], s3), jota[:, :].unsqueeze(1).to_broadcast(s3), ALU.is_equal))
                    own.step(v.tensor_scalar(is62[0:64, 0:PICK], pick[0:64, 0:PICK], float(NSB - 2), None, ALU.is_equal))
                    own.settle()
                    own.then(tt(onehot[0:64], onehot[0:64], jphys[0:64].unsqueeze(1).to_broadcast(s3)))
                    v.tensor_reduce(phys[0:64, 0:SLOTS], onehot[0:64], X, ALU.add).then_inc(phys_ready, 1)
                elif key == "ix2":
                    full(dve, "ix2")
                    free(v.tensor_scalar(line[:, :], slot("ix2")[0:SL, 0:64], 8.0, tinyf[0:SL, 2:3], ALU.mult, ALU.add), "ix2")
                    read_out(dve, "ix2")
                    dve.sem_inc(line_ready, 1)

            dve.wait_ge(states_out, 64)
            dve.wait_ge(far_ready, NH)
            n_at = len(AT)
            def queries_lo(u):
                i, h = u // NH, u % NH
                lo = 64 * (h % 2)
                dve.wait_ge(q_hi, u + 1)
                tt(qS[64 - lo:128 - lo, u % QS], qT[lo:lo + 64, h // 2, i * P:(i + 1) * P], qS[lo:lo + 64, u % QS],
                   ALU.subtract).then_inc(q_lo, 1)

            for u in range(2):
                queries_lo(u)
            for a in range(n_at + AHEAD + 1):
                if a < n_at:
                    i, h, br = AT[a][0:3]
                    if br == 1 and i * NH + h + 2 < NT * NH:
                        queries_lo(i * NH + h + 2)
                t = a - AHEAD - 1
                if t + 1 >= 0 and t + 1 < n_at:
                    rn = (t + 1) % 8
                    dve.wait_ge(exp_ready, t + 2)
                    i, _, br, _, nk = AT[t + 1]
                    if br == 0:
                        own.then(v.tensor_reduce(cst[:, 1], Pm[:, (t + 1) % NPM, 0:NH * nk]
                                                 .rearrange("p (h n) -> p h n", n=nk), X, ALU.add))
                        own.step(v.tensor_scalar(cst[:, 1], cst[:, 1], TINY, None, ALU.max))
                    else:
                        own.step(v.tensor_scalar(st[:, 24 + rn:25 + rn], st[:, 16 + rn:17 + rn], TINY, None, ALU.max))
                if a < n_at:
                    i, h, br, k0, nk = AT[a]
                    r = a % 8
                    key = ("SC", a)
                    s = slot(key)
                    full(dve, key)
                    if a >= NPM:
                        full(dve, ("TR", a - NPM))
                    x0 = T - P - i * P
                    mx = st[:, r:r + 1]
                    start, done = -SC * FLOOR, 0
                    if br == 0:
                        pm = Pm[:, a % NPM, 0:NH * nk].rearrange("p (h n) -> p h n", n=nk)
                        for odd in range(2):
                            ins = tt(pm[:, 4 * odd:4 * odd + 4],
                                     s[:, 512 * odd:512 * odd + 4 * CB].rearrange("p (h n) -> p h n", n=CB)[:, :, 0:nk],
                                     BT[:, odd::2, x0 + CB - 1::CB][:, :, 0:nk], ALU.add)
                            free(ins, key) if odd else own.step(ins)
                        own.settle()
                        read_out(dve, key)
                        own.then(v.tensor_reduce(cst[:, 0], pm, X, ALU.max))
                        own.then(v.tensor_scalar(cst[:, 0], cst[:, 0], FLOOR, None, ALU.max))
                        tt(pm, pm, bcast(cst[:, 0], [P, NH, nk]), ALU.subtract).then_inc(c_raw, 1)
                    else:
                        bias = BT[:, h, x0 + k0:x0 + k0 + nk]
                        if br == 2 and i >= 4:
                            own.then(v.tensor_tensor_reduce(out=Pm[:, a % NPM, 0:P], in0=s[:, 0:P], in1=far[:, h],
                                                            scale=-SC, scalar=start, op0=ALU.add, op1=ALU.min,
                                                            accum_out=mx))
                            start, done, bias = mx, P, bias[:, P:]
                        free(v.tensor_tensor_reduce(out=Pm[:, a % NPM, done:nk], in0=s[:, done:nk], in1=bias, scale=-SC,
                                                    scalar=start, op0=ALU.add, op1=ALU.min,
                                                    accum_out=mx if not done else st[:, 40 + r:41 + r]), key)
                if t + 1 >= 0 and t + 1 < n_at:
                    own.settle()
                    if AT[t + 1][2] == 0:
                        own.step(v.reciprocal(cst[:, 1], cst[:, 1]))
                    else:
                        own.step(v.reciprocal(st[:, 48 + rn:49 + rn], st[:, 24 + rn:25 + rn]))
                if t >= 0:
                    i, h, br, k0, nk = AT[t]
                    key = ("PV", t)
                    r = t % 8
                    full(dve, key)
                    o = oN[:, i, h * HD:(h + 1) * HD]
                    p_ = slot(key)[:, 0:HD]
                    w = st[:, 56 + r:57 + r]
                    if br == 0:
                        dve.wait_ge(dve_gate, t + 1)
                        free(tt(oN[:, i].rearrange("p (h d) -> p h d", h=NH),
                                slot(key)[:, 0:NH * HD].rearrange("p (h d) -> p h d", h=NH),
                                bcast(cst[:, 2], [P, NH, HD])), key)
                    else:
                        read_out(dve, ("PV", unit_number(i, h, br - 1)))
                        dve.wait_ge(dve_gate, t + 1)
                        free(v.scalar_tensor_tensor(o, p_, w, o, ALU.mult, ALU.add), key)
                if t + 1 >= 0 and t + 1 < n_at:
                    own.settle()
                    i, h, br = AT[t + 1][0:3]
                    if br == 0:
                        for odd in range(2):
                            ins = tt(cst[:, 2, odd::2], cst[:, 1, 4 * odd:4 * odd + 4], gates[:, i, 3 * odd::6])
                            own.step(ins) if not odd else ins.then_inc(dve_gate, 1)
                    else:
                        tt(st[:, 56 + rn:57 + rn], st[:, 48 + rn:49 + rn], gates[:, i, 3 * h + br:3 * h + br + 1])\
                            .then_inc(dve_gate, 1)
                if 0 <= a - SUMS_AT < 3 * 4 * DB:
                    sum_lines((a - SUMS_AT) // 3, (a - SUMS_AT) % 3)
                for key in BETWEEN.get(a, []):
                    compressed_branch(key)

            far_bias = V64[:, 0:1]
            own.step(v.tensor_copy(sbias[0:64], far_bias.to_broadcast([64, ROWS * SK]).rearrange("p (r c) -> p r c", r=ROWS)))
            own.settle()
            last_block = V64[:, WIN - 64:WIN].rearrange("p (c r) -> p r c", r=ROWS)
            prev_block = V64[:, WIN - 128:WIN - 64]
            own.step(v.tensor_copy(sbias[0:64, :, (SLOTS - 1) * LINES:SL], last_block))
            own.step(v.tensor_scalar(score[0:64], prev_block, far_bias, None, ALU.subtract))
            own.step(v.tensor_copy(sbias[0:64, 0, SL:SK], V64[:, WIN:WIN + 1]))
            own.step(v.memset(sbias[0:64, 1:ROWS, SL:SK], NEG))
            own.settle()
            s4 = [64, PICK, LINES]
            for r in range(ROWS):
                diff = score[0:64].rearrange("p (c r) -> p r c", r=ROWS)[:, r].unsqueeze(1).to_broadcast(s4)
                own.then(tt(sdiff[0:64], bcast(is62[0:64, 0:PICK], s4), diff))
                own.then(tt(sbias[0:64, r, 0:PICK * LINES].rearrange("p (s c) -> p s c", c=LINES),
                            sbias[0:64, r, 0:PICK * LINES].rearrange("p (s c) -> p s c", c=LINES), sdiff[0:64], ALU.add))

            full(dve, "wS")
            softmax_in(Pw[0:64].rearrange("p (j c) -> p j c", j=4), slot("wS")[0:64, 0:512].rearrange("p (j c) -> p j c", j=4),
                       V64[:, 1:WIN + 1].rearrange("p (c j) -> p j c", j=4), "wS")
            softmax_out(2, Pw[0:64]).then_inc(pw_ready, 1)
            full(dve, "wO")
            dve.wait_ge(win_stored, 16 * DB)
            for n in range(2 * DB):
                g = n % 2
                dve.wait_ge(gat[n % 3], 16 * GAT0[n % 3] + 32 * (n // 3 + 1))
                v.tensor_copy(Vs[0:SK, n], gring[0:SK, n % 3].rearrange("p (r c) -> p r c", r=ROWS)
                              [:, :, P + g * HD:P + (g + 1) * HD]).then_inc(vs_ready, 1)
            full(dve, "gS")
            two = lambda x: x.rearrange("p (a c) -> p a c", a=2)
            flatS = Ps[0:64].rearrange("p a c -> p (a c)")
            softmax_in(two(flatS), two(slot("gS")[0:64])[:, :, 0:4 * SK],
                       two(sbias[0:64].rearrange("p a c -> p (a c)")), "gS")
            softmax_out(3, flatS).then_inc(pw_ready, 1)
            gt = gates[0:DB, NT].rearrange("b (h r) -> b h r", r=3)
            for br in range(3):
                key = "oT0" if br < 2 else "oT1"
                full(dve, key)
                ins = tt(oS[0:DB, br].rearrange("b (g h d) -> b g h d", g=NKV, h=GQ),
                         slot(key)[0:DB].rearrange("b (g r h d) -> b g r h d", g=NKV, r=2, h=GQ)[:, :, br % 2],
                         bcast(gt[:, :, br].rearrange("b (g h) -> b g h", g=NKV), [DB, NKV, GQ, HD]))
                own.step(ins) if br == 0 else free(ins, key)
            own.settle()
            read_out(dve, "oT0")
            read_out(dve, "oT1")
            own.then(tt(oS[0:DB, 0], oS[0:DB, 0], oS[0:DB, 1], ALU.add))
            tt(oS[0:DB, 0], oS[0:DB, 0], oS[0:DB, 2], ALU.add).then_inc(oS_ready, 1)

            for m in range(4):
                for c in range(2):
                    read_out(dve, ("glu", m, c))
            own.then(tt(oF, oF, yF))
            dve.sem_inc(oF_ready, 1)
            for i in range(NT + 1):
                c0, n = token_tile(i)
                src = oN[:, i] if i < NT else oS[0:DB, 0]
                dve.wait_ge(on_stat, i + 1)
                own.then(v.reciprocal(st[0:n, 32 + i:33 + i], st[0:n, 16 + i:17 + i]))
                v.tensor_scalar(src, src, st[0:n, 32 + i:33 + i], None, ALU.mult).then_inc(on_ready, 1)
                key = ("n0", i)
                full(dve, key)
                free(tt(mRaw[0][:, :, c0:c0 + n], slot(key)[:, 0:512].rearrange("p (k t) -> p k t", k=4)[:, :, 0:n],
                        bcast(cols[:, 48:52], [P, 4, n])), key)
            for i in range(NT + 1):
                read_out(dve, ("n0", i))

            def weights_lo(n):
                item, it = split[n]
                dve.wait_ge(w_hi, n + 1)
                size = group_size(item)
                wh, wl = parts_at(n)
                tt(wl[:, 0:size], wRaw[:, it % NS, 0:size], wh[:, 0:size], ALU.subtract).then_inc(w_lo, 1)

            dve.wait_ge(m_hi, 1)
            tt(mAL, mRaw[0], mH[:, 0:4], ALU.subtract).then_inc(m_lo, 1)
            weights_lo(0)
            read_out(dve, ("ss", 0))
            read_out(dve, ("ss", 1))
            own.then(v.reciprocal(RS, RS))
            for k in range(4):
                v.scalar_tensor_tensor(mRaw[1 + k], oF[:, k], cols[:, 52 + k:53 + k], RS, ALU.mult, ALU.mult)\
                    .then_inc(m_ready, 1)

            for k in range(4):
                dve.wait_ge(m_hi, 2 + k)
                tt(mL[4 + k], mRaw[1 + k], mH[:, 4 + k], ALU.subtract).then_inc(m_lo, 1)
            for m in range(1, NWO):
                weights_lo(m)

            def residual(n):
                base = (n - 1) * (NT + 1)
                dve.wait_ge(grow_in, 16 * n)
                if n == 1:
                    dve.wait_ge(x1_in, 16 * (NT + 1))

                def add(i):
                    r = token_tile(i)[1]
                    key = (f"b{n}", i)
                    dve.wait_ge(res_stat, base + i + 1)
                    own.then(v.reciprocal(st[0:r, 9 + i % 2:10 + i % 2], st[0:r, 16 + i:17 + i]))
                    if i >= 2:
                        dve.wait_ge(*((res_sum, base + i - 1) if n < 3 else (out_ready, i - 1)))
                    free(v.scalar_tensor_tensor(dtmp[0:r, i % 2], slot(key)[0:r], st[0:r, 9 + i % 2:10 + i % 2], grow[0:r],
                                                ALU.mult, ALU.mult), key)
                    read_out(dve, key)
                    tt(x1[0:r, i], x1[0:r, i], dtmp[0:r, i % 2], ALU.add).then_inc(res_sum if n < 3 else out_ready, 1)

                def scale(i):
                    r = token_tile(i)[1]
                    dve.wait_ge(res_stat2, base + i + 1)
                    own.then(v.reciprocal(st[0:r, 11 + i % 2:12 + i % 2], st[0:r, 48 + i:49 + i]))
                    if i >= 2:
                        full(dve, (f"f{n}", i - 2))
                    v.tensor_scalar(tb[0:r, i % 2], x1[0:r, i], st[0:r, 11 + i % 2:12 + i % 2], None, ALU.mult)\
                        .then_inc(res_norm, 1)

                def forward(i):
                    c0, r = token_tile(i)
                    key = (f"f{n}", i)
                    full(dve, key)
                    free(tt((hT if n == 1 else hRaw)[:, :, c0:c0 + r], slot(key).rearrange("p (k t) -> p k t", k=KD)[:, :, 0:r],
                            bcast(cols[:, 16 * n:16 * n + 8], [P, KD, r])), key)

                def input_lo(i):
                    c0, r = token_tile(i)
                    dve.wait_ge(h_hi, i + 1)
                    tt(hL[:, :, c0:c0 + r], hRaw[:, :, c0:c0 + r], hH[:, :, c0:c0 + r], ALU.subtract).then_inc(h_lo, 1)

                add(0)
                add(1)
                for i in range(NT + 1):
                    if n < 3:
                        scale(i)
                    if i + 2 <= NT:
                        add(i + 2)
                    if n < 3:
                        forward(i)
                    if n == 2 and i >= 1:
                        input_lo(i - 1)
                if n == 2:
                    input_lo(NT)

            residual(1)

            for m in range(4):
                for c in range(2):
                    read_out(dve, ("xq", m, c))
            dve.wait_ge(qxz_zero, 1)
            for h in range(XH):
                own.step(v.tensor_copy(qxz[:, h].rearrange("p b c -> p (b c)")[:, h::36], q2T[:, h, T:TC]))
            own.settle()
            dve.sem_inc(qxz_ready, 1)
            full(dve, "xS")
            own.then(v.tensor_reduce(st[0:32, 32:33], slot("xS")[0:32, 0:NM], X, ALU.max))
            v.tensor_scalar(st[0:32, 33:34], st[0:32, 32:33], -XSC, None, ALU.mult).then_inc(px_raw, 1)
            read_out(dve, "xS")
            own.then(v.reciprocal(st[0:32, 36:37], st[0:32, 34:35]))
            v.tensor_scalar(Pxs[0:32], Pxs[0:32], st[0:32, 36:37], None, ALU.mult).then_inc(px_ready, 1)
            full(dve, "xO")
            free(v.tensor_copy(q2T[:, :, T:TC], slot("xO")[:, 0:32].rearrange("p (h b) -> p h b", h=XH)), "xO")
            for i in range(NT + 3):
                if i < NT:
                    key = ("XS", i)
                    full(dve, key)
                    b0 = 4 * (i % 3)
                    own.then(v.tensor_reduce(st[:, 32 + b0:36 + b0], slot(key).rearrange("p (h n) -> p h n", h=XH), X, ALU.max))
                    v.tensor_scalar(st[:, b0:b0 + 4], st[:, 32 + b0:36 + b0], -XSC, None, ALU.mult).then_inc(px_raw, 1)
                if 1 <= i <= NT:
                    t = i - 1
                    b0 = 4 * (t % 3)
                    read_out(dve, ("XS", t))
                    own.then(v.reciprocal(st[:, 48 + b0:52 + b0], st[:, 16 + b0:20 + b0]))
                    px = Px[:, t % 3].rearrange("p (h n) -> p h n", h=XH)
                    tt(px, px, bcast(st[:, 48 + b0:52 + b0], [P, XH, NM])).then_inc(px_ready, 1)
                if i >= 3:
                    t = i - 3
                    key = ("XO", t)
                    full(dve, key)
                    free(v.tensor_copy(q2T[:, :, t * P:(t + 1) * P], slot(key)[:, 0:512].rearrange("p (h n) -> p h n", h=XH)), key)
            residual(2)

            weights_lo(NWO)
            for it, item in enumerate(ffn):
                if it + 1 < FFN_ITEMS:
                    weights_lo(NWO + it + 1)
                if item[0] == "u":
                    n = item[1] % FG
                    for c in range(2):
                        read_out(dve, ("g", item[1], c))
                        full(dve, item + (c,))
                        if c == 0:
                            w, s = gRaw[:, n, 0:2 * CH].rearrange("p (a n) -> p a n", a=2), chunked(item + (0,))
                        else:
                            w, s = gRaw[:, n, 2 * CH:TC], chunked(item + (1,))[:, 0]
                        free(tt(w, w, s), item + (c,))
                    read_out(dve, item + (0,))
                    read_out(dve, item + (1,))
                    dve.sem_inc(g_prod, 1)
                    dve.wait_ge(g_hi, item[1] + 1)
                    tt(gL[:, n], gRaw[:, n], gH[:, n], ALU.subtract).then_inc(g_lo, 1)
                elif item[0] == "o":
                    grp = item[1]
                    for m in (item[2], item[2] + 1):
                        for c in range(2):
                            key = ("wf", grp, m, c)
                            full(dve, key)
                            if c == 0:
                                y, s = yT[:, m, 0:2 * CH].rearrange("p (a n) -> p a n", a=2), chunked(key)
                            else:
                                y, s = yT[:, m, 2 * CH:TC], chunked(key)[:, 0]
                            if grp == 0:
                                free(v.tensor_copy(y, s), key)
                            else:
                                read_out(dve, ("wf", grp - 1, m, c))
                                free(tt(y, y, s, ALU.add), key)
            residual(3)


_INPUTS = ["x_prompt", "x_sample", "cache_kv_cmp", "cache_kv_sel", "cache_kv_win", "state_ssm_re", "state_ssm_im",
           "cache_mem_kv", "page_table", "mem_prompt", "w_in", "w_out", "norm_g", "grp_norm_g", "cmp_pos", "cmp_proj",
           "rel_bias", "ssm_a_re", "ssm_a_im", "ssm_b_re", "ssm_b_im", "ssm_c_re", "ssm_c_im", "ssm_d", "ssm_log_dt",
           "glu_w", "glu_b", "mem_norm_g", "xq", "xkv", "xo", "ffn_wi", "ffn_wo"]
_OUTPUTS = [(1, T, D), (DB, 1, D), (1, 1, T, 2, NKV, HD), (1, 1, T, 2, NKV, HD), (1, 1, WIN, 2, NKV, HD),
            (1, 1, 32, 64), (1, 1, 32, 64), (1, 1, NM, 2, XH, P), (1, DB, 1, 2, NKV, HD), (1, DB, 1, 2, NKV, HD),
            (1, DB, WIN, 2, NKV, HD), (1, DB, 32, 64), (1, DB, 32, 64)]


def kernel(**inputs):
    import concourse.bacc as bacc
    from concourse.bass_utils import run_bass_kernel_spmd

    nc = bacc.Bacc("TRN2", target_bir_lowering=False, num_devices=1)
    arrays, args = {}, []
    for name in _INPUTS:
        a = np.ascontiguousarray(inputs[name])
        arrays[f"in_{name}"] = a
        args.append(nc.dram_tensor(f"in_{name}", a.shape, mybir.dt.from_np(a.dtype), kind="ExternalInput").ap())
    for i, shape in enumerate(_OUTPUTS):
        args.append(nc.dram_tensor(f"out_{i}", shape, F32, kind="ExternalOutput").ap())
    hymba_step(nc, *args)
    r = run_bass_kernel_spmd(nc, [arrays], core_ids=[0])
    return tuple(r.results[0][f"out_{i}"] for i in range(len(_OUTPUTS)))
```
